# Optimizing a Trainium2 kernel written in Bass

```python
import math
import jax
import jax.numpy as jnp
from jax import lax
import numpy as np

D_MODEL = 1024
BATCH = 1
SEQ = 1024
DEPTH = 2
DEC_BATCH = 1
DEC_SEQ = 256
PAST_LEN = 128

N_EVEN = (DEPTH + 1) // 2
N_ODD = DEPTH // 2

RW_HEADS = 8
RW_HEAD_DIM = 64
RW_WIDTH = RW_HEADS * RW_HEAD_DIM
RW_DECAY_RANK = 64
RW_ICLR_RANK = 64
RW_GATE_RANK = 128
RW_COLS = 3 * RW_WIDTH + 2 * RW_DECAY_RANK + 2 * RW_ICLR_RANK + RW_GATE_RANK
RW_GN_EPS = 64e-5

GD_HEADS = 4
GD_HEAD_DIM = 128
GD_WIDTH = GD_HEADS * GD_HEAD_DIM
GD_CONV = 5
GD_CHUNK = 64
GD_NORM_EPS = 1e-6
GD_COLS = 4 * GD_WIDTH + 4 * GD_HEADS

AB_COLS = RW_COLS + GD_COLS
AB_OUT = RW_WIDTH + GD_WIDTH

AT_Q_HEADS = 16
AT_KV_HEADS = 4
AT_GROUP = AT_Q_HEADS // AT_KV_HEADS
AT_HEAD_DIM = 64
AT_WINDOW = 128
AT_BLOCK = 128
AT_COLS = (AT_Q_HEADS + 2 * AT_KV_HEADS) * AT_HEAD_DIM
ROPE_DIM = AT_HEAD_DIM // 4
ROPE_THETA = 500000.0

N_EXPERTS = 32
N_GROUPS = 8
EXPERTS_PER_GROUP = N_EXPERTS // N_GROUPS
GROUP_SCORE_TOP = 2
TOP_K = 2
MOE_FF = 256
MOE_BLOCK = 128

ALPHA = (2 * DEPTH) ** 0.25
BETA = (8 * DEPTH) ** -0.25
LN_EPS = 1e-5

kernel_name = 'hybrid_bidir_rwkv7_gdn_swa_moe_encoder'

f32 = jnp.float32

def layer_norm(x, g, b):
    xf = x.astype(f32)
    mean = xf.mean(-1, keepdims=True)
    var = jnp.square(xf - mean).mean(-1, keepdims=True)
    return ((xf - mean) * lax.rsqrt(var + LN_EPS)).astype(x.dtype) * g + b

def l2_normalize(x):
    xf = x.astype(f32)
    return (xf * lax.rsqrt(jnp.sum(xf * xf, -1, keepdims=True) + 1e-12)).astype(x.dtype)

def ada_modulation(c, w, b):
    mod = (jax.nn.silu(c) @ w + b)[:, None, :]
    return jnp.split(mod, 3, axis=-1)

def bidir_stack(fwd, bwd):
    return jnp.stack([fwd, jnp.flip(bwd, axis=1)], axis=0)

def bidir_merge(y):
    return y[0] + jnp.flip(y[1], axis=1)

def centred_token_shift(z, mu):
    zp = jnp.pad(z, ((0, 0), (1, 1), (0, 0)))
    return z + mu * (0.5 * (zp[:, :-2] + zp[:, 2:]) - z)

def centred_depthwise_conv(z, w):
    K = w.shape[0]
    pad = K // 2
    S = z.shape[1]
    zp = jnp.pad(z, ((0, 0), (pad, pad), (0, 0)))
    out = zp[:, 0:S] * w[0]
    for j in range(1, K):
        out = out + zp[:, j:j + S] * w[j]
    return out

def rwkv7_scan(r, w, k, v, kk, a):
    def step(state, inp):
        r_t, w_t, k_t, v_t, kk_t, a_t = inp
        sa = jnp.einsum('...vk,...k->...v', state, kk_t)
        state = (state * w_t[..., None, :] - sa[..., :, None] * (kk_t * a_t)[..., None, :]
                 + v_t[..., :, None] * k_t[..., None, :])
        return state, jnp.einsum('...vk,...k->...v', state, r_t)
    state0 = jnp.zeros(r.shape[1:] + (r.shape[-1],), f32)
    _, y = lax.scan(step, state0, (r, w, k, v, kk, a))
    return y

def rwkv7_bidir(z, mu, w0, w_up, a0, a_up, g_up, k_k, k_a, r_k, gn_g, gn_b):
    B, S, _ = z.shape
    W, H, N = RW_WIDTH, RW_HEADS, RW_HEAD_DIM
    heads = lambda t: t.reshape(B, S, H, N)
    h32 = lambda t: heads(t).astype(f32)
    tm = lambda t: jnp.moveaxis(t, 2, 0)
    z = centred_token_shift(z, mu)
    r, k, v = z[..., :W], z[..., W:2 * W], z[..., 2 * W:3 * W]
    o1 = 3 * W
    o2 = o1 + 2 * RW_DECAY_RANK
    o3 = o2 + 2 * RW_ICLR_RANK
    w_low = jnp.tanh(z[..., o1:o2]).reshape(B, S, 2, RW_DECAY_RANK)
    a_low = z[..., o2:o3].reshape(B, S, 2, RW_ICLR_RANK)
    g_low = jax.nn.sigmoid(z[..., o3:])
    w_raw = (w0 + jnp.einsum('bsdr,drc->bsdc', w_low, w_up)).astype(f32)
    decay = jnp.exp(-jnp.exp(-jax.nn.softplus(-w_raw) - 0.5))
    iclr = jax.nn.sigmoid(a0 + jnp.einsum('bsdr,drc->bsdc', a_low, a_up))
    gate = g_low @ g_up
    kk = l2_normalize(heads(k * k_k)).astype(f32)
    k_dir = k[:, :, None, :] * (1.0 + (iclr - 1.0) * k_a)
    y = rwkv7_scan(
        tm(bidir_stack(h32(r), h32(r))),
        tm(bidir_stack(heads(decay[:, :, 0]), heads(decay[:, :, 1]))),
        tm(bidir_stack(h32(k_dir[:, :, 0]), h32(k_dir[:, :, 1]))),
        tm(bidir_stack(h32(v), h32(v))),
        tm(bidir_stack(kk, kk)),
        tm(bidir_stack(h32(iclr[:, :, 0]), h32(iclr[:, :, 1]))))
    y = bidir_merge(jnp.moveaxis(y, 0, 2))
    mean = y.mean(-1, keepdims=True)
    var = jnp.square(y - mean).mean(-1, keepdims=True)
    y = ((y - mean) * lax.rsqrt(var + RW_GN_EPS)).reshape(B, S, W).astype(z.dtype) * gn_g + gn_b
    bonus = jnp.sum(heads(r) * heads(k_dir[:, :, 0] + k_dir[:, :, 1]) * r_k, -1, keepdims=True) * heads(v)
    return (y + bonus.reshape(B, S, W)) * gate

def chunk_gated_delta_rule(q, k, v, g, beta):
    q, k, v, g, beta = (t.astype(f32) for t in (q, k, v, g, beta))
    *lead, S, dk = q.shape
    dv = v.shape[-1]
    C = GD_CHUNK
    n = S // C
    nl = len(lead)
    q = q * dk ** -0.5
    chunks = lambda t: t.reshape(*lead, n, C, *t.shape[nl + 1:])
    qc, kc, vc, gc, bc = (chunks(t) for t in (q, k, v, g, beta))
    gcum = jnp.cumsum(gc, axis=-1)
    kb = kc * bc[..., None]
    vb = vc * bc[..., None]
    idx = jnp.arange(C)
    lower = idx[:, None] >= idx[None, :]
    strict = idx[:, None] > idx[None, :]
    decay = jnp.exp(jnp.where(lower, gcum[..., :, None] - gcum[..., None, :], -jnp.inf))
    a_mat = jnp.where(strict, jnp.einsum('...id,...jd->...ij', kb, kc) * decay, 0.0)
    rhs = jnp.concatenate([vb, kb * jnp.exp(gcum)[..., None]], axis=-1)
    sol = lax.linalg.triangular_solve(a_mat + jnp.eye(C, dtype=f32), rhs, left_side=True,
                                      lower=True, unit_diagonal=True)
    u, w = sol[..., :dv], sol[..., dv:]
    qk = jnp.einsum('...id,...jd->...ij', qc, kc) * decay

    def step(state, inp):
        q_i, k_i, u_i, w_i, g_i, qk_i = inp
        v_new = u_i - jnp.einsum('...cd,...de->...ce', w_i, state)
        o = (jnp.einsum('...cd,...de->...ce', q_i * jnp.exp(g_i)[..., None], state)
             + jnp.einsum('...ij,...je->...ie', qk_i, v_new))
        g_last = g_i[..., -1:]
        state = (state * jnp.exp(g_last)[..., None]
                 + jnp.einsum('...cd,...ce->...de', k_i * jnp.exp(g_last - g_i)[..., None], v_new))
        return state, o

    mv = lambda t: jnp.moveaxis(t, nl, 0)
    state0 = jnp.zeros((*lead, dk, dv), f32)
    _, o = lax.scan(step, state0, (mv(qc), mv(kc), mv(u), mv(w), mv(gcum), mv(qk)))
    return jnp.moveaxis(o, 0, nl).reshape(*lead, S, dv)

def gated_deltanet_bidir(z, conv_w, A_log, dt_bias, norm_g):
    B, S, _ = z.shape
    W, H = GD_WIDTH, GD_HEADS
    heads = lambda t: t.reshape(B, S, H, GD_HEAD_DIM)
    sw = lambda t: jnp.swapaxes(t, 2, 3)
    qkv = jax.nn.silu(centred_depthwise_conv(z[..., :3 * W], conv_w))
    q = l2_normalize(heads(qkv[..., :W]))
    k = l2_normalize(heads(qkv[..., W:2 * W]))
    v = heads(qkv[..., 2 * W:])
    out_gate = heads(z[..., 3 * W:4 * W])
    a = z[..., 4 * W:4 * W + 2 * H].reshape(B, S, 2, H).astype(f32)
    b = z[..., 4 * W + 2 * H:].reshape(B, S, 2, H).astype(f32)
    log_decay = -jnp.exp(A_log.astype(f32)) * jax.nn.softplus(a + dt_bias.astype(f32))
    beta = jax.nn.sigmoid(b)
    o = chunk_gated_delta_rule(
        sw(bidir_stack(q, q)), sw(bidir_stack(k, k)), sw(bidir_stack(v, v)),
        sw(bidir_stack(log_decay[:, :, 0], log_decay[:, :, 1])),
        sw(bidir_stack(beta[:, :, 0], beta[:, :, 1])))
    o = bidir_merge(sw(o))
    o = o * lax.rsqrt(jnp.mean(o * o, -1, keepdims=True) + GD_NORM_EPS)
    return (o.astype(z.dtype) * norm_g * jax.nn.silu(out_gate)).reshape(B, S, W)

def rotary_tables(S):
    inv_freq = ROPE_THETA ** (-jnp.arange(0, ROPE_DIM, 2, dtype=f32) / ROPE_DIM)
    ang = jnp.arange(S, dtype=f32)[:, None] * inv_freq[None, :]
    return jnp.cos(ang), jnp.sin(ang)

def partial_rotary(x, cos, sin):
    half = ROPE_DIM // 2
    c = cos[None, :, None, :].astype(x.dtype)
    s = sin[None, :, None, :].astype(x.dtype)
    x1, x2 = x[..., :half], x[..., half:ROPE_DIM]
    return jnp.concatenate([x1 * c - x2 * s, x2 * c + x1 * s, x[..., ROPE_DIM:]], axis=-1)

def banded_window_attention(q, k, v, sink):
    B, S = q.shape[:2]
    L = AT_BLOCK
    nb = S // L
    qb = q.reshape(B, nb, L, AT_KV_HEADS, AT_GROUP, AT_HEAD_DIM)

    def neighbour_blocks(t):
        tp = jnp.pad(t, ((0, 0), (L, L), (0, 0), (0, 0))).reshape(B, nb + 2, L, AT_KV_HEADS, AT_HEAD_DIM)
        return jnp.concatenate([tp[:, :-2], tp[:, 1:-1], tp[:, 2:]], axis=2)

    kb, vb = neighbour_blocks(k), neighbour_blocks(v)
    qpos = jnp.arange(nb)[:, None] * L + jnp.arange(L)[None, :]
    kpos = jnp.arange(nb)[:, None] * L - L + jnp.arange(3 * L)[None, :]
    rel = kpos[:, None, :] - qpos[:, :, None]
    valid = (jnp.abs(rel) <= AT_WINDOW) & (kpos[:, None, :] >= 0) & (kpos[:, None, :] < S)
    sink_g = sink.astype(f32).reshape(AT_KV_HEADS, AT_GROUP)[:, :, None, None]
    scale = AT_HEAD_DIM ** -0.5

    def one_sequence(args):
        qs, ks, vs = args
        s = jnp.einsum('nqhgd,nkhd->nhgqk', qs, ks).astype(f32) * scale
        s = jnp.where(valid[:, None, None], s, -jnp.inf)
        m = jnp.maximum(s.max(-1, keepdims=True), sink_g)
        p = jnp.exp(s - m)
        denom = p.sum(-1, keepdims=True) + jnp.exp(sink_g - m)
        return jnp.einsum('nhgqk,nkhd->nqhgd', (p / denom).astype(vs.dtype), vs)

    o = lax.map(one_sequence, (qb, kb, vb))
    return o.reshape(B, S, AT_Q_HEADS * AT_HEAD_DIM)

def windowed_gqa(h, w_in, sink, w_out, cos, sin):
    B, S, _ = h.shape
    nq = AT_Q_HEADS * AT_HEAD_DIM
    nk = AT_KV_HEADS * AT_HEAD_DIM
    z = h @ w_in
    q = partial_rotary(z[..., :nq].reshape(B, S, AT_Q_HEADS, AT_HEAD_DIM), cos, sin)
    k = partial_rotary(z[..., nq:nq + nk].reshape(B, S, AT_KV_HEADS, AT_HEAD_DIM), cos, sin)
    v = z[..., nq + nk:].reshape(B, S, AT_KV_HEADS, AT_HEAD_DIM)
    return banded_window_attention(q, k, v, sink) @ w_out

def route(t, router_w, router_bias):
    T = t.shape[0]
    scores = jax.nn.sigmoid((t @ router_w).astype(f32))
    grouped = (scores + router_bias.astype(f32)).reshape(T, N_GROUPS, EXPERTS_PER_GROUP)
    group_score = lax.top_k(grouped, GROUP_SCORE_TOP)[0].sum(-1)
    best = jnp.argmax(group_score, axis=-1)
    in_group = grouped[jnp.arange(T), best]
    _, local = lax.top_k(in_group, TOP_K)
    experts = (best[:, None] * EXPERTS_PER_GROUP + local).astype(jnp.int32)
    gates = jnp.take_along_axis(scores, experts, axis=1)
    return experts, gates / gates.sum(-1, keepdims=True)

def grouped_moe(h, router_w, router_bias, w_gate, w_up, w_down):
    B, S, D = h.shape
    t = h.reshape(-1, D)
    T = t.shape[0]
    experts, gates = route(t, router_w, router_bias)
    A = T * TOP_K
    flat_e = experts.reshape(-1)
    order = jnp.argsort(flat_e)
    sorted_e = flat_e[order]
    counts = jnp.bincount(flat_e, length=N_EXPERTS)
    padded = (counts + MOE_BLOCK - 1) // MOE_BLOCK * MOE_BLOCK
    start = jnp.cumsum(counts) - counts
    pad_end = jnp.cumsum(padded)
    pad_start = pad_end - padded
    dest = pad_start[sorted_e] + jnp.arange(A) - start[sorted_e]
    nblk = (A + MOE_BLOCK - 1) // MOE_BLOCK + N_EXPERTS
    P = nblk * MOE_BLOCK
    row_tok = jnp.zeros((P,), jnp.int32).at[dest].set((order // TOP_K).astype(jnp.int32))
    row_w = jnp.zeros((P,), f32).at[dest].set(gates.reshape(-1)[order])
    blk_exp = jnp.minimum(jnp.searchsorted(pad_end, jnp.arange(nblk) * MOE_BLOCK, side='right'),
                          N_EXPERTS - 1).astype(jnp.int32)

    def expert_block(args):
        tok, e = args
        xb = t[tok]
        hid = jax.nn.silu(xb @ w_gate[e]) * (xb @ w_up[e])
        return hid @ w_down[e]

    y = lax.map(expert_block, (row_tok.reshape(nblk, MOE_BLOCK), blk_exp)).reshape(P, D)
    out = jax.ops.segment_sum(y * row_w[:, None].astype(y.dtype), row_tok, num_segments=T)
    return out.reshape(B, S, D)

def setup_inputs(seed: int = 0) -> dict:
    key = jax.random.key(seed)
    ks = iter(jax.random.split(key, 48))
    D = D_MODEL

    def nrm(shape, std):
        return std * jax.random.normal(next(ks), shape, f32)

    def unif(shape, lo, hi):
        return jax.random.uniform(next(ks), shape, f32, lo, hi)

    lin = jnp.linspace(0.0, 1.0, RW_WIDTH, dtype=f32)
    dt = jnp.exp(unif((N_EVEN, 2, GD_HEADS), math.log(0.001), math.log(0.1)))
    return {
        'x_prompt': nrm((BATCH, SEQ, D), 1.0),
        'x_sample': nrm((DEC_BATCH, DEC_SEQ, D), 1.0),
        'c_prompt': nrm((BATCH, D), 1.0),
        'c_sample': nrm((DEC_BATCH, D), 1.0),
        'ada_w': nrm((DEPTH, 2, D, 3 * D), 0.1 * D ** -0.5),
        'ada_b': nrm((DEPTH, 2, 3 * D), 0.02),
        'ln_g': 1.0 + nrm((DEPTH, 2, D), 0.02),
        'ln_b': nrm((DEPTH, 2, D), 0.02),
        'ab_w_in': nrm((N_EVEN, D, AB_COLS), D ** -0.5),
        'rw_mu': unif((N_EVEN, RW_COLS), 0.0, 1.0),
        'rw_w0': -6.5 + 5.0 * lin ** 0.85 + nrm((N_EVEN, 2, RW_WIDTH), 0.1),
        'rw_w_up': nrm((N_EVEN, 2, RW_DECAY_RANK, RW_WIDTH), 0.1 * RW_DECAY_RANK ** -0.5),
        'rw_a0': nrm((N_EVEN, 2, RW_WIDTH), 0.1),
        'rw_a_up': nrm((N_EVEN, 2, RW_ICLR_RANK, RW_WIDTH), 0.5 * RW_ICLR_RANK ** -0.5),
        'rw_g_up': nrm((N_EVEN, RW_GATE_RANK, RW_WIDTH), RW_GATE_RANK ** -0.5),
        'rw_k_k': 0.85 + nrm((N_EVEN, RW_WIDTH), 0.02),
        'rw_k_a': 1.0 + nrm((N_EVEN, RW_WIDTH), 0.02),
        'rw_r_k': nrm((N_EVEN, RW_HEADS, RW_HEAD_DIM), 0.1),
        'rw_gn_g': 1.0 + nrm((N_EVEN, RW_WIDTH), 0.02),
        'rw_gn_b': nrm((N_EVEN, RW_WIDTH), 0.02),
        'gd_conv': nrm((N_EVEN, GD_CONV, 3 * GD_WIDTH), GD_CONV ** -0.5),
        'gd_A_log': jnp.log(unif((N_EVEN, 2, GD_HEADS), 1.0, 16.0)),
        'gd_dt_bias': dt + jnp.log(-jnp.expm1(-dt)),
        'gd_norm_g': 1.0 + nrm((N_EVEN, GD_HEAD_DIM), 0.02),
        'ab_w_out': nrm((N_EVEN, AB_OUT, D), BETA * AB_OUT ** -0.5),
        'at_w_in': nrm((N_ODD, D, AT_COLS), D ** -0.5),
        'at_sink': nrm((N_ODD, AT_Q_HEADS), 0.5),
        'at_w_out': nrm((N_ODD, AT_Q_HEADS * AT_HEAD_DIM, D), BETA * (AT_Q_HEADS * AT_HEAD_DIM) ** -0.5),
        'router_w': nrm((D, N_EXPERTS), D ** -0.5),
        'router_bias': nrm((N_EXPERTS,), 0.01),
        'moe_w_gate': nrm((DEPTH, N_EXPERTS, D, MOE_FF), D ** -0.5),
        'moe_w_up': nrm((DEPTH, N_EXPERTS, D, MOE_FF), D ** -0.5),
        'moe_w_down': nrm((DEPTH, N_EXPERTS, MOE_FF, D), BETA * MOE_FF ** -0.5),
    }

def reference(x_prompt, x_sample, c_prompt, c_sample, ada_w, ada_b, ln_g, ln_b,
              ab_w_in, rw_mu, rw_w0, rw_w_up, rw_a0, rw_a_up, rw_g_up, rw_k_k, rw_k_a, rw_r_k,
              rw_gn_g, rw_gn_b, gd_conv, gd_A_log, gd_dt_bias, gd_norm_g, ab_w_out,
              at_w_in, at_sink, at_w_out, router_w, router_bias, moe_w_gate, moe_w_up, moe_w_down):
    def trunk(x, c):
        cos, sin = rotary_tables(x.shape[1])
        for layer in range(DEPTH):
            i = layer // 2
            shift, scale, gate = ada_modulation(c, ada_w[layer, 0], ada_b[layer, 0])
            h = x * (1.0 + scale) + shift
            if layer % 2 == 0:
                z = h @ ab_w_in[i]
                ya = rwkv7_bidir(z[..., :RW_COLS], rw_mu[i], rw_w0[i], rw_w_up[i], rw_a0[i], rw_a_up[i],
                                 rw_g_up[i], rw_k_k[i], rw_k_a[i], rw_r_k[i], rw_gn_g[i], rw_gn_b[i])
                yb = gated_deltanet_bidir(z[..., RW_COLS:], gd_conv[i], gd_A_log[i], gd_dt_bias[i], gd_norm_g[i])
                mixed = jnp.concatenate([ya, yb], axis=-1) @ ab_w_out[i]
            else:
                mixed = windowed_gqa(h, at_w_in[i], at_sink[i], at_w_out[i], cos, sin)
            x = layer_norm(ALPHA * x + (1.0 + gate) * mixed, ln_g[layer, 0], ln_b[layer, 0])
            shift, scale, gate = ada_modulation(c, ada_w[layer, 1], ada_b[layer, 1])
            h = x * (1.0 + scale) + shift
            ffn = grouped_moe(h, router_w, router_bias, moe_w_gate[layer], moe_w_up[layer], moe_w_down[layer])
            x = layer_norm(ALPHA * x + (1.0 + gate) * ffn, ln_g[layer, 1], ln_b[layer, 1])
        return x

    y_prompt = trunk(x_prompt, c_prompt)
    y_sample = trunk(x_sample, c_sample)
    return (y_prompt, y_sample)


_drawn_inputs = setup_inputs


def setup_inputs(seed=0):
    import zlib

    import numpy as np

    out = dict(_drawn_inputs(seed))
    spreads = {}
    factors = {'rw_w_up': 6.426,
     'rw_k_k': 4.205,
     'rw_k_a': 2.936,
     'rw_gn_g': 4.084,
     'rw_gn_b': 3.752,
     'at_sink': 48.086,
     'gd_norm_g': 2.788}
    for name, (base, spread) in spreads.items():
        noise = np.random.default_rng([zlib.crc32(name.encode()), seed]).standard_normal(out[name].shape)
        drawn = base * np.exp(spread * noise) if base else spread * noise
        out[name] = jnp.asarray(drawn.astype(out[name].dtype))
    for name, factor in factors.items():
        out[name] = (out[name] * factor).astype(out[name].dtype)
    return out
```

```python
import math
from contextlib import ExitStack

import concourse.bass as bass
import numpy as np
from concourse import mybir

F32 = mybir.dt.float32
I32 = mybir.dt.int32
U32 = mybir.dt.uint32
ALU = mybir.AluOpType
ACT = mybir.ActivationFunctionType
AX = mybir.AxisListType
ds = bass.ds

P = 128
D = 1024
KC = D // P
S_PROMPT, S_SAMPLE = 1024, 256
T = S_PROMPT + S_SAMPLE
TILES = T // P
TP = S_PROMPT // P
SEQ_TILES = ((0, TP), (TP, TILES))
DEPTH = 2
ALPHA = (2 * DEPTH) ** 0.25
LN_EPS = 1e-5

RW_H, RW_N = 8, 64
RW_W = RW_H * RW_N
GD_H, GD_N = 4, 128
GD_W = GD_H * GD_N
RW_GN_EPS = 64e-5
GD_NORM_EPS = 1e-6
AT_H, AT_KV, AT_N = 16, 4, 64
AT_COLS = (AT_H + 2 * AT_KV) * AT_N
ROPE = 16
HALF_ROPE = ROPE // 2
E, GROUPS, PER = 32, 8, 4
FF = 256
OVER = 20
MAX_OVER = T // P
BLOCKS = E + OVER

CONST = {}
_at = 0
for _name, _w in [("ident", P), ("ones", P), ("before", P), ("diag2", P), ("rank", 64), ("half", 1)] + [
        (f"{n}{d}", w) for d in range(2) for n, w in
        [("cum_incl", P), ("cum_excl", P), ("incl", P), ("strict", P), ("mask_b", 2 * P), ("mask_k", 2 * P),
         ("floor", P)]]:
    CONST[_name] = slice(_at, _at + _w)
    _at += _w
CONST_W = _at
LEVELS = 7
DECAY = math.exp(-0.5)
NEG = -1e30


def constant_tables():
    c = np.zeros((P, CONST_W), np.float32)
    s, t = np.arange(P)[:, None], np.arange(P)[None, :]
    c[:, CONST["ident"]] = s == t
    c[:, CONST["ones"]] = 1
    c[:, CONST["before"]] = s < t
    c[:, CONST["diag2"]] = s // 64 == t // 64
    c[:, CONST["rank"]] = np.arange(64)[None, :]
    c[:, CONST["half"]] = -0.5 * DECAY
    for d in range(2):
        incl, strict = ((s <= t), (s < t)) if d == 0 else ((s >= t), (s > t))
        c[:, CONST[f"cum_incl{d}"]] = -DECAY * (incl - 0.5)
        c[:, CONST[f"cum_excl{d}"]] = -DECAY * (strict - 0.5)
        c[:, CONST[f"incl{d}"]] = incl
        c[:, CONST[f"strict{d}"]] = strict
        c[:, CONST[f"mask_b{d}"]] = np.concatenate([-1.0 * strict, 1.0 * incl], 1)
        c[:, CONST[f"mask_k{d}"]] = np.concatenate([1.0 * strict, 1.0 * incl], 1)
        c[:, CONST[f"floor{d}"]] = np.where(incl, 0, NEG)
    levels = np.zeros((P, 2, LEVELS, P), np.int32)
    for n in range(LEVELS):
        b = 1 << n
        pair = (s // (2 * b) == t // (2 * b)) & (s // b != t // b)
        levels[:, 0, n] = pair & (s < t)
        levels[:, 1, n] = pair & (s > t)
    f32 = np.float32
    inv = f32(500000.0) ** (-np.arange(0, ROPE, 2, dtype=f32) / f32(ROPE))
    rope = []
    for length in (S_PROMPT, S_SAMPLE):
        ang = (np.arange(length, dtype=f32)[:, None] * inv.astype(f32)[None, :]).astype(f32)
        rope.append(np.concatenate([np.cos(ang), np.sin(ang)], 1))
    rope = np.concatenate(rope).astype(f32)
    band = np.full((3, P, 3 * P), NEG, f32)
    q, k = np.arange(P)[:, None], np.arange(P)[None, :]
    for n in range(3):
        if n > 0:
            band[n, :, 0:P] = np.where(k >= q, 0, NEG)
        band[n, :, P:2 * P] = 0
        if n < 2:
            band[n, :, 2 * P:] = np.where(k <= q, 0, NEG)
    which = [0] + [1] * (TP - 2) + [2] + [0] + [1] * (TILES - TP - 2) + [2]
    return {"const_f": c, "const_levels": levels.reshape(P, -1), "const_rope": rope,
            "const_tok": (np.arange(P)[:, None] + P * np.arange(TILES)[None, :]).astype(np.int32),
            "const_band": band[which]}


class Phase:

    def __init__(self, nc, name):
        self.nc, self.name, self.sems, self.ctx = nc, name, [], ExitStack()

    def sb(self, name, shape, dt=F32):
        return self.ctx.enter_context(self.nc.sbuf_tensor(f"{self.name}__{name}", shape, dt))

    def banks(self, n=8):
        return [self.ctx.enter_context(self.nc.psum_tensor(f"{self.name}__bank{b}", [P, 512], F32)) for b in range(n)]

    def sem(self, name):
        s = self.nc.alloc_semaphore(f"{self.name}__{name}")
        self.sems.append(s)
        return s

    def __enter__(self):
        return self

    def __exit__(self, *exc):
        if exc[0] is None:
            nums = sorted(s.num for s in self.sems)
            assert nums == list(range(nums[0], nums[-1] + 1))
            self.nc.clear_and_free_semaphores(range(nums[0], nums[-1] + 1))
            self.nc.all_engine_barrier()
        self.ctx.close()
        return False


class Chain:

    def __init__(self, eng, sem, per=0, base=0):
        self.eng, self.sem, self.per, self.base, self.n, self.i = eng, sem, per, base, 0, 0

    def turn(self, i):
        self.i, self.n = i, 0

    def end(self):
        assert self.n == self.per, f"{self.sem.name}: {self.n} links a turn, not {self.per}"

    def __call__(self, ins):
        self.n += 1
        ins.then_inc(self.sem, 1)
        self.eng.wait_ge(self.sem, self.i * self.per + (self.base + self.n))


def ada_modulation(nc, a):
    N = 3 * D // 512
    w_dram = a["ada_w"].rearrange("l s (k p) n -> (l s) p k n", p=P)
    b_dram = a["ada_b"].rearrange("l s n -> (l s) n")
    with Phase(nc, "ada") as ph:
        c_col = ph.sb("c_col", [P, KC, 2])
        c_exp = ph.sb("c_exp", [P, KC, 2])
        c_silu = ph.sb("c_silu", [P, KC, 2])
        w = ph.sb("w", [P, 2, KC, 512])
        bias = ph.sb("bias", [2, 3 * D])
        row = ph.sb("row", [2, 3 * D])
        bank = ph.banks(2)
        c_loaded, w_loaded0, w_loaded1 = ph.sem("c_loaded"), ph.sem("w_loaded0"), ph.sem("w_loaded1")
        w_loaded = (w_loaded0, w_loaded1)
        b_loaded, exp_done, silu_done = ph.sem("b_loaded"), ph.sem("exp_done"), ph.sem("silu_done")
        mm_done, row_done, stored, vec = ph.sem("mm_done"), ph.sem("row_done"), ph.sem("stored"), ph.sem("vec")
        with nc.Block() as block:

            @block.sync
            def _(sp):
                for q, src in enumerate((a["c_prompt"], a["c_sample"])):
                    sp.dma_start(c_col[:, :, q], src.rearrange("a (k p) -> p (a k)", p=P),
                                 allow_slow_non_contiguous=True).then_inc(c_loaded, 16)
                with sp.Fori(0, 4) as m:
                    for n in range(N):
                        i = m * N + n
                        at = sp.snap(i + 1)
                        which = sp.snap(m)
                        sp.wait_ge(mm_done, at)
                        sp.dma_start(w[:, n % 2], w_dram[ds(which, 1), :, :, n * 512:(n + 1) * 512].rearrange(
                            "a p k n -> p (a k) n")).then_inc(w_loaded[n % 2], 16)

            @block.scalar
            def _(act):
                act.wait_ge(c_loaded, 32)
                nc.scalar.activation(c_exp[:], c_col[:], ACT.Exp, scale=-1.0).then_inc(exp_done, 1)
                with act.Fori(0, 4) as m:
                    act.wait_ge(row_done, m * N + 1)
                    act.dma_start(bias[:], b_dram[ds(m, 1), :].broadcast_to([2, 3 * D])).then_inc(b_loaded, 16)
                    act.wait_ge(row_done, m * N + N + 1)
                    act.dma_start(a["mod"][ds(m, 1)].rearrange("a s n -> (a s) n"), row[:]).then_inc(stored, 16)
                act.wait_ge(stored, 16 * 5)

            @block.vector
            def _(dve):
                link = Chain(dve, vec, 2)
                dve.wait_ge(exp_done, 1)
                link(nc.vector.tensor_scalar(c_exp[:], c_exp[:], 1.0, None, ALU.add))
                link(nc.vector.reciprocal(c_exp[:], c_exp[:]))
                nc.vector.tensor_tensor(c_silu[:], c_col[:], c_exp[:], ALU.mult).then_inc(silu_done, 1)
                dve.sem_inc(row_done, 1)
                dve.sem_inc(stored, 16)
                with dve.Fori(0, 4) as m:
                    dve.wait_ge(b_loaded, m * 16 + 16)
                    dve.wait_ge(stored, m * 16 + 16)
                    for n in range(N):
                        dve.wait_ge(mm_done, m * N + (n + 3))
                        cols = slice(n * 512, (n + 1) * 512)
                        nc.vector.tensor_tensor(row[:, cols], bank[n % 2][0:2, :], bias[:, cols],
                                                ALU.add).then_inc(row_done, 1)

            @block.tensor
            def _(pe):
                pe.wait_ge(silu_done, 1)
                pe.sem_inc(mm_done, 2)
                with pe.Fori(0, 4) as m:
                    for n in range(N):
                        i = m * N + n
                        pe.wait_ge(w_loaded[n % 2], m * (16 * N // 2) + 16 * (n // 2 + 1))
                        if n >= 2:
                            pe.wait_ge(row_done, i)
                        else:
                            pe.wait_ge(row_done, m * N + 1)
                        for k in range(KC):
                            mm = nc.tensor.matmul(bank[n % 2][0:2, :], c_silu[:, k, :], w[:, n % 2, k, :],
                                                  start=k == 0, stop=k == KC - 1)
                        mm.then_inc(mm_done, 1)


RWC = 12
CONV0, GATE0, LOW0, AB0 = 12, 24, 28, 31
CHUNKS = 32
PAD = 2
SAMPLE0 = PAD + S_PROMPT + 2 * PAD
ZW = SAMPLE0 + S_SAMPLE + PAD
SPAN = ZW - 2 * PAD


def column_of(c):
    if c < RWC:
        return c * P
    if c < LOW0:
        return (c + 3) * P
    return (c - 16) * P if c < AB0 else AB0 * P


def input_projection(nc, a):
    x_dram, mod, zt, zf = a["x_in"], a["mod"], a["zt"], a["zf"]
    w_dram = a["ab_w_in"][0].rearrange("(k p) n -> p k n", p=P)
    GR = ((0, 512), (512, 512), (1024, 256))
    with Phase(nc, "inp") as ph:
        ident = ph.sb("ident", [P, P])
        hT = ph.sb("hT", [P, KC, T])
        x = ph.sb("x", [P, 2, D])
        scol = ph.sb("scol", [P, 2, 2, KC])
        w = ph.sb("w", [P, 2, KC, P])
        z = ph.sb("z", [P, 2, ZW])
        cb = ph.sb("cb", [P, 2, T])
        tb = ph.sb("tb", [P, 2, TILES, P])
        mu = ph.sb("mu", [P, 15])
        half_mu = ph.sb("half_mu", [P, 15])
        keep = ph.sb("keep", [P, 15])
        taps = ph.sb("taps", [P, 5, 12])
        acc = ph.sb("acc", [P, 2, ZW])
        bank = ph.banks(8)
        zbank = ((bank[0], bank[1], bank[2]), (bank[3], bank[4], bank[5]))
        tbank = (bank[6], bank[7], bank[6])
        cst, xt, ht, prep, vec = (ph.sem(n) for n in ("cst", "x_turned", "hT_ready", "prep", "vec"))
        x_loaded = (ph.sem("x_loaded0"), ph.sem("x_loaded1"))
        w_loaded = (ph.sem("w_loaded0"), ph.sem("w_loaded1"))
        stored = (ph.sem("stored0"), ph.sem("stored1"))
        z_mm, z_ev, cb_ready, conv, tr_mm, t_ev = (
            ph.sem(n) for n in ("z_mm", "z_ev", "cb_ready", "conv", "tr_mm", "t_ev"))
        zf_stored = [ph.sem(f"zf_stored{n}") for n in range(3)]

        def parts(j):
            return ((z[:, j, PAD:PAD + S_PROMPT], cb[:, j, 0:S_PROMPT]),
                    (z[:, j, SAMPLE0:SAMPLE0 + S_SAMPLE], cb[:, j, S_PROMPT:T]))

        with nc.Block() as block:

            @block.sync
            def _(sp):
                sp.dma_start(ident[:], a["const_f"][:, CONST["ident"]]).then_inc(cst, 16)
                for q in range(2):
                    for part in range(2):
                        sp.dma_start(scol[:, q, part], mod[0, q, part * D:(part + 1) * D].rearrange("(k p) -> p k", p=P),
                                     allow_slow_non_contiguous=True).then_inc(cst, 16)
                sp.dma_start(mu[:], a["rw_mu"][0].rearrange("(c p) -> p c", p=P),
                             allow_slow_non_contiguous=True).then_inc(cst, 16)
                for tap in range(5):
                    sp.dma_start(taps[:, tap], a["gd_conv"][0, tap].rearrange("(c p) -> p c", p=P),
                                 allow_slow_non_contiguous=True).then_inc(cst, 16)
                with sp.Fori(0, TILES // 2) as p:
                    for j in range(2):
                        at = sp.snap(2 * p + (j + 1))
                        row = sp.snap((2 * p + j) * P)
                        sp.wait_ge(xt, at)
                        sp.dma_start(x[:, j], x_dram[ds(row, P), :]).then_inc(x_loaded[j], 16)
                sp.sem_inc(stored[0], 16)
                sp.sem_inc(stored[1], 16)

                def store(c, j):
                    at, col = (3 * c + 6, c * P) if isinstance(c, int) else (sp.snap(3 * c + 6), sp.snap(c * P))
                    sp.wait_ge(t_ev, at)
                    sp.dma_start(zt[:, ds(col, P)].rearrange("(t p) f -> p t f", p=P), tb[:, j]).then_inc(stored[j], 16)

                with sp.Fori(0, LOW0 // 2) as p:
                    for j in range(2):
                        store(2 * p + j, j)
                for c in range(LOW0, CHUNKS):
                    if c < AB0:
                        sp.wait_ge(cb_ready, c + 3)
                        sp.dma_start(zf[(c - LOW0) * P:(c - LOW0 + 1) * P, :], cb[:, c % 2]).then_inc(zf_stored[c - LOW0], 16)
                    store(c, c % 2)
                for j in range(2):
                    sp.wait_ge(stored[j], 16 * (CHUNKS // 2 + 1))
                for n in range(3):
                    sp.wait_ge(zf_stored[n], 16)

            @block.tensor
            def _(pe):
                pe.wait_ge(cst, 16 * 11)
                pe.sem_inc(xt, 2)
                with pe.Fori(0, TILES // 2) as p:
                    for j in range(2):
                        pe.wait_ge(x_loaded[j], 16 * p + 16)
                        pe.wait_ge(ht, 2 * p + (j + 1))
                        for k in range(KC):
                            mm = nc.tensor.transpose(bank[2 * j + k // 4][:, (k % 4) * P:(k % 4 + 1) * P],
                                                     x[:, j, k * P:(k + 1) * P], ident[:])
                        mm.then_inc(xt, 1)
                pe.wait_ge(ht, TILES + 2)
                pe.sem_inc(z_mm, 6)
                pe.sem_inc(tr_mm, 6)

                def project(c, j, pair):
                    pe.wait_ge(w_loaded[j], 16 * pair + 16)
                    if not isinstance(c, int) or c > 0:
                        pe.wait_ge(z_ev, 3 * c)
                    for g, (t0, n) in enumerate(GR):
                        for k in range(KC):
                            mm = nc.tensor.matmul(zbank[j][g][:, 0:n], w[:, j, k, :], hT[:, k, t0:t0 + n],
                                                  start=k == 0, stop=k == KC - 1)
                        mm.then_inc(z_mm, 1)

                def turn(c, j):
                    pe.wait_ge(cb_ready, c + 3)
                    pe.wait_ge(t_ev, 3 * c + 3)
                    for g, (t0, n) in enumerate(GR):
                        if g == 2:
                            pe.wait_ge(t_ev, 3 * c + 4)
                        for t in range(n // P):
                            mm = nc.tensor.transpose(tbank[g][:, t * P:(t + 1) * P],
                                                     cb[:, j, t0 + t * P:t0 + (t + 1) * P], ident[:])
                        mm.then_inc(tr_mm, 1)

                project(0, 0, 0)
                with pe.Fori(0, CHUNKS // 2 - 1) as p:
                    project(2 * p + 1, 1, p)
                    turn(2 * p, 0)
                    project(2 * p + 2, 0, p + 1)
                    turn(2 * p + 1, 1)
                project(CHUNKS - 1, 1, CHUNKS // 2 - 1)
                turn(CHUNKS - 2, 0)
                turn(CHUNKS - 1, 1)

            @block.scalar
            def _(act):
                act.sem_inc(z_ev, 3)
                act.sem_inc(t_ev, 3)

                def evacuate(c, j):
                    act.wait_ge(cb_ready, c + 1)
                    for g in range(3):
                        n = GR[g][1]
                        act.wait_ge(z_mm, 3 * c + (g + 7))
                        start = PAD + GR[g][0] if g < 2 else SAMPLE0
                        nc.scalar.activation(z[:, j, start:start + n], zbank[j][g][:, 0:n], ACT.Copy).then_inc(z_ev, 1)

                def turned(c, j, pair):
                    act.wait_ge(stored[j], 16 * pair + 16)
                    for g, (t0, n) in enumerate(GR):
                        act.wait_ge(tr_mm, 3 * c + (g + 7))
                        nc.scalar.activation(tb[:, j, t0 // P:(t0 + n) // P, :].rearrange("p t f -> p (t f)"),
                                             tbank[g][:, 0:n], ACT.Copy).then_inc(t_ev, 1)

                def from_z(c, j, f, n_prep):
                    act.wait_ge(z_ev, 3 * c + 6)
                    act.wait_ge(tr_mm, 3 * c + 3)
                    (z0, c0), (z1, c1) = parts(j)
                    nc.scalar.activation(c0, z0, f).then_inc(prep, 1)
                    act.wait_ge(prep, n_prep)
                    nc.scalar.activation(c1, z1, f).then_inc(cb_ready, 1)

                def in_place(j, f, n_conv):
                    act.wait_ge(conv, n_conv)
                    nc.scalar.activation(cb[:, j], cb[:, j], f).then_inc(cb_ready, 1)

                act.wait_ge(prep, 4)
                evacuate(0, 0)
                with act.Fori(0, RWC // 2) as p:
                    for j in range(2):
                        evacuate(2 * p + (j + 1), 1 - j)
                        turned(2 * p + j, j, p)
                with act.Fori(CONV0 // 2, GATE0 // 2) as p:
                    for j in range(2):
                        in_place(j, ACT.Silu, 2 * p + (j + 2 - CONV0))
                        evacuate(2 * p + (j + 1), 1 - j)
                        turned(2 * p + j, j, p)
                with act.Fori(GATE0 // 2, LOW0 // 2) as p:
                    for j in range(2):
                        from_z(2 * p + j, j, ACT.Silu, 2 * p + (j + 5 - GATE0))
                        evacuate(2 * p + (j + 1), 1 - j)
                        turned(2 * p + j, j, p)
                in_place(0, ACT.Tanh, 14)
                evacuate(LOW0 + 1, 1)
                turned(LOW0, 0, LOW0 // 2)
                evacuate(LOW0 + 2, 0)
                turned(LOW0 + 1, 1, LOW0 // 2)
                in_place(0, ACT.Sigmoid, 15)
                evacuate(AB0, 1)
                turned(LOW0 + 2, 0, LOW0 // 2 + 1)
                act.wait_ge(zf_stored[1], 16)
                from_z(AB0, 1, ACT.Copy, 9)
                turned(AB0, 1, AB0 // 2)

            @block.vector
            def _(dve):
                for lo, hi in ((0, PAD), (PAD + S_PROMPT, SAMPLE0), (SAMPLE0 + S_SAMPLE, ZW)):
                    nc.vector.memset(z[:, :, lo:hi], 0.0).then_inc(prep, 1)
                dve.wait_ge(cst, 16 * 11)
                link = Chain(dve, vec, 3)
                link(nc.vector.tensor_scalar(scol[:, :, 1], scol[:, :, 1], 1.0, None, ALU.add))
                link(nc.vector.tensor_scalar(half_mu[:], mu[:], 0.5, None, ALU.mult))
                link(nc.vector.tensor_scalar(keep[:], mu[:], -1.0, 1.0, ALU.mult, ALU.add))
                dve.sem_inc(prep, 1)
                dve.sem_inc(ht, 2)
                for q, (first, last) in enumerate(SEQ_TILES):
                    with dve.Fori(first // 2, last // 2) as p:
                        for j in range(2):
                            dve.wait_ge(xt, 2 * p + (j + 3))
                            at = dve.snap((2 * p + j) * P)
                            for k in range(KC):
                                ins = nc.vector.tensor_scalar(hT[:, k, ds(at, P)],
                                                              bank[2 * j + k // 4][:, (k % 4) * P:(k % 4 + 1) * P],
                                                              scol[:, q, 1, k:k + 1], scol[:, q, 0, k:k + 1], ALU.mult, ALU.add)
                            ins.then_inc(ht, 1)
                dve.sem_inc(cb_ready, 2)
                dve.sem_inc(conv, 1)

                def shift(c, j, m, step, signal, last, n_last):
                    dve.wait_ge(z_ev, 3 * c + 6)
                    dve.wait_ge(tr_mm, 3 * c + 3)
                    dve.wait_ge(last, n_last)
                    nc.vector.tensor_tensor(acc[:, 0, 0:SPAN], z[:, j, PAD - 1:PAD - 1 + SPAN],
                                            z[:, j, PAD + 1:PAD + 1 + SPAN], ALU.add).then_inc(vec, 1)
                    dve.wait_ge(vec, step + 1)
                    nc.vector.tensor_scalar(acc[:, 1, 0:SPAN], z[:, j, PAD:PAD + SPAN], keep[:, m], None,
                                            ALU.mult).then_inc(vec, 1)
                    dve.wait_ge(vec, step + 2)
                    for n, (lo, hi, out) in enumerate(((0, S_PROMPT, 0), (SAMPLE0 - PAD, SAMPLE0 - PAD + S_SAMPLE, S_PROMPT))):
                        nc.vector.scalar_tensor_tensor(cb[:, j, out:out + hi - lo], acc[:, 0, lo:hi], half_mu[:, m],
                                                       acc[:, 1, lo:hi], ALU.mult, ALU.add).then_inc(signal if n else vec, 1)

                with dve.Fori(0, RWC // 2) as p:
                    for j in range(2):
                        shift(2 * p + j, j, ds(dve.snap(2 * p + j), 1), 6 * p + (3 * j + 3),
                              cb_ready, cb_ready, 2 * p + (j + 2))
                steps = 3 + 3 * RWC
                dve.wait_ge(cb_ready, RWC + 2)
                with dve.Fori(CONV0 // 2, GATE0 // 2) as p:
                    for j in range(2):
                        tap = [taps[:, k, ds(dve.snap(2 * p + (j - CONV0)), 1)] for k in range(5)]
                        step = 10 * p + (5 * j + steps - 5 * CONV0)
                        dve.wait_ge(z_ev, 6 * p + (3 * j + 6))
                        dve.wait_ge(tr_mm, 6 * p + (3 * j + 3))
                        dve.wait_ge(conv, 2 * p + (j + 1 - CONV0))
                        nc.vector.tensor_scalar(acc[:, 0, 0:SPAN], z[:, j, 0:SPAN], tap[0], None, ALU.mult).then_inc(vec, 1)
                        for k in range(1, 4):
                            dve.wait_ge(vec, step + k)
                            nc.vector.scalar_tensor_tensor(acc[:, k % 2, 0:SPAN], z[:, j, k:k + SPAN], tap[k],
                                                           acc[:, (k - 1) % 2, 0:SPAN], ALU.mult, ALU.add).then_inc(vec, 1)
                        dve.wait_ge(vec, step + 4)
                        for n, (lo, hi, out) in enumerate(((0, S_PROMPT, 0), (SAMPLE0 - PAD, SAMPLE0 - PAD + S_SAMPLE, S_PROMPT))):
                            nc.vector.scalar_tensor_tensor(cb[:, j, out:out + hi - lo], z[:, j, lo + 4:hi + 4], tap[4],
                                                           acc[:, 1, lo:hi], ALU.mult, ALU.add).then_inc(conv if n else vec, 1)
                steps += 5 * (GATE0 - CONV0)
                shift(LOW0, 0, slice(12, 13), steps, conv, conv, 13)
                shift(LOW0 + 1, 1, slice(13, 14), steps + 3, cb_ready, conv, 14)
                dve.wait_ge(zf_stored[0], 16)
                shift(LOW0 + 2, 0, slice(14, 15), steps + 6, conv, cb_ready, LOW0 + 4)

            @block.gpsimd
            def _(pool):
                for first, last, shift in ((0, RWC, 0), (RWC, LOW0, 3 * P)):
                    with pool.Fori(first // 2, last // 2) as p:
                        for j in range(2):
                            at = pool.snap(6 * p + (3 * j + 3))
                            col = pool.snap((2 * p + j) * P + shift)
                            pool.wait_ge(z_mm, at)
                            pool.dma_start(w[:, j], w_dram[:, :, ds(col, P)]).then_inc(w_loaded[j], 16)
                for c in range(LOW0, CHUNKS):
                    n = P if c < AB0 else 4 * GD_H
                    pool.wait_ge(z_mm, 3 * c + 3)
                    pool.dma_start(w[:, c % 2, :, 0:n], w_dram[:, :, column_of(c):column_of(c) + n]).then_inc(w_loaded[c % 2], 16)




def mixer_runs():
    return [(lo, hi, 0, lo + hi - 1) for lo, hi in SEQ_TILES]


class Inverse:
    X_TURN, Y_TURN, D_TURN = 2 * LEVELS, LEVELS, LEVELS - 1

    def __init__(self, ph, neg_aT, y_bank, t_bank):
        self.neg_aT, self.y_bank, self.t_bank = neg_aT, y_bank, t_bank
        self.X = ph.sb("X", [P, 2, 4, P])
        self.XT = ph.sb("XT", [P, 2, 4, P])
        self.Y = ph.sb("Y", [P, 2, 4, P])
        self.x_done = [ph.sem(f"x_done{e}") for e in range(2)]
        self.y_mm = [ph.sem(f"y_mm{e}") for e in range(2)]
        self.y_ev = [ph.sem(f"y_ev{e}") for e in range(2)]
        self.d_mm = [ph.sem(f"d_mm{e}") for e in range(2)]
        self.update = ph.sem("update")
        self.dt_mm = [ph.sem(f"dt_mm{e}") for e in range(2)]

    def tensor(self, pe, i):
        for n in range(LEVELS):
            for e in range(2):
                pe.wait_ge(self.x_done[e], i * self.X_TURN + max(1, 2 * n))
                for q in range(4):
                    mm = pe.matmul(self.y_bank[e][:, q * P:(q + 1) * P], self.neg_aT(e, q), self.X[:, e, q, :],
                                   start=True, stop=True)
                mm.then_inc(self.y_mm[e], 1)
            for e in range(2):
                pe.wait_ge(self.y_ev[e], i * self.Y_TURN + (n + 1))
                pe.wait_ge(self.x_done[e], i * self.X_TURN + (2 * n + 1))
                if n < LEVELS - 1:
                    for q in range(4):
                        mm = pe.matmul(self.y_bank[e][:, q * P:(q + 1) * P], self.XT[:, e, q, :], self.Y[:, e, q, :],
                                       start=True, stop=True)
                    mm.then_inc(self.d_mm[e], 1)
                for q in range(4):
                    mm = pe.matmul(self.t_bank[e][:, q * P:(q + 1) * P], self.Y[:, e, q, :], self.XT[:, e, q, :],
                                   start=True, stop=True)
                mm.then_inc(self.dt_mm[e], 1)

    def scalar(self, act, i):
        for n in range(LEVELS):
            for e in range(2):
                act.wait_ge(self.y_mm[e], i * self.Y_TURN + (n + 1))
                if n > 0:
                    act.wait_ge(self.dt_mm[e], i * self.Y_TURN + n)
                act.activation(self.Y[:, e].rearrange("p q t -> p (q t)"), self.y_bank[e][:], ACT.Copy).then_inc(
                    self.y_ev[e], 1)

    def vector(self, dve, i, mask):
        for n in range(LEVELS):
            for e in range(2):
                dve.wait_ge(self.dt_mm[e], i * self.Y_TURN + (n + 1))
                dve.sem_inc(self.update, 1)
                if n < LEVELS - 1:
                    dve.copy_predicated(self.X[:, e], mask(e, n, False).unsqueeze(1).broadcast_to([P, 4, P]),
                                        self.y_bank[e][:].rearrange("p (q t) -> p q t", q=4)).then_inc(self.x_done[e], 1)
                dve.copy_predicated(self.XT[:, e], mask(e, n, True).unsqueeze(1).broadcast_to([P, 4, P]),
                                    self.t_bank[e][:].rearrange("p (q t) -> p q t", q=4)).then_inc(self.x_done[e], 1)


def heads(ap, n):
    return ap.rearrange("p (h n) -> p h n", n=n)


def per_head(col, n):
    return col.unsqueeze(2).broadcast_to([P, col.shape[1], n])


def rwkv_mixer(nc, a):
    zt, zf, y_out, bonus_out = a["zt"], a["zf"], a["rw_y"], a["rw_bonus"]
    with Phase(nc, "rwkv") as ph:
        cf = ph.sb("consts", [P, CONST_W])
        levels = ph.sb("levels", [P, 2, LEVELS, P], I32)
        rkv = ph.sb("rkv", [P, 3, RW_W])
        low = ph.sb("low", [65, 2, P])
        up = ph.sb("up", [65, 2, 2, RW_W])
        rows = ph.sb("rows", [P, 3, RW_W])
        gates = ph.sb("gates", [P, 2, RW_W])
        dec = ph.sb("dec", [P, 3, RW_W])
        ec = ph.sb("ec", [P, 4])
        zero = ph.sb("zero", [P, D])
        kk = ph.sb("kk", [P, RW_W])
        kdir = ph.sb("kdir", [P, RW_W])
        tmp = ph.sb("tmp", [P, RW_W])
        tmp2 = ph.sb("tmp2", [P, RW_W])
        norm = ph.sb("norm", [P, RW_H])
        bonus = ph.sb("bonus", [P, RW_H])
        alpha = ph.sb("alpha", [P, RW_W])
        rho = ph.sb("rho", [P, RW_W])
        beta = ph.sb("beta", [P, RW_W])
        kappa = ph.sb("kappa", [P, RW_W])
        arT = ph.sb("arT", [P, 4, 2, P])
        bT = ph.sb("bT", [P, 4, P])
        kT = ph.sb("kT", [P, 4, P])
        BP = ph.sb("BP", [P, 2, 4, 2, P])
        KP = ph.sb("KP", [P, 2, 4, 2, P])
        H = ph.sb("H", [P, 4, P])
        Hp = ph.sb("Hp", [P, 4, P])
        Xs = ph.sb("Xs", [P, RW_W])
        Un = ph.sb("Un", [P, RW_W])
        y = ph.sb("y", [P, RW_W])
        bank = ph.banks(8)
        inv = Inverse(ph, lambda e, q: BP[:, e, q, 0, :], (bank[1], bank[3]), (bank[2], bank[4]))
        cst, ins_l, v_l, vec, reset = (ph.sem(n) for n in ("cst", "inputs_loaded", "v_loaded", "vec", "reset"))
        zeroed, zero_st = ph.sem("zeroed"), ph.sem("zero_stored")
        raw, e_done, sig, cum, dec_ready, sq, root = (
            ph.sem(n) for n in ("raw_mm", "exp_raw", "sigmoids", "cum_mm", "decays", "squares", "root"))
        ops, tr, tr_ev, prod, prod_ev, hp, x_mm, x_ev, u_mm, u_ev, y_mm, y_ev, h_mm, done, prep_done, y_st, b_rd, b_st, b_free = (
            ph.sem(n) for n in ("operands", "turned", "turned_ev", "products", "products_ev", "state_scaled", "x_mm", "x_ev",
                                "u_mm", "u_ev", "out_mm", "out_ev", "state_mm", "turn_done", "prep_done", "y_stored",
                                "bonus_ready", "bonus_stored", "bonus_free"))

        plan = [(d, d * TILES + lo, d * TILES + hi, lo, hi) for d in range(2) for lo, hi in SEQ_TILES]

        def row_of(d, lo, hi, i):
            return i * P if d == 0 else i * -P + (hi - 1 + lo + TILES) * P

        with nc.Block() as block:

            @block.sync
            def _(sp):
                sp.dma_start(cf[:], a["const_f"]).then_inc(cst, 16)
                sp.dma_start(levels[:].rearrange("p d n t -> p (d n t)"), a["const_levels"]).then_inc(cst, 16)
                for n, name in enumerate(("rw_k_k", "rw_k_a")):
                    sp.dma_start(rows[:, n], a[name].broadcast_to([P, RW_W])).then_inc(cst, 16)
                sp.dma_start(rows[:, 2], a["rw_r_k"].rearrange("a h n -> a (h n)").broadcast_to([P, RW_W])).then_inc(cst, 16)
                for n, (u, b) in enumerate((("rw_w_up", "rw_w0"), ("rw_a_up", "rw_a0"))):
                    sp.dma_start(up[0:64, :, n], a[u][0].rearrange("d r c -> r d c")).then_inc(cst, 16)
                    sp.dma_start(up[64:65, :, n], a[b]).then_inc(cst, 16)
                sp.wait_ge(zeroed, 1)
                sp.dma_start(a["y_rows"][E * P:, :].rearrange("(n p) c -> p n c", p=P),
                             zero[:].unsqueeze(1).broadcast_to([P, OVER, D])).then_inc(zero_st, 16)
                for d, first, last, lo, hi in plan:
                    with sp.Fori(first, last) as i:
                        at = sp.snap(i + 1)
                        row = sp.snap(row_of(d, lo, hi, i))
                        sp.wait_ge(prep_done, at)
                        sp.dma_start(rkv[:, 0:2, :].rearrange("p a c -> p (a c)"), zt[ds(row, P), 0:2 * RW_W]).then_inc(ins_l, 16)
                        for n in range(2):
                            sp.dma_start(low[0:64, n, :], zf[n * P + 64 * d:n * P + 64 * d + 64, ds(row, P)]).then_inc(ins_l, 16)
                        at2 = sp.snap(i + 1)
                        sp.wait_ge(done, at2)
                        sp.dma_start(rkv[:, 2, :], zt[ds(row, P), 2 * RW_W:3 * RW_W]).then_inc(v_l, 16)

                sp.wait_ge(zero_st, 16)

            @block.tensor
            def _(pe):
                pe.wait_ge(cst, 16 * 9)
                ident = cf[:, CONST["ident"]]
                for d, first, last, lo, hi in plan:
                    with pe.Fori(first, last) as i:
                        pe.wait_ge(done, i + 1)
                        pe.wait_ge(ins_l, i * 48 + 48)
                        for n in range(2):
                            mm = pe.matmul(bank[n][:], low[:, n, :], up[:, d, n, :], start=True, stop=True)
                            mm.then_inc(raw, 1)
                        pe.wait_ge(sig, i + 1)
                        pe.matmul(bank[2][:], cf[:, CONST[f"cum_incl{d}"]], gates[:, 0], start=True, stop=True)
                        pe.matmul(bank[3][:], cf[:, CONST[f"cum_excl{d}"]], gates[:, 0], start=True, stop=True)
                        for q in range(4):
                            mm = pe.matmul(bank[4][:, q:q + 1], gates[:, 0, q * P:(q + 1) * P], cf[:, CONST["half"]],
                                           start=True, stop=True)
                        mm.then_inc(cum, 1)
                        for n, (src, b) in enumerate(((alpha, 5), (rho, 6), (beta, 7), (kappa, 0))):
                            pe.wait_ge(ops, i * 4 + (n + 1))
                            for q in range(4):
                                mm = pe.transpose(bank[b][:, q * P:(q + 1) * P], src[:, q * P:(q + 1) * P], ident)
                            mm.then_inc(tr, 1)
                        pe.wait_ge(tr_ev, i * 4 + 4)
                        pe.wait_ge(dec_ready, i * 4 + 4)
                        for kind, src in ((0, bT), (1, kT)):
                            for q in range(4):
                                for e in range(2):
                                    half = slice(64 * e, 64 * e + 64)
                                    b = bank[(1 + 2 * kind + 4 * e + q // 2) % 8]
                                    mm = pe.matmul(b[:, (q % 2) * 256:(q % 2 + 1) * 256], src[half, q, :],
                                                   arT[half, q].rearrange("p a t -> p (a t)"), start=True, stop=True)
                                    if q % 2 == 1:
                                        mm.then_inc(prod, 1)
                        pe.wait_ge(prod_ev, i * 8 + 8)
                        pe.wait_ge(hp, i + 1)
                        pe.wait_ge(v_l, i * 16 + 16)
                        for b, part in ((5, 0), (6, 1)):
                            for q in range(4):
                                pe.matmul(bank[b][:, q * P:(q + 1) * P], arT[:, q, part, :], Hp[:, q, :], start=q == 0, stop=False,
                                          skip_group_check=True)
                                for e in range(2):
                                    c = (2 * q + e) * 64
                                    mm = pe.matmul(bank[b][:, c:c + 64], KP[:, e, q, part, :], rkv[:, 2, c:c + 64],
                                                   start=False, stop=part == 0, skip_group_check=True)
                            if part == 0:
                                mm.then_inc(x_mm, 1)
                        inv.tensor(pe, i)
                        pe.wait_ge(x_ev, i + 1)
                        for e in range(2):
                            pe.wait_ge(inv.x_done[e], i * inv.X_TURN + inv.X_TURN)
                        for q in range(4):
                            for e in range(2):
                                c = (2 * q + e) * 64
                                mm = pe.matmul(bank[7][:, c:c + 64], inv.XT[:, e, q, :], Xs[:, c:c + 64], start=True, stop=True)
                        mm.then_inc(u_mm, 1)
                        pe.wait_ge(u_ev, i + 1)
                        for q in range(4):
                            for e in range(2):
                                c = (2 * q + e) * 64
                                mm = pe.matmul(bank[6][:, c:c + 64], BP[:, e, q, 1, :], Un[:, c:c + 64], start=False, stop=True,
                                               skip_group_check=True)
                        mm.then_inc(y_mm, 1)
                        for q in range(4):
                            pair = slice(q * P, (q + 1) * P)
                            pe.matmul(bank[0][:, pair], kappa[:, pair], rkv[:, 2, pair], start=True, stop=False)
                            mm = pe.matmul(bank[0][:, pair], beta[:, pair], Un[:, pair], start=False, stop=True)
                        mm.then_inc(h_mm, 1)

            @block.scalar
            def _(act):
                act.sem_inc(y_st, 16)
                for d, first, last, lo, hi in plan:
                    with act.Fori(first, last) as i:
                        for n in range(2):
                            act.wait_ge(raw, i * 2 + (n + 1))
                            act.activation(gates[:, n], bank[n][:], ACT.Exp, scale=-1.0).then_inc(e_done, 1)
                        act.wait_ge(cum, i + 1)
                        act.activation(dec[:, 2], bank[3][:], ACT.Exp).then_inc(dec_ready, 1)
                        act.activation(dec[:, 0], bank[2][:], ACT.Exp).then_inc(dec_ready, 1)
                        act.activation(dec[:, 1], bank[2][:], ACT.Exp, scale=-1.0).then_inc(dec_ready, 1)
                        act.activation(ec[:], bank[4][:, 0:4], ACT.Exp).then_inc(dec_ready, 1)
                        act.wait_ge(sq, i + 1)
                        act.activation(norm[:], norm[:], ACT.Sqrt).then_inc(root, 1)
                        for n, (dst, b) in enumerate(((arT[:, :, 0, :], 5), (arT[:, :, 1, :], 6), (bT[:], 7), (kT[:], 0))):
                            act.wait_ge(tr, i * 4 + (n + 1))
                            act.activation(dst, heads(bank[b][:], P), ACT.Copy).then_inc(tr_ev, 1)
                        act.wait_ge(x_mm, i + 1)
                        act.activation(Xs[:], bank[5][:], ACT.Copy).then_inc(x_ev, 1)
                        inv.scalar(act, i)
                        act.wait_ge(u_mm, i + 1)
                        act.activation(Un[:], bank[7][:], ACT.Copy, scale=-1.0).then_inc(u_ev, 1)
                        act.wait_ge(y_mm, i + 1)
                        act.wait_ge(y_st, i * 16 + 16)
                        act.activation(y[:], bank[6][:], ACT.Copy).then_inc(y_ev, 1)
                        act.wait_ge(y_ev, i + 1)
                        act.dma_start(y_out[d, ds(act.snap(row_of(d, lo, hi, i)), P), :], y[:]).then_inc(y_st, 16)
                act.wait_ge(y_st, 16 * (2 * TILES + 1))

            @block.gpsimd
            def _(pool):
                for d, first, last, lo, hi in plan:
                    with pool.Fori(first, last) as i:
                        pool.wait_ge(b_rd, i + 1)
                        pool.dma_start(bonus_out[d, ds(pool.snap(row_of(d, lo, hi, i)), P), :], bonus[:]).then_inc(b_st, 16)
                        pool.wait_ge(b_st, i * 16 + 16)
                        pool.sem_inc(b_free, 1)

            @block.vector
            def _(dve):
                dve.memset(zero[:], 0.0).then_inc(zeroed, 1)
                dve.memset(low[64:65], 1.0).then_inc(vec, 1)
                dve.wait_ge(vec, 1)
                dve.wait_ge(cst, 16 * 9)
                dve.sem_inc(prep_done, 1)
                dve.sem_inc(done, 1)
                dve.sem_inc(b_free, 1)
                link = Chain(dve, vec, 20, 1)
                for d, first, last, lo, hi in plan:
                    dve.memset(H[:], 0.0).then_inc(reset, 1)
                    dve.wait_ge(reset, 1 + plan.index((d, first, last, lo, hi)))
                    with dve.Fori(first, last) as i:
                        link.turn(i)
                        dve.wait_ge(ins_l, i * 48 + 48)
                        dve.wait_ge(done, i + 1)
                        link(dve.tensor_tensor(kk[:], rkv[:, 1], rows[:, 0], ALU.mult))
                        link(dve.tensor_tensor(tmp[:], kk[:], kk[:], ALU.mult))
                        link(dve.tensor_reduce(norm[:], heads(tmp[:], 64), AX.X, ALU.add))
                        dve.tensor_scalar(norm[:], norm[:], 1e-12, None, ALU.add).then_inc(sq, 1)
                        dve.wait_ge(e_done, i * 2 + 1)
                        link(dve.tensor_scalar(gates[:, 0], gates[:, 0], 1.0, None, ALU.add))
                        dve.reciprocal(gates[:, 0], gates[:, 0]).then_inc(sig, 1)
                        dve.wait_ge(e_done, i * 2 + 2)
                        link(dve.tensor_scalar(gates[:, 1], gates[:, 1], 1.0, None, ALU.add))
                        link(dve.reciprocal(gates[:, 1], gates[:, 1]))
                        link(dve.scalar_tensor_tensor(tmp[:], gates[:, 1], -1.0, rows[:, 1], ALU.add, ALU.mult))
                        link(dve.scalar_tensor_tensor(kdir[:], tmp[:], 1.0, rkv[:, 1], ALU.add, ALU.mult))
                        link(dve.tensor_tensor(tmp[:], rkv[:, 0], rows[:, 2], ALU.mult))
                        link(dve.tensor_tensor(tmp2[:], tmp[:], kdir[:], ALU.mult))
                        dve.wait_ge(b_free, i + 1)
                        dve.tensor_reduce(bonus[:], heads(tmp2[:], 64), AX.X, ALU.add).then_inc(b_rd, 1)
                        dve.wait_ge(root, i + 1)
                        link(dve.reciprocal(norm[:], norm[:]))
                        link(dve.tensor_tensor(heads(kk[:], 64), heads(kk[:], 64), per_head(norm[:], 64), ALU.mult))
                        link(dve.tensor_tensor(tmp[:], kk[:], gates[:, 1], ALU.mult))
                        dve.wait_ge(dec_ready, i * 4 + 3)
                        dve.tensor_tensor(alpha[:], kk[:], dec[:, 2], ALU.mult).then_inc(ops, 1)
                        dve.tensor_tensor(rho[:], rkv[:, 0], dec[:, 0], ALU.mult).then_inc(ops, 1)
                        dve.tensor_tensor(beta[:], tmp[:], dec[:, 1], ALU.mult).then_inc(ops, 1)
                        dve.tensor_tensor(kappa[:], kdir[:], dec[:, 1], ALU.mult).then_inc(ops, 1)
                        dve.wait_ge(ops, i * 4 + 4)
                        dve.sem_inc(prep_done, 1)
                        dve.wait_ge(dec_ready, i * 4 + 4)
                        dve.tensor_tensor(Hp[:], H[:], per_head(ec[:], P), ALU.mult).then_inc(hp, 1)
                        for e in range(2):
                            for x in (inv.X, inv.XT):
                                link(dve.tensor_copy(x[:, e], cf[:, CONST["ident"]].unsqueeze(1).broadcast_to([P, 4, P])))
                            dve.sem_inc(inv.x_done[e], 1)
                        for kind, dst, mask in ((0, BP, f"mask_b{d}"), (1, KP, f"mask_k{d}")):
                            for q in (0, 2):
                                for e in range(2):
                                    b = bank[(1 + 2 * kind + 4 * e + q // 2) % 8]
                                    dve.wait_ge(prod, i * 8 + (4 * kind + q + e + 1))
                                    dve.tensor_tensor(dst[:, e, q:q + 2].rearrange("p q a t -> p q (a t)"),
                                                      heads(b[:], 256),
                                                      cf[:, CONST[mask]].unsqueeze(1).broadcast_to([P, 2, 256]),
                                                      ALU.mult).then_inc(prod_ev, 1)
                        inv.vector(dve, i, lambda e, n, t: levels[:, d if t else 1 - d, n, :])
                        dve.wait_ge(h_mm, i + 1)
                        link(dve.tensor_tensor(H[:], heads(bank[0][:], P),
                                               cf[:, CONST["diag2"]].unsqueeze(1).broadcast_to([P, 4, P]), ALU.mult))
                        link(dve.tensor_tensor(H[:], H[:], Hp[:], ALU.add))
                        link(dve.tensor_tensor(H[:], H[:], per_head(ec[:], P), ALU.mult))
                        dve.wait_ge(y_ev, i + 1)
                        dve.sem_inc(done, 1)
                        link.end()


def deltanet_mixer(nc, a):
    zt, o_out = a["zt"], a["gd_o"]
    QKV0, AB = RWC * P, AB0 * P
    with Phase(nc, "delta") as ph:
        cf = ph.sb("consts", [P, CONST_W])
        levels = ph.sb("levels", [P, 2, LEVELS, P], I32)
        dt = ph.sb("dt", [P, 8])
        neg_a = ph.sb("neg_a", [P, 8])
        qkv = ph.sb("qkv", [P, 2, 3, GD_W])
        ab = ph.sb("ab", [P, 2, 16])
        sqr = ph.sb("sqr", [P, 2, 8, P])
        norm = ph.sb("norm", [P, 16])
        g = ph.sb("g", [P, 8])
        t8 = ph.sb("t8", [P, 3, 8])
        beta = ph.sb("beta", [P, 8])
        gb = ph.sb("gb", [P, 8, P])
        gc = ph.sb("gc", [P, 16])
        eg = ph.sb("eg", [P, 3, 8])
        bg = ph.sb("bg", [P, 8])
        DD = ph.sb("DD", [P, 2, 4, 2, P])
        kb = ph.sb("kb", [P, 2, GD_W])
        kd = ph.sb("kd", [P, 2, GD_W])
        kT = ph.sb("kT", [P, 2, 4, P])
        kqT = ph.sb("kqT", [P, 2, 4, 2, P])
        BP = ph.sb("BP", [P, 2, 4, 2, P])
        S = ph.sb("S", [P, 2, 4, P])
        vb = ph.sb("vb", [P, 2, GD_W])
        W = ph.sb("W", [P, 2, GD_W])
        qs = ph.sb("qs", [P, 2, GD_W])
        o = ph.sb("o", [P, 2, GD_W])
        bank = ph.banks(8)
        inv = Inverse(ph, lambda e, q: BP[:, e, q, 0, :], (bank[0], bank[2]), (bank[1], bank[3]))
        cst, q_l, vec, reset, go = (ph.sem(n) for n in ("cst", "inputs_loaded", "vec", "reset", "go"))
        (sq, root, e1, ln, ln_in, g_r, gsum, g_ev, grow, dd_in, dd_e, kb_r, tr, tr_ev, prod, prod_ev, ks, x_r, w_mm, w_ev, o_mm,
         o_r, done, free, st, eb, ex) = (
            ph.sem(n) for n in ("squares", "root", "exp_abs", "softplus_ln", "ln_in", "g_ready", "g_summed", "g_exps", "g_rows",
                                "diff", "diff_exp", "operands", "turned", "turned_ev", "products", "products_ev", "state_mm",
                                "x_ready", "w_mm", "w_ev", "out_mm", "out_ready", "turn_done", "inputs_free", "stored",
                                "exp_b", "exp_in"))

        with nc.Block() as block:

            @block.sync
            def _(sp):
                sp.dma_start(cf[:], a["const_f"]).then_inc(cst, 16)
                sp.dma_start(levels[:].rearrange("p d n t -> p (d n t)"), a["const_levels"]).then_inc(cst, 16)
                sp.dma_start(dt[:], a["gd_dt_bias"].rearrange("a d h -> a (d h)").broadcast_to([P, 8])).then_inc(cst, 16)
                sp.dma_start(neg_a[:], a["gd_A_log"].rearrange("a d h -> a (d h)").broadcast_to([P, 8])).then_inc(cst, 16)
                for first, last, shift, total in mixer_runs():
                    with sp.Fori(first, last) as i:
                        at = sp.snap(i + 1)
                        row = (sp.snap(i * P), sp.snap(i * -P + total * P))
                        sp.wait_ge(free, at)
                        for d in range(2):
                            sp.dma_start(qkv[:, d].rearrange("p a c -> p (a c)"), zt[ds(row[d], P), QKV0:QKV0 + 3 * GD_W]).then_inc(q_l, 16)
                            sp.dma_start(ab[:, d], zt[ds(row[d], P), AB:AB + 16]).then_inc(q_l, 16)

            @block.tensor
            def _(pe):
                pe.wait_ge(cst, 64)
                ident = cf[:, CONST["ident"]]
                for first, last, shift, total in mixer_runs():
                    with pe.Fori(first, last) as i:
                        pe.wait_ge(done, i + 1)
                        pe.wait_ge(g_r, i * 2 + 1)
                        for d in range(2):
                            pe.matmul(bank[0][:, 4 * d:4 * d + 4], cf[:, CONST[f"incl{d}"]], g[:, 4 * d:4 * d + 4],
                                      start=True, stop=True)
                        pe.matmul(bank[0][:, 8:16], cf[:, CONST["ones"]], g[:], start=True, stop=True).then_inc(gsum, 1)
                        pe.wait_ge(g_r, i * 2 + 2)
                        for d in range(2):
                            for h in range(4):
                                mm = pe.matmul(bank[1 + d][:, h * P:(h + 1) * P], gb[:, 4 * d + h, :], cf[:, CONST[f"incl{d}"]],
                                               start=True, stop=True)
                            mm.then_inc(grow, 1)
                        pe.wait_ge(kb_r, i + 1)
                        for n in range(6):
                            d, part = n % 2, n // 2
                            src = (qkv[:, d, 1], kb[:, d], qkv[:, d, 0])[part]
                            b = (3, 4, 5, 6, 7, 3)[n]
                            if n == 5:
                                pe.wait_ge(tr_ev, i * 6 + 1)
                            for h in range(4):
                                mm = pe.transpose(bank[b][:, h * P:(h + 1) * P], src[:, h * P:(h + 1) * P], ident)
                            mm.then_inc(tr, 1)
                        pe.wait_ge(tr_ev, i * 6 + 6)
                        pe.wait_ge(dd_e, i * 2 + 2)
                        for d in range(2):
                            for h in range(4):
                                mm = pe.matmul(bank[2 * d + h // 2][:, (h % 2) * 256:(h % 2 + 1) * 256], kT[:, d, h, :],
                                               kqT[:, d, h].rearrange("p a t -> p (a t)"), start=True, stop=True)
                                if h % 2:
                                    mm.then_inc(prod, 1)
                        for d in range(2):
                            for part, src in ((0, kT[:, d]), (1, kqT[:, d, :, 1, :])):
                                for h in range(4):
                                    mm = pe.matmul(bank[4 + 2 * d + part][:, h * P:(h + 1) * P], src[:, h, :], S[:, d, h, :],
                                                   start=True, stop=True)
                                mm.then_inc(ks, 1)
                        pe.wait_ge(prod_ev, i * 4 + 4)
                        inv.tensor(pe, i)
                        pe.wait_ge(x_r, i * 2 + 2)
                        for d in range(2):
                            pe.wait_ge(inv.x_done[d], i * inv.X_TURN + inv.X_TURN)
                            for h in range(4):
                                mm = pe.matmul(bank[4 + 2 * d][:, h * P:(h + 1) * P], inv.XT[:, d, h, :], vb[:, d, h * P:(h + 1) * P],
                                               start=True, stop=True)
                            mm.then_inc(w_mm, 1)
                        for d in range(2):
                            pe.wait_ge(w_ev, i * 2 + (d + 1))
                            for h in range(4):
                                mm = pe.matmul(bank[5 + 2 * d][:, h * P:(h + 1) * P], BP[:, d, h, 1, :], W[:, d, h * P:(h + 1) * P],
                                               start=True, stop=True)
                            mm.then_inc(o_mm, 1)
                            for h in range(4):
                                mm = pe.matmul(bank[4 + 2 * d][:, h * P:(h + 1) * P], kd[:, d, h * P:(h + 1) * P], W[:, d, h * P:(h + 1) * P],
                                               start=True, stop=True)
                            mm.then_inc(o_mm, 1)

            @block.scalar
            def _(act):
                act.wait_ge(cst, 64)
                act.activation(neg_a[:], neg_a[:], ACT.Exp).then_inc(reset, 1)
                act.sem_inc(st, 32)
                for first, last, shift, total in mixer_runs():
                    with act.Fori(first, last) as i:
                        act.wait_ge(sq, i + 1)
                        act.activation(norm[:], norm[:], ACT.Sqrt).then_inc(root, 1)
                        act.wait_ge(ex, i + 1)
                        act.activation(t8[:, 1], t8[:, 1], ACT.Exp, scale=-1.0).then_inc(e1, 1)
                        act.activation(beta[:].rearrange("p (d h) -> p d h", d=2), t8[:, 2].rearrange("p (d h) -> p d h", d=2),
                                       ACT.Exp, scale=-1.0).then_inc(eb, 1)
                        act.wait_ge(ln_in, i + 1)
                        act.activation(t8[:, 1], t8[:, 1], ACT.Ln).then_inc(ln, 1)
                        act.wait_ge(gsum, i + 1)
                        act.activation(gc[:], bank[0][:, 0:16], ACT.Copy).then_inc(g_ev, 1)
                        act.wait_ge(g_ev, i * 4 + 1)
                        act.activation(eg[:, 0:2].rearrange("p a h -> p (a h)"), gc[:], ACT.Exp).then_inc(g_ev, 1)
                        act.wait_ge(go, i + 1)
                        act.activation(eg[:, 2], t8[:, 0], ACT.Exp).then_inc(g_ev, 1)
                        act.sem_inc(g_ev, 1)
                        for d in range(2):
                            act.wait_ge(dd_in, i * 2 + (d + 1))
                            act.activation(DD[:, d, :, 1, :], DD[:, d, :, 1, :], ACT.Exp).then_inc(dd_e, 1)
                        for n in range(6):
                            d, part = n % 2, n // 2
                            b = (3, 4, 5, 6, 7, 3)[n]
                            dst = (kT[:, d], kqT[:, d, :, 0, :], kqT[:, d, :, 1, :])[part]
                            act.wait_ge(tr, i * 6 + (n + 1))
                            act.activation(dst, heads(bank[b][:], P), ACT.Copy).then_inc(tr_ev, 1)
                        inv.scalar(act, i)
                        for d in range(2):
                            act.wait_ge(w_mm, i * 2 + (d + 1))
                            act.activation(W[:, d], bank[4 + 2 * d][:], ACT.Copy).then_inc(w_ev, 1)
                        for d in range(2):
                            row = i * P if d == 0 else i * -P + total * P
                            act.wait_ge(o_r, i * 2 + (d + 1))
                            act.dma_start(o_out[d, ds(act.snap(row), P), :], o[:, d]).then_inc(st, 16)
                act.wait_ge(st, 32 * (TILES + 1))

            @block.vector
            def _(dve):
                dve.wait_ge(cst, 64)
                dve.wait_ge(reset, 1)
                link = Chain(dve, vec, 36, 1)
                dve.tensor_scalar(neg_a[:], neg_a[:], -1.0, None, ALU.mult).then_inc(vec, 1)
                dve.wait_ge(vec, 1)
                dve.sem_inc(done, 1)
                dve.sem_inc(free, 1)
                for run, (first, last, shift, total) in enumerate(mixer_runs()):
                    dve.memset(S[:], 0.0).then_inc(reset, 1)
                    dve.wait_ge(reset, run + 2)
                    with dve.Fori(first, last) as i:
                        link.turn(i)
                        dve.wait_ge(q_l, i * 64 + 64)
                        for d in range(2):
                            x = qkv[:, d, 0:2].rearrange("p a (h n) -> p (a h) n", n=P)
                            link(dve.tensor_tensor(sqr[:, d], x, x, ALU.mult))
                        link(dve.tensor_reduce(norm[:], sqr[:].rearrange("p d h n -> p (d h) n"), AX.X, ALU.add))
                        dve.tensor_scalar(norm[:], norm[:], 1e-12, None, ALU.add).then_inc(sq, 1)
                        by_d = lambda t: t.rearrange("p (d h) -> p d h", d=2)
                        for d in range(2):
                            link(dve.tensor_tensor(t8[:, 0, 4 * d:4 * d + 4], ab[:, d, 4 * d:4 * d + 4], dt[:, 4 * d:4 * d + 4], ALU.add))
                            link(dve.tensor_copy(t8[:, 2, 4 * d:4 * d + 4], ab[:, d, 8 + 4 * d:12 + 4 * d]))
                        link(dve.tensor_scalar(t8[:, 1], t8[:, 0], -1.0, None, ALU.mult))
                        dve.tensor_tensor(t8[:, 1], t8[:, 1], t8[:, 0], ALU.max).then_inc(ex, 1)
                        dve.wait_ge(e1, i + 1)
                        dve.tensor_scalar(t8[:, 1], t8[:, 1], 1.0, None, ALU.add).then_inc(ln_in, 1)
                        dve.wait_ge(eb, i + 1)
                        link(dve.tensor_scalar(beta[:], beta[:], 1.0, None, ALU.add))
                        link(dve.reciprocal(beta[:], beta[:]))
                        dve.wait_ge(ln, i + 1)
                        link(dve.scalar_tensor_tensor(t8[:, 0], t8[:, 0], 0.0, t8[:, 1], ALU.max, ALU.add))
                        dve.tensor_tensor(g[:], t8[:, 0], neg_a[:], ALU.mult).then_inc(g_r, 1)
                        dve.wait_ge(g_r, i * 2 + 1)
                        dve.tensor_copy(gb[:], per_head(g[:], P)).then_inc(g_r, 1)
                        dve.wait_ge(root, i + 1)
                        link(dve.reciprocal(norm[:], norm[:]))
                        n4 = norm[:].rearrange("p (d a h) -> p d a h", d=2, a=2)
                        for d in range(2):
                            link(dve.scalar_tensor_tensor(heads(qkv[:, d, 0], P), heads(qkv[:, d, 0], P), GD_N ** -0.5,
                                                          per_head(n4[:, d, 0], P), ALU.mult, ALU.mult))
                            link(dve.tensor_tensor(heads(qkv[:, d, 1], P), heads(qkv[:, d, 1], P), per_head(n4[:, d, 1], P), ALU.mult))
                        for d in range(2):
                            ins = dve.tensor_tensor(heads(kb[:, d], P), heads(qkv[:, d, 1], P), per_head(beta[:, 4 * d:4 * d + 4], P), ALU.mult)
                            if d == 0:
                                link(ins)
                            else:
                                ins.then_inc(kb_r, 1)
                        dve.wait_ge(g_ev, i * 4 + 2)
                        dve.tensor_tensor(t8[:, 0], gc[:, 8:16], gc[:, 0:8], ALU.subtract).then_inc(go, 1)
                        link(dve.tensor_tensor(bg[:], beta[:], eg[:, 0], ALU.mult))
                        for d in range(2):
                            dve.wait_ge(grow, i * 2 + (d + 1))
                            for h in range(4):
                                ins = dve.scalar_tensor_tensor(DD[:, d, h, 1, :], bank[1 + d][:, h * P:(h + 1) * P],
                                                               gc[:, 4 * d + h:4 * d + h + 1], cf[:, CONST[f"floor{d}"]],
                                                               ALU.subtract, ALU.add)
                                if h == 3:
                                    ins.then_inc(dd_in, 1)
                        dve.wait_ge(g_ev, i * 4 + 4)
                        for d in range(2):
                            link(dve.tensor_tensor(heads(kd[:, d], P), heads(qkv[:, d, 1], P), per_head(eg[:, 2, 4 * d:4 * d + 4], P), ALU.mult))
                            link(dve.tensor_tensor(heads(vb[:, d], P), heads(qkv[:, d, 2], P), per_head(beta[:, 4 * d:4 * d + 4], P), ALU.mult))
                            dve.wait_ge(dd_e, i * 2 + (d + 1))
                            link(dve.tensor_tensor(DD[:, d, :, 0, :], DD[:, d, :, 1, :],
                                                   cf[:, CONST[f"mask_b{d}"]][:, 0:P].unsqueeze(1).broadcast_to([P, 4, P]), ALU.mult))
                        dve.wait_ge(tr, i * 6 + 6)
                        dve.sem_inc(free, 1)
                        for e in range(2):
                            for x in (inv.X, inv.XT):
                                link(dve.tensor_copy(x[:, e], cf[:, CONST["ident"]].unsqueeze(1).broadcast_to([P, 4, P])))
                            dve.sem_inc(inv.x_done[e], 1)
                        for d in range(2):
                            for n in range(2):
                                dve.wait_ge(prod, i * 4 + (2 * d + n + 1))
                                dve.tensor_tensor(BP[:, d, 2 * n:2 * n + 2].rearrange("p h a t -> p (h a t)"), bank[2 * d + n][:],
                                                  DD[:, d, 2 * n:2 * n + 2].rearrange("p h a t -> p (h a t)"), ALU.mult).then_inc(prod_ev, 1)
                        for d in range(2):
                            dve.wait_ge(ks, i * 4 + (2 * d + 2))
                            link(dve.tensor_tensor(sqr[:, d, 0:4], heads(bank[4 + 2 * d][:], P), per_head(bg[:, 4 * d:4 * d + 4], P), ALU.mult))
                            dve.tensor_tensor(vb[:, d], vb[:, d], sqr[:, d, 0:4].rearrange("p h n -> p (h n)"), ALU.subtract).then_inc(x_r, 1)
                            link(dve.tensor_tensor(heads(qs[:, d], P), heads(bank[5 + 2 * d][:], P), per_head(eg[:, 0, 4 * d:4 * d + 4], P), ALU.mult))
                        inv.vector(dve, i, lambda e, n, t: levels[:, e if t else 1 - e, n, :])
                        dve.wait_ge(st, i * 32 + 32)
                        for d in range(2):
                            link(dve.tensor_tensor(S[:, d], S[:, d], per_head(eg[:, 1, 4 * d:4 * d + 4], P), ALU.mult))
                            dve.wait_ge(o_mm, i * 4 + (2 * d + 2))
                            dve.tensor_tensor(o[:, d], bank[5 + 2 * d][:], qs[:, d], ALU.add).then_inc(o_r, 1)
                            link(dve.tensor_tensor(S[:, d].rearrange("p h n -> p (h n)"), S[:, d].rearrange("p h n -> p (h n)"),
                                                   bank[4 + 2 * d][:], ALU.add))
                        dve.sem_inc(done, 1)
                        link.end()




def mod_row(a, m, q, part):
    return a["mod"][m, q:q + 1, part * D:(part + 1) * D].broadcast_to([P, D])


def normed(dve, link, step, x, out, stats, mv, var_ready, root, n_ready, g_row, b_row):
    for c in range(2):
        link(dve.bn_stats(stats[:, c], x[:, c * 512:(c + 1) * 512]))
    dve.sem_inc(step, 1)
    link(dve.bn_aggr(mv[:, 0:2], stats[:].rearrange("p a b -> p (a b)")))
    dve.tensor_scalar(mv[:, 2:3], mv[:, 1:2], LN_EPS, None, ALU.add).then_inc(var_ready, 1)
    dve.wait_ge(root, n_ready)
    link(dve.reciprocal(mv[:, 2:3], mv[:, 2:3]))
    link(dve.tensor_scalar(x[:], x[:], mv[:, 0:1], mv[:, 2:3], ALU.subtract, ALU.mult))
    link(dve.tensor_tensor(x[:], x[:], g_row, ALU.mult))
    link(dve.tensor_tensor(out[:], x[:], b_row, ALU.add))


def close_mixer(nc, a, layer):
    x_in, x_out, h_out = a["x_in" if layer == 0 else "x_mid2"], a["x_mid"], a["h_rows"]
    w_dram = (a["ab_w_out"] if layer == 0 else a["at_w_out"])[0]
    m = 2 * layer
    with Phase(nc, f"close{layer}") as ph:
        cf = ph.sb("consts", [P, CONST["incl0"].start])
        tok = ph.sb("tok", [P, TILES], I32)
        zero = ph.sb("zero", [P, BLOCKS], I32)
        w_out = ph.sb("w_out", [P, KC, D])
        rows = ph.sb("rows", [P, 5, D])
        x = ph.sb("x", [P, 2, D])
        cat = ph.sb("cat", [P, 2, D])
        catT = ph.sb("catT", [P, KC, P])
        x1 = ph.sb("x1", [P, D])
        x2 = ph.sb("x2", [P, D])
        h = ph.sb("h", [P, D])
        hT = ph.sb("hT", [P, KC, P])
        stats = ph.sb("stats", [P, 2, 6])
        mv = ph.sb("mv", [P, 3])
        rw = ph.sb("rw", [P, KC, E])
        rb = ph.sb("rb", [P, E])
        sc = ph.sb("sc", [P, 2, E])
        r8 = ph.sb("r8", [P, 8, 8])
        r32 = ph.sb("r32", [P, 2, E])
        r4 = ph.sb("r4", [P, 8, PER])
        r1 = ph.sb("r1", [P, 4])
        one = ph.sb("one", [P, 2, TILES + 1, E])
        gate = ph.sb("gate", [P, 2, TILES])
        gsum = ph.sb("gsum", [P, TILES])
        upto = ph.sb("upto", [P, TILES + 1, E])
        place = ph.sb("place", [P, TILES + 1, E])
        nb = ph.sb("nb", [P, 4, E])
        cmp = ph.sb("cmp", [P, BLOCKS, E])
        dest = ph.sb("dest", [P, 2, TILES])
        dest_i = ph.sb("dest_i", [P, 2, TILES], I32)
        blk = ph.sb("blk", [P, 2, BLOCKS])
        blk_i = ph.sb("blk_i", [P, BLOCKS], I32)
        if layer == 0:
            yo = ph.sb("yo", [P, 2, 2, RW_W])
            bon = ph.sb("bon", [P, 2, RW_H])
            v = ph.sb("v", [P, RW_W])
            og = ph.sb("og", [P, GD_W])
            glow = ph.sb("glow", [P, P])
            gup = ph.sb("gup", [P, RW_W])
            gn = ph.sb("gn", [P, 2, RW_W])
            ng = ph.sb("ng", [P, GD_N])
            sq_t = ph.sb("sq_t", [P, RW_W])
            hs = ph.sb("hs", [P, 4, RW_H])
        bank = ph.banks(8)
        cst, rows_l, rows_free, heads_l, heads_free, x_free, vec, vec_a, vec_c, vec_r, own, step = (
            ph.sem(n) for n in ("cst", "rows_loaded", "rows_free", "heads_loaded", "heads_free", "x_free", "vec", "vec_join",
                                "vec_norm", "vec_route", "own", "step"))
        x_l = [ph.sem(f"x_loaded{j}") for j in range(2)]
        gate_mm, hv, hroot, cat_r, cat_tr, cat_ev, out_mm, var_r, root, x1_r, h_r, x_st, h_st, h_tr, h_ev, lg, sg = (
            ph.sem(n) for n in ("gate_mm", "head_vars", "head_roots", "cat_ready", "cat_turned", "cat_ev", "out_mm", "var_ready",
                                "root", "x1_ready", "h_ready", "x_stored", "h_stored", "h_turned", "h_ev", "logits",
                                "exp_logits"))
        pos_in, pos_mm, dest_r, tab, tab_z = (ph.sem(n) for n in ("one_hots_ready", "pos_mm", "dest_ready", "tables_stored", "table_zeroed"))
        scat = ph.sem("scattered")
        XW = 16 if layer == 0 else 32
        NCST = 9 if layer == 0 else 5

        with nc.Block() as block:

            @block.sync
            def _(sp):
                sp.dma_start(cf[:], a["const_f"][:, 0:CONST["incl0"].start]).then_inc(cst, 16)
                sp.dma_start(tok[:], a["const_tok"]).then_inc(cst, 16)
                sp.dma_start(w_out[:], w_dram.rearrange("(k p) n -> p k n", p=P)).then_inc(cst, 16)
                sp.dma_start(rw[:], a["router_w"].rearrange("(k p) n -> p k n", p=P)).then_inc(cst, 16)
                sp.dma_start(rb[:], a["router_bias"].rearrange("(a n) -> a n", a=1).broadcast_to([P, E])).then_inc(cst, 16)
                if layer == 0:
                    sp.dma_start(gup[:], a["rw_g_up"][0]).then_inc(cst, 16)
                    sp.dma_start(gn[:, 0], a["rw_gn_g"].broadcast_to([P, RW_W])).then_inc(cst, 16)
                    sp.dma_start(gn[:, 1], a["rw_gn_b"].broadcast_to([P, RW_W])).then_inc(cst, 16)
                    sp.dma_start(ng[:], a["gd_norm_g"].broadcast_to([P, GD_N])).then_inc(cst, 16)
                sp.wait_ge(tab_z, 1)
                sp.dma_start(a["row_tok"].rearrange("(b p) o -> p (b o)", p=P), zero[:],
                             allow_slow_non_contiguous=True).then_inc(tab, 16)
                def load_rows(q):
                    sp.wait_ge(rows_free, q + 1)
                    for n, src in enumerate((mod_row(a, m, q, 2), mod_row(a, m + 1, q, 1), mod_row(a, m + 1, q, 0),
                                             a["ln_g"][layer, 0:1].broadcast_to([P, D]),
                                             a["ln_b"][layer, 0:1].broadcast_to([P, D]))):
                        sp.dma_start(rows[:, n], src).then_inc(rows_l, 16)

                def load(i, j):
                    dyn = not isinstance(i, int)
                    at, at2, row = (sp.snap(i + 1), sp.snap(i + 1), sp.snap(i * P)) if dyn else (i + 1, i + 1, i * P)
                    if layer == 0:
                        sp.wait_ge(heads_free, at)
                        sp.dma_start(yo[:, 0], a["rw_y"][:, ds(row, P), :].rearrange("d p c -> p d c")).then_inc(heads_l, 16)
                        sp.dma_start(yo[:, 1], a["gd_o"][:, ds(row, P), :].rearrange("d p c -> p d c")).then_inc(heads_l, 16)
                        sp.dma_start(bon[:], a["rw_bonus"][:, ds(row, P), :].rearrange("d p c -> p d c"),
                                     allow_slow_non_contiguous=True).then_inc(heads_l, 16)
                        sp.dma_start(v[:], a["zt"][ds(row, P), 2 * RW_W:3 * RW_W]).then_inc(heads_l, 16)
                        sp.dma_start(og[:], a["zt"][ds(row, P), GATE0 * P:LOW0 * P]).then_inc(heads_l, 16)
                        sp.dma_start(glow[:], a["zf"][2 * P:3 * P, ds(row, P)]).then_inc(heads_l, 16)
                    sp.wait_ge(x_free, at2)
                    sp.dma_start(x[:, j], x_in[ds(row, P), :]).then_inc(x_l[j], 16)
                    if layer == 1:
                        sp.dma_start(cat[:, j], a["at_o"][ds(row, P), :]).then_inc(x_l[j], 16)

                load_rows(0)
                with sp.Fori(0, TP // 2) as p:
                    for j in range(2):
                        load(2 * p + j, j)
                for i in range(TP, TILES):
                    load(i, i % 2)
                load_rows(1)

            @block.tensor
            def _(pe):
                pe.wait_ge(cst, 16 * NCST)
                ident = cf[:, CONST["ident"]]

                def gate_product(i):
                    if layer == 0:
                        pe.wait_ge(heads_l, i * 96 + 96)
                        pe.matmul(bank[7][:], glow[:], gup[:], start=True, stop=True).then_inc(gate_mm, 1)

                def project(i, j, p):
                    pe.wait_ge(cat_r, i + 1) if layer == 0 else pe.wait_ge(x_l[j], XW * p + XW)
                    pe.wait_ge(cat_ev, 2 * i + 2)
                    for k in range(KC):
                        mm = pe.transpose(bank[k // 4][:, (k % 4) * P:(k % 4 + 1) * P], cat[:, j, k * P:(k + 1) * P], ident)
                        if k % 4 == 3:
                            mm.then_inc(cat_tr, 1)
                    pe.wait_ge(cat_ev, 2 * i + 4)
                    for c in range(2):
                        for k in range(KC):
                            mm = pe.matmul(bank[2 + c][:], catT[:, k, :], w_out[:, k, c * 512:(c + 1) * 512],
                                           start=k == 0, stop=k == KC - 1)
                        mm.then_inc(out_mm, 1)

                def router(i):
                    pe.wait_ge(h_r, i + 1)
                    for k in range(KC):
                        mm = pe.transpose(bank[4 + k // 4][:, (k % 4) * P:(k % 4 + 1) * P], h[:, k * P:(k + 1) * P], ident)
                        if k % 4 == 3:
                            mm.then_inc(h_tr, 1)
                    pe.wait_ge(h_ev, i * 2 + 2)
                    for k in range(KC):
                        mm = pe.matmul(bank[6][:, 0:E], hT[:, k, :], rw[:, k, :], start=k == 0, stop=k == KC - 1)
                    mm.then_inc(lg, 1)

                gate_product(0)
                project(0, 0, 0)
                gate_product(1)
                with pe.Fori(0, TP // 2) as p:
                    for j in range(2):
                        router(2 * p + j)
                        gate_product(2 * p + (j + 2))
                        project(2 * p + (j + 1), 1 - j, p + j)
                router(TP)
                project(TP + 1, 1, TP // 2)
                router(TP + 1)
                pe.wait_ge(pos_in, 1)
                pe.matmul(bank[0][:, 0:TILES * E], cf[:, CONST["before"]],
                          one[:, 0, 0:TILES].rearrange("p t e -> p (t e)"), start=True, stop=False, skip_group_check=True)
                pe.matmul(bank[0][:, 0:TILES * E], cf[:, CONST["before"]],
                          one[:, 1, 0:TILES].rearrange("p t e -> p (t e)"), start=False, stop=False, skip_group_check=True)
                pe.matmul(bank[0][:, 0:(TILES + 1) * E], cf[:, CONST["ones"]], upto[:].rearrange("p t e -> p (t e)"),
                          start=False, stop=True, skip_group_check=True).then_inc(pos_mm, 1)

            @block.scalar
            def _(act):
                act.sem_inc(x_st, 16)
                act.sem_inc(h_st, 16)
                act.sem_inc(cat_ev, 2)

                def head_roots(i):
                    if layer == 0:
                        act.wait_ge(hv, i + 1)
                        act.activation(hs[:, 0:2], hs[:, 0:2], ACT.Sqrt).then_inc(hroot, 1)

                def copy_cat(i):
                    for c in range(2):
                        act.wait_ge(cat_tr, 2 * i + (c + 1))
                        act.activation(catT[:, 4 * c:4 * c + 4].rearrange("p k t -> p (k t)"), bank[c][:], ACT.Copy).then_inc(cat_ev, 1)

                def close(i):
                    row = i * P if isinstance(i, int) else act.snap(i * P)
                    act.wait_ge(var_r, i + 1)
                    act.activation(mv[:, 2:3], mv[:, 2:3], ACT.Sqrt).then_inc(root, 1)
                    act.wait_ge(x1_r, i + 1)
                    act.dma_start(x_out[ds(row, P), :], x1[:]).then_inc(x_st, 16)
                    act.wait_ge(h_r, i + 1)
                    act.dma_start(h_out[ds(row, P), :], h[:]).then_inc(h_st, 16)
                    for c in range(2):
                        act.wait_ge(h_tr, 2 * i + (c + 1))
                        act.activation(hT[:, 4 * c:4 * c + 4].rearrange("p k t -> p (k t)"), bank[4 + c][:], ACT.Copy).then_inc(h_ev, 1)
                    act.wait_ge(lg, i + 1)
                    act.activation(sc[:, 0], bank[6][:, 0:E], ACT.Exp, scale=-1.0).then_inc(sg, 1)

                head_roots(0)
                copy_cat(0)
                head_roots(1)
                with act.Fori(0, TP // 2) as p:
                    for j in range(2):
                        close(2 * p + j)
                        copy_cat(2 * p + (j + 1))
                        head_roots(2 * p + (j + 2))
                close(TP)
                copy_cat(TP + 1)
                close(TP + 1)
                act.wait_ge(x_st, 16 * (TILES + 1))
                act.wait_ge(h_st, 16 * (TILES + 1))

            @block.vector
            def _(dve):
                dve.memset(zero[:], 0).then_inc(tab_z, 1)
                dve.wait_ge(cst, 16 * NCST)
                dve.sem_inc(rows_free, 1)
                dve.sem_inc(heads_free, 1)
                dve.sem_inc(x_free, 2)
                rank = cf[:, CONST["rank"]]

                def join(i, j):
                    if layer == 1:
                        return
                    link = Chain(dve, vec_a, 21)
                    link.turn(i)
                    dve.wait_ge(heads_l, i * 96 + 96)
                    ys, os_ = yo[:, 0, 0], yo[:, 1, 0]
                    link(dve.tensor_tensor(ys, ys, yo[:, 0, 1], ALU.add))
                    link(dve.tensor_tensor(os_, os_, yo[:, 1, 1], ALU.add))
                    link(dve.tensor_reduce(hs[:, 2], heads(ys, 64), AX.X, ALU.add))
                    link(dve.tensor_scalar(hs[:, 2], hs[:, 2], 1.0 / RW_N, None, ALU.mult))
                    link(dve.tensor_tensor(heads(ys, 64), heads(ys, 64), per_head(hs[:, 2], 64), ALU.subtract))
                    link(dve.tensor_tensor(sq_t[:], ys, ys, ALU.mult))
                    link(dve.tensor_reduce(hs[:, 0], heads(sq_t[:], 64), AX.X, ALU.add))
                    link(dve.tensor_scalar(hs[:, 0], hs[:, 0], 1.0 / RW_N, RW_GN_EPS, ALU.mult, ALU.add))
                    link(dve.tensor_tensor(sq_t[:], os_, os_, ALU.mult))
                    link(dve.tensor_reduce(hs[:, 1, 0:4], heads(sq_t[:], P), AX.X, ALU.add))
                    link(dve.tensor_copy(hs[:, 1, 4:8], hs[:, 1, 0:4]))
                    dve.tensor_scalar(hs[:, 1], hs[:, 1], 1.0 / GD_N, GD_NORM_EPS, ALU.mult, ALU.add).then_inc(hv, 1)
                    link(dve.tensor_tensor(bon[:, 0], bon[:, 0], bon[:, 1], ALU.add))
                    link(dve.tensor_tensor(heads(v[:], 64), heads(v[:], 64), per_head(bon[:, 0], 64), ALU.mult))
                    dve.wait_ge(hroot, i + 1)
                    link(dve.reciprocal(hs[:, 0:2], hs[:, 0:2]))
                    link(dve.tensor_tensor(heads(ys, 64), heads(ys, 64), per_head(hs[:, 0], 64), ALU.mult))
                    link(dve.tensor_tensor(ys, ys, gn[:, 0], ALU.mult))
                    link(dve.tensor_tensor(ys, ys, gn[:, 1], ALU.add))
                    link(dve.tensor_tensor(ys, ys, v[:], ALU.add))
                    dve.wait_ge(gate_mm, i + 1)
                    link(dve.tensor_tensor(cat[:, j, 0:RW_W], ys, bank[7][:], ALU.mult))
                    link(dve.tensor_tensor(heads(os_, P), heads(os_, P), per_head(hs[:, 1, 0:4], P), ALU.mult))
                    link(dve.tensor_tensor(heads(os_, P), heads(os_, P), ng[:].unsqueeze(1).broadcast_to([P, 4, P]), ALU.mult))
                    dve.tensor_tensor(cat[:, j, RW_W:], os_, og[:], ALU.mult).then_inc(cat_r, 1)
                    dve.wait_ge(cat_r, i + 1)
                    dve.sem_inc(heads_free, 1)
                    link.end()

                def residual(i, j, p):
                    link = Chain(dve, vec_c, 11)
                    link.turn(i)
                    dve.wait_ge(x_l[j], XW * p + XW)
                    dve.wait_ge(x_st, i * 16 + 16)
                    for c in range(2):
                        cols = slice(c * 512, (c + 1) * 512)
                        dve.wait_ge(out_mm, 2 * i + (c + 1))
                        link(dve.tensor_tensor(x2[:, cols], bank[2 + c][:], rows[:, 0, cols], ALU.mult))
                    link(dve.scalar_tensor_tensor(x2[:], x[:, j], ALPHA, x2[:], ALU.mult, ALU.add))
                    dve.sem_inc(x_free, 1)
                    normed(dve, link, step, x2, x1, stats, mv, var_r, root, i + 1, rows[:, 3], rows[:, 4])
                    dve.sem_inc(x1_r, 1)
                    link(dve.tensor_tensor(x2[:], x1[:], rows[:, 1], ALU.mult))
                    dve.wait_ge(h_st, i * 16 + 16)
                    dve.tensor_tensor(h[:], x2[:], rows[:, 2], ALU.add).then_inc(h_r, 1)
                    link.end()

                def route(i):
                    link = Chain(dve, vec_r, 29)
                    link.turn(i)
                    dve.wait_ge(sg, i + 1)
                    link(dve.tensor_scalar(sc[:, 0], sc[:, 0], 1.0, None, ALU.add))
                    link(dve.reciprocal(sc[:, 0], sc[:, 0]))
                    link(dve.tensor_tensor(sc[:, 1], sc[:, 0], rb[:], ALU.add))
                    g4 = sc[:, 1].rearrange("p (g e) -> p g e", e=PER)
                    pairs = [(e1, e2) for e1 in range(PER) for e2 in range(e1 + 1, PER)]
                    for n, (e1, e2) in enumerate(pairs):
                        ins = dve.tensor_tensor(r8[:, n], g4[:, :, e1], g4[:, :, e2], ALU.add)
                    link(ins)
                    link(dve.tensor_reduce(r8[:, 6], r8[:, 0:6].rearrange("p a g -> p g a"), AX.X, ALU.max))
                    link(dve.tensor_reduce(r1[:, 0:1], r8[:, 6], AX.X, ALU.max))
                    link(dve.tensor_scalar(r8[:, 6], r8[:, 6], r1[:, 0:1], None, ALU.is_equal))
                    link(dve.scalar_tensor_tensor(r8[:, 6], rank[:, 0:8], -64.0, r8[:, 6], ALU.add, ALU.mult))
                    link(dve.tensor_reduce(r1[:, 1:2], r8[:, 6], AX.X, ALU.min))
                    link(dve.tensor_scalar(r8[:, 7], r8[:, 6], r1[:, 1:2], None, ALU.is_equal))
                    pick = per_head(r8[:, 7], PER)
                    for n in range(2):
                        ins = dve.tensor_tensor(r32[:, n].rearrange("p (g e) -> p g e", e=PER),
                                                sc[:, n].rearrange("p (g e) -> p g e", e=PER), pick, ALU.mult)
                    link(ins)
                    for n in range(2):
                        ins = dve.tensor_reduce(r4[:, n], r32[:, n].rearrange("p (g e) -> p e g", e=PER), AX.X, ALU.add)
                    link(ins)
                    for c in range(2):
                        link(dve.tensor_reduce(r1[:, 2:3], r4[:, 1], AX.X, ALU.max))
                        link(dve.tensor_scalar(r4[:, 4], r4[:, 1], r1[:, 2:3], None, ALU.is_equal))
                        link(dve.scalar_tensor_tensor(r4[:, 4], rank[:, 0:PER], -64.0, r4[:, 4], ALU.add, ALU.mult))
                        link(dve.tensor_reduce(r1[:, 3:4], r4[:, 4], AX.X, ALU.min))
                        link(dve.tensor_scalar(r4[:, 2 + c], r4[:, 4], r1[:, 3:4], None, ALU.is_equal))
                        if c == 0:
                            link(dve.scalar_tensor_tensor(r4[:, 1], r4[:, 2], NEG, r4[:, 1], ALU.mult, ALU.add))
                        link(dve.tensor_tensor(r4[:, 5 + c], r4[:, 2 + c], r4[:, 0], ALU.mult))
                        link(dve.tensor_reduce(gate[:, c, ds(i, 1)], r4[:, 5 + c], AX.X, ALU.add))
                        link(dve.tensor_tensor(one[:, c, ds(i, 1)].rearrange("p t (g e) -> p (t g) e", e=PER), pick,
                                               r4[:, 2 + c].unsqueeze(1).broadcast_to([P, GROUPS, PER]), ALU.mult))
                    link.end()

                def rows_of(q):
                    dve.wait_ge(rows_l, 80 * (q + 1))
                    dve.tensor_scalar(rows[:, 0:2], rows[:, 0:2], 1.0, None, ALU.add).then_inc(own, 1)
                    dve.wait_ge(own, q + 1)

                join(0, 0)
                rows_of(0)
                join(1, 1)
                with dve.Fori(0, TP // 2) as p:
                    for j in range(2):
                        residual(2 * p + j, j, p)
                        join(2 * p + (j + 2), j)
                        route(dve.snap(2 * p + j))
                dve.sem_inc(rows_free, 1)
                rows_of(1)
                residual(TP, 0, TP // 2)
                route(TP)
                residual(TP + 1, 1, TP // 2)
                route(TP + 1)
                more = Chain(dve, vec)
                more(dve.tensor_tensor(gsum[:], gate[:, 0], gate[:, 1], ALU.add))
                more(dve.reciprocal(gsum[:], gsum[:]))
                for c in range(2):
                    more(dve.tensor_tensor(gate[:, c], gate[:, c], gsum[:], ALU.mult))
                more(dve.memset(upto[:, 0], 0.0))
                for t in range(TILES):
                    more(dve.tensor_tensor(place[:, 0], one[:, 0, t], one[:, 1, t], ALU.add))
                    more(dve.tensor_tensor(upto[:, t + 1], upto[:, t], place[:, 0], ALU.add))
                dve.sem_inc(pos_in, 1)
                dve.wait_ge(pos_mm, 1)
                more(dve.tensor_copy(place[:].rearrange("p t e -> p (t e)"), bank[0][:, 0:(TILES + 1) * E]))
                more(dve.tensor_scalar(nb[:, 0], place[:, TILES], 1.0 / P, None, ALU.mult))
                more(dve.tensor_tensor(cmp[:, 0:MAX_OVER].rearrange("p m e -> p e m"), per_head(nb[:, 0], MAX_OVER),
                                       rank[:, 1:1 + MAX_OVER].unsqueeze(1).broadcast_to([P, E, MAX_OVER]), ALU.is_gt))
                more(dve.tensor_reduce(nb[:, 1], cmp[:, 0:MAX_OVER].rearrange("p m e -> p e m"), AX.X, ALU.add))
                more(dve.tensor_tensor_scan(nb[:, 2], cf[:, CONST["ones"]][:, 0:E], nb[:, 1], 0.0, ALU.mult, ALU.add))
                more(dve.tensor_tensor(nb[:, 3], nb[:, 2], nb[:, 1], ALU.subtract))
                more(dve.tensor_tensor(nb[:, 3], nb[:, 3], rank[:, 0:E], ALU.subtract))
                more(dve.tensor_scalar(nb[:, 3], nb[:, 3], float(E - 1), float(P), ALU.add, ALU.mult))
                more(dve.tensor_scalar(upto[:, 0:TILES], place[:, 0:TILES], float(P), None, ALU.is_ge))
                more(dve.tensor_tensor(upto[:, 0:TILES], upto[:, 0:TILES], nb[:, 3].unsqueeze(1).broadcast_to([P, TILES, E]), ALU.mult))
                more(dve.tensor_tensor(place[:, 0:TILES], place[:, 0:TILES], upto[:, 0:TILES], ALU.add))
                more(dve.tensor_scalar(nb[:, 0], rank[:, 0:E], float(P), None, ALU.mult))
                more(dve.tensor_tensor(place[:, 0:TILES], place[:, 0:TILES], nb[:, 0].unsqueeze(1).broadcast_to([P, TILES, E]), ALU.add))
                for c in range(2):
                    more(dve.tensor_tensor(one[:, c, 0:TILES], one[:, c, 0:TILES], place[:, 0:TILES], ALU.mult))
                    more(dve.tensor_reduce(dest[:, c], one[:, c, 0:TILES], AX.X, ALU.add))
                more(dve.tensor_copy(dest_i[:], dest[:]))
                more(dve.tensor_tensor(cmp[:, 0:OVER], nb[:, 2].unsqueeze(1).broadcast_to([P, OVER, E]), per_head(rank[:, 0:OVER], E), ALU.is_le))
                more(dve.tensor_reduce(blk[:, 0, 0:OVER], cmp[:, 0:OVER], AX.X, ALU.add))
                more(dve.tensor_scalar(blk[:, 1, 0:OVER], blk[:, 0, 0:OVER], float(E - 1), None, ALU.min))
                more(dve.tensor_copy(blk[:, 1, OVER:OVER + 1], nb[:, 2, E - 1:E]))
                more(dve.tensor_copy(blk_i[:, 0:OVER + 1], blk[:, 1, 0:OVER + 1]))
                dve.sem_inc(dest_r, 1)

            @block.gpsimd
            def _(pool):
                pool.wait_ge(dest_r, 1)
                pool.wait_ge(tab, 16)
                for c in range(2):
                    for t in range(TILES):
                        pool.indirect_dma_start(out=a["row_tok"], out_offset=bass.IndirectOffsetOnAxis(ap=dest_i[:, c, t:t + 1], axis=0),
                                                in_=tok[:, t:t + 1], in_offset=None).then_inc(scat, 16)
                pool.dma_start(a["dest"], dest_i[:].rearrange("p c t -> p (c t)")).then_inc(scat, 16)
                pool.dma_start(a["gates"], gate[:].rearrange("p c t -> p (c t)")).then_inc(scat, 16)
                pool.dma_start(a["blk"], blk_i[0:1, 0:OVER + 1]).then_inc(scat, 16)
                pool.wait_ge(scat, 16 * (2 * TILES + 3))


def experts(nc, a, layer):
    wg, wu, wd = (a[n][layer] for n in ("moe_w_gate", "moe_w_up", "moe_w_down"))
    with Phase(nc, f"moe{layer}") as ph:
        ident = ph.sb("ident", [P, P])
        rt = ph.sb("rt", [BLOCKS, P], I32)
        rtf = ph.sb("rtf", [BLOCKS, P])
        idx = ph.sb("idx", [P, BLOCKS], I32)
        idxc = ph.sb("idxc", [P, 2, 1], I32)
        blk = ph.sb("blk", [1, OVER + 1], I32)
        wgu = ph.sb("wgu", [P, 2, KC, 2, FF])
        wdn = ph.sb("wdn", [P, 2, 2, D])
        x = ph.sb("x", [P, 2, D])
        xT = ph.sb("xT", [P, 2, KC, P])
        sg = ph.sb("sg", [P, 2, FF])
        hid = ph.sb("hid", [P, 2, FF])
        hidT = ph.sb("hidT", [P, 2, 2, P])
        y = ph.sb("y", [P, 2, D])
        bank = ph.banks(8)
        cst, t_mm, idx_r, idx_c, x_tr, xt_ev, gu_mm, sg_r, hid_r, h_tr, ht_ev, y_mm, own = (ph.sem(n) for n in (
            "cst", "idx_turned", "idx_ready", "idx_copied", "x_turned", "xT_ev", "gate_up_mm", "silu_ready", "hid_ready",
            "hid_turned", "hidT_ev", "y_mm", "own"))
        y_ev = [ph.sem(f"y_ev{c}") for c in range(2)]
        w_l = [ph.sem(f"gate_up_loaded{j}") for j in range(2)]
        wd_l = [ph.sem(f"down_loaded{j}") for j in range(2)]
        x_l = [ph.sem(f"x_loaded{j}") for j in range(2)]
        y_st = [ph.sem(f"y_stored{j}") for j in range(2)]
        SECTIONS = ((0, E), (E, OVER))

        def both_sections(eng, body):
            body(0, E)
            more = eng.value_load(blk[0:1, OVER:OVER + 1], min_val=0, max_val=OVER)
            with eng.If(more > 0):
                body(E, OVER)
            with eng.Else():
                pass

        with nc.Block() as block:

            @block.sync
            def _(sp):
                sp.dma_start(ident[:], a["const_f"][:, CONST["ident"]]).then_inc(cst, 16)
                sp.dma_start(rt[:], a["row_tok"].rearrange("(b p) o -> b (p o)", p=P)).then_inc(cst, 16)
                sp.dma_start(blk[:], a["blk"]).then_inc(cst, 16)

                def body(first, count):
                    with sp.Fori(first // 2, (first + count) // 2) as p:
                        for j in range(2):
                            e = sp.snap(2 * p + j) if first == 0 else sp.value_load(blk[0:1, ds(2 * p + (j - E), 1)], min_val=0, max_val=E - 1)
                            at = sp.snap(2 * p + (j + 1))
                            sp.wait_ge(gu_mm, at)
                            sp.dma_start(wgu[:, j, :, 0, :], wg[ds(e, 1)].rearrange("a (k p) n -> p (a k) n", p=P)).then_inc(w_l[j], 16)
                            sp.dma_start(wgu[:, j, :, 1, :], wu[ds(e, 1)].rearrange("a (k p) n -> p (a k) n", p=P)).then_inc(w_l[j], 16)

                sp.wait_ge(cst, 48)
                both_sections(sp, body)

            @block.gpsimd
            def _(pool):
                pool.wait_ge(cst, 48)
                pool.wait_ge(idx_r, 2)

                def body(first, count):
                    with pool.Fori(first // 2, (first + count) // 2) as p:
                        for j in range(2):
                            pool.wait_ge(x_tr, 2 * p + (j + 1))
                            pool.tensor_copy(idxc[:, j], idx[:, ds(pool.snap(2 * p + j), 1)]).then_inc(idx_c, 1)
                            pool.wait_ge(idx_c, 2 * p + (j + 1))
                            pool.sem_inc(own, 1)
                            pool.indirect_dma_start(out=x[:, j], out_offset=None, in_=a["h_rows"],
                                                    in_offset=bass.IndirectOffsetOnAxis(ap=idxc[:, j], axis=0)).then_inc(x_l[j], 16)

                both_sections(pool, body)

            @block.tensor
            def _(pe):
                pe.wait_ge(cst, 48)
                pe.wait_ge(idx_r, 1)
                pe.transpose(bank[0][:, 0:BLOCKS], rtf[:], ident[0:BLOCKS, 0:BLOCKS]).then_inc(t_mm, 1)
                pe.wait_ge(idx_r, 2)
                pe.sem_inc(x_tr, 2)
                pe.sem_inc(y_mm, 4)
                pe.sem_inc(gu_mm, 2)

                def turn_x(b, j, p):
                    pe.wait_ge(x_l[j], 16 * p + 16)
                    pe.wait_ge(xt_ev, 2 * b + 2)
                    for k in range(KC):
                        mm = pe.transpose(bank[k // 4][:, (k % 4) * P:(k % 4 + 1) * P], x[:, j, k * P:(k + 1) * P], ident[:])
                    mm.then_inc(x_tr, 1)

                def gate_up(b, j, p):
                    pe.wait_ge(w_l[j], 32 * p + 32)
                    pe.wait_ge(xt_ev, 2 * b + 4)
                    for k in range(KC):
                        mm = pe.matmul(bank[2 + j][:], xT[:, j, k, :], wgu[:, j, k].rearrange("p a n -> p (a n)"),
                                       start=k == 0, stop=k == KC - 1)
                    mm.then_inc(gu_mm, 1)

                def turn_hid(b, j, p):
                    pe.wait_ge(hid_r, b + 1)
                    pe.wait_ge(ht_ev, b + 1)
                    for k in range(2):
                        mm = pe.transpose(bank[4][:, k * P:(k + 1) * P], hid[:, j, k * P:(k + 1) * P], ident[:])
                    mm.then_inc(h_tr, 1)

                def down(b, j, p):
                    pe.wait_ge(ht_ev, b + 2)
                    pe.wait_ge(wd_l[j], 16 * p + 16)
                    for c in range(2):
                        pe.wait_ge(y_ev[c], b + 1)
                        for k in range(2):
                            mm = pe.matmul(bank[5 + c][:], hidT[:, j, k, :], wdn[:, j, k, c * 512:(c + 1) * 512],
                                           start=k == 0, stop=k == 1)
                        mm.then_inc(y_mm, 1)

                def body(first, count):
                    h = first // 2
                    last = first + count - 1
                    turn_x(first, 0, h)
                    gate_up(first, 0, h)
                    turn_x(first + 1, 1, h)
                    turn_hid(first, 0, h)
                    with pe.Fori(h, h + count // 2 - 1) as p:
                        gate_up(2 * p + 1, 1, p)
                        turn_x(2 * p + 2, 0, p + 1)
                        down(2 * p, 0, p)
                        turn_hid(2 * p + 1, 1, p)
                        gate_up(2 * p + 2, 0, p + 1)
                        turn_x(2 * p + 3, 1, p + 1)
                        down(2 * p + 1, 1, p)
                        turn_hid(2 * p + 2, 0, p + 1)
                    gate_up(last, 1, last // 2)
                    down(last - 1, 0, last // 2)
                    turn_hid(last, 1, last // 2)
                    down(last, 1, last // 2)

                both_sections(pe, body)

            @block.scalar
            def _(act):
                act.wait_ge(cst, 48)
                act.sem_inc(xt_ev, 2)
                act.sem_inc(ht_ev, 1)
                act.sem_inc(y_ev[0], 1)
                act.sem_inc(y_st[0], 16)
                act.sem_inc(y_st[1], 16)
                over = [False]

                def copy_x(b, j):
                    act.wait_ge(x_tr, b + 3)
                    for c in range(2):
                        act.activation(xT[:, j, 4 * c:4 * c + 4].rearrange("p k t -> p (k t)"), bank[c][:], ACT.Copy).then_inc(xt_ev, 1)

                def silu(b, j):
                    act.wait_ge(gu_mm, b + 3)
                    act.activation(sg[:, j], bank[2 + j][:, 0:FF], ACT.Silu).then_inc(sg_r, 1)

                def copy_hid(b, j):
                    act.wait_ge(h_tr, b + 1)
                    act.activation(hidT[:, j].rearrange("p k t -> p (k t)"), bank[4][:, 0:FF], ACT.Copy).then_inc(ht_ev, 1)

                def load_down(b, j):
                    e = b if isinstance(b, int) and b < E else None
                    if e is None:
                        e = act.snap(b * 1) if not over[0] else act.value_load(blk[0:1, ds(b - E, 1)], min_val=0, max_val=E - 1)
                    act.dma_start(wdn[:, j], wd[ds(e, 1)].rearrange("a (k p) n -> p (a k) n", p=P)).then_inc(wd_l[j], 16)

                def store(b, j, p, ahead=True):
                    act.wait_ge(y_mm, 2 * b + 6)
                    if ahead:
                        load_down(b + 2, j)
                    act.wait_ge(y_st[j], 16 * p + 16)
                    act.activation(y[:, j, 0:512], bank[5][:], ACT.Copy).then_inc(y_ev[0], 1)
                    row = b * P if isinstance(b, int) else act.snap(b * P)
                    act.wait_ge(y_ev[0], b + 2)
                    act.wait_ge(y_ev[1], b + 2)
                    act.dma_start(a["y_rows"][ds(row, P), :], y[:, j]).then_inc(y_st[j], 16)

                def body(first, count):
                    h = first // 2
                    last = first + count - 1
                    over[0] = first > 0
                    load_down(first, 0)
                    load_down(first + 1, 1)
                    copy_x(first, 0)
                    silu(first, 0)
                    copy_x(first + 1, 1)
                    copy_hid(first, 0)
                    with act.Fori(h, h + count // 2 - 1) as p:
                        silu(2 * p + 1, 1)
                        copy_x(2 * p + 2, 0)
                        store(2 * p, 0, p)
                        copy_hid(2 * p + 1, 1)
                        silu(2 * p + 2, 0)
                        copy_x(2 * p + 3, 1)
                        store(2 * p + 1, 1, p)
                        copy_hid(2 * p + 2, 0)
                    silu(last, 1)
                    store(last - 1, 0, last // 2, False)
                    copy_hid(last, 1)
                    store(last, 1, last // 2, False)
                    for j in range(2):
                        act.wait_ge(y_st[j], 16 * ((first + count) // 2 + 1))

                both_sections(act, body)

            @block.vector
            def _(dve):
                dve.wait_ge(cst, 48)
                dve.tensor_copy(rtf[:], rt[:]).then_inc(idx_r, 1)
                dve.wait_ge(t_mm, 1)
                dve.tensor_copy(idx[:], bank[0][:, 0:BLOCKS]).then_inc(idx_r, 1)
                dve.sem_inc(y_ev[1], 1)

                def hidden(b, j):
                    dve.wait_ge(sg_r, b + 1)
                    dve.tensor_tensor(hid[:, j], sg[:, j], bank[2 + j][:, FF:2 * FF], ALU.mult).then_inc(hid_r, 1)

                def second_half(b, j, p):
                    dve.wait_ge(y_mm, 2 * b + 6)
                    dve.wait_ge(y_st[j], 16 * p + 16)
                    dve.tensor_copy(y[:, j, 512:D], bank[6][:]).then_inc(y_ev[1], 1)

                def body(first, count):
                    h = first // 2
                    last = first + count - 1
                    hidden(first, 0)
                    with dve.Fori(h, h + count // 2 - 1) as p:
                        hidden(2 * p + 1, 1)
                        second_half(2 * p, 0, p)
                        hidden(2 * p + 2, 0)
                        second_half(2 * p + 1, 1, p)
                    hidden(last, 1)
                    second_half(last - 1, 0, last // 2)
                    second_half(last, 1, last // 2)

                both_sections(dve, body)


def combine(nc, a, layer):
    m = 2 * layer + 1
    with Phase(nc, f"comb{layer}") as ph:
        rows = ph.sb("rows", [P, 3, D])
        dest = ph.sb("dest", [P, 2, TILES], I32)
        gates = ph.sb("gates", [P, 2, TILES])
        idxc = ph.sb("idxc", [P, 2, 2, 1], I32)
        y = ph.sb("y", [P, 2, 2, D])
        x = ph.sb("x", [P, 2, D])
        t = ph.sb("t", [P, D])
        out = ph.sb("out", [P, 2, D])
        stats = ph.sb("stats", [P, 2, 6])
        mv = ph.sb("mv", [P, 3])
        cst, rows_l, rows_free, in_free, vec, own, step, idx_c, idx_s, var_r, root, out_r = (ph.sem(n) for n in (
            "cst", "rows_loaded", "rows_free", "inputs_free", "vec", "own", "step", "idx_copied", "idx_waited", "var_ready", "root", "out_ready"))
        x_l = [ph.sem(f"x_loaded{j}") for j in range(2)]
        y_l = [ph.sem(f"y_loaded{j}") for j in range(2)]
        st = [ph.sem(f"stored{j}") for j in range(2)]

        with nc.Block() as block:

            @block.sync
            def _(sp):
                sp.dma_start(dest[:].rearrange("p c t -> p (c t)"), a["dest"]).then_inc(cst, 16)
                sp.dma_start(gates[:].rearrange("p c t -> p (c t)"), a["gates"]).then_inc(cst, 16)
                for q, (lo, hi) in enumerate(SEQ_TILES):
                    sp.wait_ge(rows_free, q + 1)
                    for n, src in enumerate((mod_row(a, m, q, 2), a["ln_g"][layer, 1:2].broadcast_to([P, D]),
                                             a["ln_b"][layer, 1:2].broadcast_to([P, D]))):
                        sp.dma_start(rows[:, n], src).then_inc(rows_l, 16)
                    with sp.Fori(lo // 2, hi // 2) as p:
                        for j in range(2):
                            at = sp.snap(2 * p + (j + 1))
                            row = sp.snap((2 * p + j) * P)
                            sp.wait_ge(in_free, at)
                            sp.dma_start(x[:, j], a["x_mid"][ds(row, P), :]).then_inc(x_l[j], 16)

            @block.gpsimd
            def _(pool):
                pool.wait_ge(cst, 32)
                with pool.Fori(0, TILES // 2) as p:
                    for j in range(2):
                        pool.wait_ge(in_free, 2 * p + (j + 1))
                        for c in range(2):
                            pool.tensor_copy(idxc[:, j, c], dest[:, c, ds(pool.snap(2 * p + j), 1)]).then_inc(idx_c, 1)
                        pool.wait_ge(idx_c, 4 * p + (2 * j + 2))
                        pool.sem_inc(idx_s, 1)
                        for c in range(2):
                            pool.indirect_dma_start(out=y[:, j, c], out_offset=None, in_=a["y_rows"],
                                                    in_offset=bass.IndirectOffsetOnAxis(ap=idxc[:, j, c], axis=0)).then_inc(y_l[j], 16)

            @block.scalar
            def _(act):
                act.sem_inc(st[0], 16)
                act.sem_inc(st[1], 16)
                for q, (lo, hi) in enumerate(SEQ_TILES):
                    with act.Fori(lo // 2, hi // 2) as p:
                        for j in range(2):
                            act.wait_ge(var_r, 2 * p + (j + 1))
                            act.activation(mv[:, 2:3], mv[:, 2:3], ACT.Sqrt).then_inc(root, 1)
                            row = act.snap(2 * p * P + (j - lo) * P if layer else 2 * p * P + j * P)
                            act.wait_ge(out_r, 2 * p + (j + 1))
                            if layer == 0:
                                dst = a["x_mid2"][ds(row, P), :]
                            else:
                                dst = a["y_prompt" if q == 0 else "y_sample"][0, ds(row, P), :]
                            act.dma_start(dst, out[:, j]).then_inc(st[j], 16)
                for j in range(2):
                    act.wait_ge(st[j], 16 * (TILES // 2 + 1))

            @block.vector
            def _(dve):
                dve.sem_inc(rows_free, 1)
                dve.sem_inc(in_free, 2)
                dve.wait_ge(cst, 32)
                per = 11
                link = Chain(dve, vec, 2 * per)
                for q, (lo, hi) in enumerate(SEQ_TILES):
                    dve.wait_ge(rows_l, 48 * (q + 1))
                    dve.tensor_scalar(rows[:, 0], rows[:, 0], 1.0, None, ALU.add).then_inc(own, 1)
                    dve.wait_ge(own, q + 1)
                    with dve.Fori(lo // 2, hi // 2) as p:
                        link.turn(p)
                        for j in range(2):
                            g = [gates[:, c, ds(dve.snap(2 * p + j), 1)] for c in range(2)]
                            dve.wait_ge(y_l[j], 32 * p + 32)
                            link(dve.tensor_scalar(y[:, j, 0], y[:, j, 0], g[0], None, ALU.mult))
                            link(dve.scalar_tensor_tensor(y[:, j, 0], y[:, j, 1], g[1], y[:, j, 0], ALU.mult, ALU.add))
                            link(dve.tensor_tensor(y[:, j, 0], y[:, j, 0], rows[:, 0], ALU.mult))
                            dve.wait_ge(x_l[j], 16 * p + 16)
                            dve.wait_ge(st[j], 16 * p + 16)
                            link(dve.scalar_tensor_tensor(t[:], x[:, j], ALPHA, y[:, j, 0], ALU.mult, ALU.add))
                            dve.sem_inc(in_free, 1)
                            normed(dve, link, step, t, out[:, j], stats, mv, var_r, root, 2 * p + (j + 1), rows[:, 1], rows[:, 2])
                            dve.sem_inc(out_r, 1)
                    if q == 0:
                        dve.sem_inc(rows_free, 1)
                link.end()



PAIRS = AT_H // 2
KV0 = AT_H * AT_N
V0 = KV0 + AT_KV * AT_N
VW = AT_KV * AT_N
SLOTS = TILES + 3
EMPTY = (0, TP + 1, SLOTS - 1)


def attention_projection(nc, a):
    with Phase(nc, "qkv") as ph:
        ident = ph.sb("ident", [P, P])
        w = ph.sb("w", [P, KC, AT_COLS])
        scol = ph.sb("scol", [P, 2, 2, KC])
        x = ph.sb("x", [P, 2, D])
        rope = ph.sb("rope", [P, 2, ROPE])
        hT = ph.sb("hT", [P, 2, KC, P])
        z = ph.sb("z", [P, 2, AT_COLS])
        r = ph.sb("r", [P, 4, AT_H + AT_KV, HALF_ROPE])
        kd = ph.sb("kd", [P, 2, AT_KV, 2, AT_N])
        qT = ph.sb("qT", [P, 2, PAIRS, P])
        kT = ph.sb("kT", [P, 2, AT_KV, P])
        zero = ph.sb("zero", [P, AT_KV, P])
        bank = ph.banks(8)
        cst, zeroed, z_st, x_tr, h_ev, z_mm, z_ev, rot, vec, kd_r, tr, tr_ev = (ph.sem(n) for n in (
            "cst", "zeroed", "zero_stored", "x_turned", "hT_ev", "z_mm", "z_ev", "rotated", "vec", "k_doubled", "turned",
            "turned_ev"))
        x_l = [ph.sem(f"x_loaded{j}") for j in range(2)]
        st = [ph.sem(f"stored{j}") for j in range(2)]

        with nc.Block() as block:

            @block.sync
            def _(sp):
                sp.dma_start(ident[:], a["const_f"][:, CONST["ident"]]).then_inc(cst, 16)
                for q in range(2):
                    for part in range(2):
                        sp.dma_start(scol[:, q, part], a["mod"][2, q, part * D:(part + 1) * D].rearrange("(k p) -> p k", p=P),
                                     allow_slow_non_contiguous=True).then_inc(cst, 16)
                sp.dma_start(w[:], a["at_w_in"][0].rearrange("(k p) n -> p k n", p=P)).then_inc(cst, 16)
                sp.wait_ge(zeroed, 1)
                for slot in EMPTY:
                    sp.dma_start(a["kT_rows"][:, :, slot * P:(slot + 1) * P], zero[:]).then_inc(z_st, 16)
                    sp.dma_start(a["v_rows"][slot * P:(slot + 1) * P, :],
                                 zero[:].rearrange("p g t -> p (g t)")[:, 0:VW]).then_inc(z_st, 16)
                with sp.Fori(0, TILES // 2) as p:
                    for j in range(2):
                        at = sp.snap(2 * p + (j + 1))
                        row = sp.snap((2 * p + j) * P)
                        sp.wait_ge(rot, at)
                        sp.dma_start(x[:, j], a["x_mid2"][ds(row, P), :]).then_inc(x_l[j], 16)
                        sp.dma_start(rope[:, j], a["const_rope"][ds(row, P), :]).then_inc(x_l[j], 16)
                sp.wait_ge(z_st, 16 * 6)

            @block.tensor
            def _(pe):
                pe.wait_ge(cst, 16 * 6)
                with pe.Fori(0, TILES // 2) as p:
                    for j in range(2):
                        i = 2 * p + j
                        pe.wait_ge(x_l[j], 32 * p + 32)
                        pe.wait_ge(h_ev, i + 1)
                        for k in range(KC):
                            mm = pe.transpose(bank[k // 4][:, (k % 4) * P:(k % 4 + 1) * P], x[:, j, k * P:(k + 1) * P], ident[:])
                        mm.then_inc(x_tr, 1)
                        pe.wait_ge(h_ev, i + 2)
                        for c in range(3):
                            pe.wait_ge(z_ev, 3 * i + (c + 1))
                            for k in range(KC):
                                mm = pe.matmul(bank[2 + c][:], hT[:, j, k, :], w[:, k, c * 512:(c + 1) * 512],
                                               start=k == 0, stop=k == KC - 1)
                            mm.then_inc(z_mm, 1)
                        pe.wait_ge(kd_r, i + 1)
                        pe.wait_ge(tr_ev, 3 * i + 3)
                        for n in range(12):
                            src = z[:, j, n * P:(n + 1) * P] if n < PAIRS else kd[:, j, n - PAIRS].rearrange("p a c -> p (a c)")
                            mm = pe.transpose(bank[5 + n // 4][:, (n % 4) * P:(n % 4 + 1) * P], src, ident[:])
                            if n % 4 == 3:
                                mm.then_inc(tr, 1)

            @block.scalar
            def _(act):
                act.wait_ge(cst, 16 * 6)
                act.sem_inc(z_ev, 3)
                act.sem_inc(tr_ev, 3)
                act.sem_inc(st[0], 48)
                act.sem_inc(st[1], 48)
                for q, (lo, hi) in enumerate(SEQ_TILES):
                    with act.Fori(lo // 2, hi // 2) as p:
                        for j in range(2):
                            i = 2 * p + j
                            act.wait_ge(st[j], 48 * p + 48)
                            for c in range(3):
                                act.wait_ge(z_mm, 3 * i + (c + 1))
                                act.activation(z[:, j, c * 512:(c + 1) * 512], bank[2 + c][:], ACT.Copy).then_inc(z_ev, 1)
                            act.wait_ge(rot, i + 3)
                            act.activation(kd[:, j], z[:, j, KV0:V0].rearrange("p (g n) -> p g n", n=AT_N).unsqueeze(2)
                                           .broadcast_to([P, AT_KV, 2, AT_N]), ACT.Copy).then_inc(kd_r, 1)
                            for c in range(3):
                                act.wait_ge(tr, 3 * i + (c + 1))
                                dst = (qT[:, j, 0:4], qT[:, j, 4:8], kT[:, j])[c]
                                act.activation(dst.rearrange("p k t -> p (k t)"), bank[5 + c][:], ACT.Copy,
                                               scale=AT_N ** -0.5 if c < 2 else 1.0).then_inc(tr_ev, 1)
                            act.wait_ge(tr_ev, 3 * i + 6)
                            tile = act.snap(i * 1)
                            slot = act.snap(i * P + (1 + q) * P)
                            act.dma_start(a["qT_rows"][ds(tile, 1)].rearrange("a p n -> (a p) n"),
                                          qT[:, j].rearrange("p k t -> p (k t)")).then_inc(st[j], 16)
                            act.dma_start(a["kT_rows"][:, :, ds(slot, P)], kT[:, j]).then_inc(st[j], 16)
                            act.dma_start(a["v_rows"][ds(slot, P), :], z[:, j, V0:AT_COLS]).then_inc(st[j], 16)
                for j in range(2):
                    act.wait_ge(st[j], 48 * (TILES // 2 + 1))

            @block.vector
            def _(dve):
                dve.memset(zero[:], 0.0).then_inc(zeroed, 1)
                dve.wait_ge(cst, 16 * 6)
                link = Chain(dve, vec, 5, 1)
                dve.tensor_scalar(scol[:, :, 1], scol[:, :, 1], 1.0, None, ALU.add).then_inc(vec, 1)
                dve.wait_ge(vec, 1)
                dve.sem_inc(h_ev, 1)
                dve.sem_inc(rot, 2)
                for q, (lo, hi) in enumerate(SEQ_TILES):
                    with dve.Fori(lo // 2, hi // 2) as p:
                        for j in range(2):
                            i = 2 * p + j
                            link.turn(i)
                            dve.wait_ge(x_tr, i + 1)
                            for k in range(KC):
                                ins = dve.tensor_scalar(hT[:, j, k], bank[k // 4][:, (k % 4) * P:(k % 4 + 1) * P],
                                                        scol[:, q, 1, k:k + 1], scol[:, q, 0, k:k + 1], ALU.mult, ALU.add)
                            ins.then_inc(h_ev, 1)
                            hz = z[:, j, 0:V0].rearrange("p (h n) -> p h n", n=AT_N)
                            x1, x2 = hz[:, :, 0:HALF_ROPE], hz[:, :, HALF_ROPE:ROPE]
                            cos, sin = (rope[:, j, c * HALF_ROPE:(c + 1) * HALF_ROPE].unsqueeze(1)
                                        .broadcast_to([P, AT_H + AT_KV, HALF_ROPE]) for c in range(2))
                            dve.wait_ge(z_ev, 3 * i + 6)
                            dve.wait_ge(rot, i + 2)
                            link(dve.tensor_tensor(r[:, 0], x1, cos, ALU.mult))
                            link(dve.tensor_tensor(r[:, 1], x2, sin, ALU.mult))
                            link(dve.tensor_tensor(r[:, 2], x2, cos, ALU.mult))
                            link(dve.tensor_tensor(r[:, 3], x1, sin, ALU.mult))
                            link(dve.tensor_tensor(x1, r[:, 0], r[:, 1], ALU.subtract))
                            dve.tensor_tensor(x2, r[:, 2], r[:, 3], ALU.add).then_inc(rot, 1)
                link.end()


def window_attention(nc, a):
    W3 = 3 * P
    with Phase(nc, "attn") as ph:
        ident = ph.sb("ident", [P, P])
        sink = ph.sb("sink", [P, AT_H])
        qT = ph.sb("qT", [P, PAIRS, P])
        kT = ph.sb("kT", [P, AT_KV, W3])
        v = ph.sb("v", [P, 3, VW])
        band = ph.sb("band", [P, W3])
        s = ph.sb("s", [P, 4, W3])
        pT = ph.sb("pT", [P, 2, 3, P])
        mx = ph.sb("mx", [P, AT_H])
        neg = ph.sb("neg", [P, AT_H])
        total = ph.sb("total", [P, AT_H])
        es = ph.sb("es", [P, AT_H])
        o = ph.sb("o", [P, AT_H, AT_N])
        bank = ph.banks(8)
        cst, in_l, in_free, s_mm, m_r, n_r, e_r, t_mm, o_mm, es_in, es_r, o_r, done, vec, init, step = (ph.sem(n) for n in (
            "cst", "inputs_loaded", "inputs_free", "scores_mm", "max_ready", "neg_ready", "exp_ready", "probs_turned", "out_mm",
            "sink_diff", "sink_exp", "out_ready", "turn_done", "vec", "total_zeroed", "step"))
        t_ev = [ph.sem(f"turned_ev{e}") for e in range(2)]
        st = ph.sem("stored")

        with nc.Block() as block:

            @block.sync
            def _(sp):
                sp.dma_start(ident[:], a["const_f"][:, CONST["ident"]]).then_inc(cst, 16)
                sp.dma_start(sink[:], a["at_sink"].broadcast_to([P, AT_H])).then_inc(cst, 16)
                for q, (lo, hi) in enumerate(SEQ_TILES):
                    with sp.Fori(lo, hi) as i:
                        at = sp.snap(i + 1)
                        tile = sp.snap(i * 1)
                        slot = sp.snap(i * P + q * P)
                        sp.wait_ge(in_free, at)
                        sp.dma_start(qT[:].rearrange("p k t -> p (k t)"),
                                     a["qT_rows"][ds(tile, 1)].rearrange("a p n -> (a p) n")).then_inc(in_l, 16)
                        sp.dma_start(kT[:], a["kT_rows"][:, :, ds(slot, W3)]).then_inc(in_l, 16)
                        sp.dma_start(v[:], a["v_rows"][ds(slot, W3), :].rearrange("(c p) n -> p c n", p=P)).then_inc(in_l, 16)
                        sp.dma_start(band[:], a["const_band"][ds(tile, 1)].rearrange("a p n -> (a p) n")).then_inc(in_l, 16)

            @block.tensor
            def _(pe):
                pe.wait_ge(cst, 32)
                with pe.Fori(0, TILES) as i:
                    pe.wait_ge(done, i + 1)
                    pe.wait_ge(in_l, 64 * i + 64)
                    for n in range(AT_H + 3):
                        if n < AT_H:
                            half = slice(64 * (n % 2), 64 * (n % 2) + 64)
                            if n >= 3:
                                pe.wait_ge(m_r, i * AT_H + (n - 2))
                            pe.matmul(bank[n % 3][:, 0:W3], qT[half, n // 2, :], kT[half, n // 4, :],
                                      start=True, stop=True).then_inc(s_mm, 1)
                        h = n - 2
                        if 0 <= h < AT_H:
                            pe.wait_ge(e_r, i * AT_H + (h + 1))
                            if h >= 2:
                                pe.wait_ge(t_ev[h % 2], i * PAIRS + h // 2)
                            for c in range(3):
                                mm = pe.transpose(bank[3 + h % 2][:, c * P:(c + 1) * P], s[:, h % 4, c * P:(c + 1) * P], ident[:])
                            mm.then_inc(t_mm, 1)
                        h = n - 3
                        if 0 <= h < AT_H:
                            pe.wait_ge(t_ev[h % 2], i * PAIRS + (h // 2 + 1))
                            g = (h // 4) * AT_N
                            for c in range(3):
                                mm = pe.matmul(bank[5 + h // 8][:, (h % 8) * AT_N:(h % 8 + 1) * AT_N], pT[:, h % 2, c, :],
                                               v[:, c, g:g + AT_N], start=c == 0, stop=c == 2)
                            mm.then_inc(o_mm, 1)

            @block.scalar
            def _(act):
                act.sem_inc(st, 16)
                with act.Fori(0, TILES) as i:
                    act.wait_ge(init, i + 1)
                    for n in range(AT_H + 2):
                        if n < AT_H:
                            act.wait_ge(n_r, i * AT_H + (n + 1))
                            act.activation(s[:, n % 4], s[:, n % 4], ACT.Exp, bias=neg[:, n:n + 1],
                                           accum_out=total[:, n:n + 1]).then_inc(e_r, 1)
                        h = n - 2
                        if h >= 0 and h % 2:
                            act.wait_ge(t_mm, i * AT_H + (h + 1))
                            if h >= 2:
                                act.wait_ge(o_mm, i * AT_H + (h - 1))
                            act.activation(pT[:, 1].rearrange("p c t -> p (c t)"), bank[4][:, 0:W3], ACT.Copy).then_inc(t_ev[1], 1)
                    act.wait_ge(es_in, i + 1)
                    act.activation(es[:], es[:], ACT.Exp).then_inc(es_r, 1)
                    row = act.snap(i * P)
                    act.wait_ge(o_r, i + 1)
                    act.dma_start(a["at_o"][ds(row, P), :], o[:].rearrange("p h n -> p (h n)")).then_inc(st, 16)
                act.wait_ge(st, 16 * (TILES + 1))

            @block.vector
            def _(dve):
                dve.wait_ge(cst, 32)
                dve.sem_inc(done, 1)
                dve.sem_inc(in_free, 1)
                link = Chain(dve, vec, 4)
                with dve.Fori(0, TILES) as i:
                    link.turn(i)
                    link(dve.memset(total[:], 0.0))
                    dve.sem_inc(init, 1)
                    dve.wait_ge(in_l, 64 * i + 64)
                    for n in range(AT_H + 2):
                        if n < AT_H:
                            if n >= 4:
                                dve.wait_ge(t_mm, i * AT_H + (n - 3))
                            dve.wait_ge(s_mm, i * AT_H + (n + 1))
                            dve.sem_inc(step, 1)
                            dve.tensor_tensor_reduce(s[:, n % 4], bank[n % 3][:, 0:W3], band[:], 1.0, sink[:, n:n + 1],
                                                     ALU.add, ALU.max, mx[:, n:n + 1]).then_inc(m_r, 1)
                            dve.wait_ge(m_r, i * AT_H + (n + 1))
                            dve.tensor_scalar(neg[:, n:n + 1], mx[:, n:n + 1], -1.0, None, ALU.mult).then_inc(n_r, 1)
                        h = n - 2
                        if h >= 0 and h % 2 == 0:
                            dve.wait_ge(t_mm, i * AT_H + (h + 1))
                            if h >= 2:
                                dve.wait_ge(o_mm, i * AT_H + (h - 1))
                            dve.tensor_copy(pT[:, 0].rearrange("p c t -> p (c t)"), bank[3][:, 0:W3]).then_inc(t_ev[0], 1)
                    dve.wait_ge(n_r, i * AT_H + AT_H)
                    dve.tensor_tensor(es[:], sink[:], neg[:], ALU.add).then_inc(es_in, 1)
                    dve.wait_ge(es_r, i + 1)
                    link(dve.tensor_tensor(total[:], total[:], es[:], ALU.add))
                    link(dve.reciprocal(total[:], total[:]))
                    dve.wait_ge(o_mm, i * AT_H + AT_H)
                    dve.sem_inc(in_free, 1)
                    dve.wait_ge(st, 16 * i + 16)
                    link(dve.tensor_tensor(o[:, 0:8], heads(bank[5][:], AT_N), per_head(total[:, 0:8], AT_N), ALU.mult))
                    dve.tensor_tensor(o[:, 8:16], heads(bank[6][:], AT_N), per_head(total[:, 8:16], AT_N), ALU.mult).then_inc(o_r, 1)
                    dve.wait_ge(o_r, i + 1)
                    dve.sem_inc(done, 1)
                    link.end()


def trunk(nc, a):
    def scratch(name, shape, dt=F32):
        a[name] = nc.dram_tensor(f"scratch_{name}", shape, dt).ap()

    scratch("mod", (2 * DEPTH, 2, 3 * D))
    scratch("zt", (T, CHUNKS * P))
    scratch("zf", (3 * P, T))
    scratch("rw_y", (2, T, RW_W))
    scratch("rw_bonus", (2, T, RW_H))
    scratch("gd_o", (2, T, GD_W))
    scratch("x_mid", (T, D))
    scratch("x_mid2", (T, D))
    scratch("h_rows", (T, D))
    scratch("y_rows", (BLOCKS * P, D))
    scratch("row_tok", (BLOCKS * P, 1), I32)
    scratch("dest", (P, 2 * TILES), I32)
    scratch("gates", (P, 2 * TILES))
    scratch("blk", (1, OVER + 1), I32)
    scratch("qT_rows", (TILES, P, PAIRS * P))
    scratch("kT_rows", (P, AT_KV, SLOTS * P))
    scratch("v_rows", (SLOTS * P, VW))
    scratch("at_o", (T, D))
    ada_modulation(nc, a)
    input_projection(nc, a)
    rwkv_mixer(nc, a)
    deltanet_mixer(nc, a)
    close_mixer(nc, a, 0)
    experts(nc, a, 0)
    combine(nc, a, 0)
    attention_projection(nc, a)
    window_attention(nc, a)
    close_mixer(nc, a, 1)
    experts(nc, a, 1)
    combine(nc, a, 1)


_WEIGHTS = ["c_prompt", "c_sample", "ada_w", "ada_b", "ln_g", "ln_b", "ab_w_in", "rw_mu", "rw_w0", "rw_w_up", "rw_a0",
            "rw_a_up", "rw_g_up", "rw_k_k", "rw_k_a", "rw_r_k", "rw_gn_g", "rw_gn_b", "gd_conv", "gd_A_log", "gd_dt_bias",
            "gd_norm_g", "ab_w_out", "at_w_in", "at_sink", "at_w_out", "router_w", "router_bias", "moe_w_gate", "moe_w_up",
            "moe_w_down"]


def kernel(**inputs):
    import concourse.bacc as _bacc
    from concourse import mybir as _mybir
    from concourse.bass_utils import run_bass_kernel_spmd as _run

    nc = _bacc.Bacc("TRN2", target_bir_lowering=False, num_devices=1)
    given = {n: np.ascontiguousarray(inputs[n]) for n in _WEIGHTS}
    given["x_in"] = np.concatenate([np.asarray(inputs["x_prompt"])[0], np.asarray(inputs["x_sample"])[0]])
    given.update(constant_tables())
    arrays = {f"in_{n}_dram": v for n, v in given.items()}
    args = {n: nc.dram_tensor(f"in_{n}_dram", v.shape, _mybir.dt.from_np(v.dtype), kind="ExternalInput").ap()
            for n, v in given.items()}
    for n, length in (("y_prompt", S_PROMPT), ("y_sample", S_SAMPLE)):
        args[n] = nc.dram_tensor(f"out_{n}_dram", (1, length, D), F32, kind="ExternalOutput").ap()
    trunk(nc, args)
    r = _run(nc, [arrays], core_ids=[0])
    return tuple(r.results[0][f"out_{n}_dram"] for n in ("y_prompt", "y_sample"))
```

```python
import math
from contextlib import ExitStack

import concourse.bass as bass
import numpy as np
from concourse import mybir

F32 = mybir.dt.float32
I32 = mybir.dt.int32
U32 = mybir.dt.uint32
ALU = mybir.AluOpType
ACT = mybir.ActivationFunctionType
AX = mybir.AxisListType
ds = bass.ds

P = 128
D = 1024
KC = D // P
S_PROMPT, S_SAMPLE = 1024, 256
T = S_PROMPT + S_SAMPLE
TILES = T // P
TP = S_PROMPT // P
SEQ_TILES = ((0, TP), (TP, TILES))
DEPTH = 2
ALPHA = (2 * DEPTH) ** 0.25
LN_EPS = 1e-5

RW_H, RW_N = 8, 64
RW_W = RW_H * RW_N
GD_H, GD_N = 4, 128
GD_W = GD_H * GD_N
RW_GN_EPS = 64e-5
GD_NORM_EPS = 1e-6
AT_H, AT_KV, AT_N = 16, 4, 64
AT_COLS = (AT_H + 2 * AT_KV) * AT_N
ROPE = 16
HALF_ROPE = ROPE // 2
E, GROUPS, PER = 32, 8, 4
FF = 256
OVER = 20
MAX_OVER = T // P
BLOCKS = E + OVER

CONST = {}
_at = 0
for _name, _w in [("ident", P), ("ones", P), ("before", P), ("diag2", P), ("rank", 64), ("half", 1)] + [
        (f"{n}{d}", w) for d in range(2) for n, w in
        [("cum_incl", P), ("cum_excl", P), ("incl", P), ("strict", P), ("mask_b", 2 * P), ("mask_k", 2 * P),
         ("floor", P)]]:
    CONST[_name] = slice(_at, _at + _w)
    _at += _w
CONST_W = _at
LEVELS = 7
DECAY = math.exp(-0.5)
NEG = -1e30


def constant_tables():
    c = np.zeros((P, CONST_W), np.float32)
    s, t = np.arange(P)[:, None], np.arange(P)[None, :]
    c[:, CONST["ident"]] = s == t
    c[:, CONST["ones"]] = 1
    c[:, CONST["before"]] = s < t
    c[:, CONST["diag2"]] = s // 64 == t // 64
    c[:, CONST["rank"]] = np.arange(64)[None, :]
    c[:, CONST["half"]] = -0.5 * DECAY
    for d in range(2):
        incl, strict = ((s <= t), (s < t)) if d == 0 else ((s >= t), (s > t))
        c[:, CONST[f"cum_incl{d}"]] = -DECAY * (incl - 0.5)
        c[:, CONST[f"cum_excl{d}"]] = -DECAY * (strict - 0.5)
        c[:, CONST[f"incl{d}"]] = incl
        c[:, CONST[f"strict{d}"]] = strict
        c[:, CONST[f"mask_b{d}"]] = np.concatenate([-1.0 * strict, 1.0 * incl], 1)
        c[:, CONST[f"mask_k{d}"]] = np.concatenate([1.0 * strict, 1.0 * incl], 1)
        c[:, CONST[f"floor{d}"]] = np.where(incl, 0, NEG)
    levels = np.zeros((P, 2, LEVELS, P), np.int32)
    for n in range(LEVELS):
        b = 1 << n
        pair = (s // (2 * b) == t // (2 * b)) & (s // b != t // b)
        levels[:, 0, n] = pair & (s < t)
        levels[:, 1, n] = pair & (s > t)
    f32 = np.float32
    inv = f32(500000.0) ** (-np.arange(0, ROPE, 2, dtype=f32) / f32(ROPE))
    rope = []
    for length in (S_PROMPT, S_SAMPLE):
        ang = (np.arange(length, dtype=f32)[:, None] * inv.astype(f32)[None, :]).astype(f32)
        rope.append(np.concatenate([np.cos(ang), np.sin(ang)], 1))
    rope = np.concatenate(rope).astype(f32)
    band = np.full((3, P, 3 * P), NEG, f32)
    q, k = np.arange(P)[:, None], np.arange(P)[None, :]
    for n in range(3):
        if n > 0:
            band[n, :, 0:P] = np.where(k >= q, 0, NEG)
        band[n, :, P:2 * P] = 0
        if n < 2:
            band[n, :, 2 * P:] = np.where(k <= q, 0, NEG)
    which = [0] + [1] * (TP - 2) + [2] + [0] + [1] * (TILES - TP - 2) + [2]
    return {"const_f": c, "const_levels": levels.reshape(P, -1), "const_rope": rope,
            "const_tok": (np.arange(P)[:, None] + P * np.arange(TILES)[None, :]).astype(np.int32),
            "const_band": band[which]}


class Phase:

    def __init__(self, nc, name):
        self.nc, self.name, self.sems, self.ctx = nc, name, [], ExitStack()

    def sb(self, name, shape, dt=F32):
        return self.ctx.enter_context(self.nc.sbuf_tensor(f"{self.name}__{name}", shape, dt))

    def banks(self, n=8):
        return [self.ctx.enter_context(self.nc.psum_tensor(f"{self.name}__bank{b}", [P, 512], F32)) for b in range(n)]

    def sem(self, name):
        s = self.nc.alloc_semaphore(f"{self.name}__{name}")
        self.sems.append(s)
        return s

    def __enter__(self):
        return self

    def __exit__(self, *exc):
        if exc[0] is None:
            nums = sorted(s.num for s in self.sems)
            assert nums == list(range(nums[0], nums[-1] + 1))
            self.nc.clear_and_free_semaphores(range(nums[0], nums[-1] + 1))
            self.nc.all_engine_barrier()
        self.ctx.close()
        return False


class Chain:

    def __init__(self, eng, sem, per=0, base=0):
        self.eng, self.sem, self.per, self.base, self.n, self.i = eng, sem, per, base, 0, 0

    def turn(self, i):
        self.i, self.n = i, 0

    def end(self):
        assert self.n == self.per, f"{self.sem.name}: {self.n} links a turn, not {self.per}"

    def __call__(self, ins):
        self.n += 1
        ins.then_inc(self.sem, 1)
        self.eng.wait_ge(self.sem, self.i * self.per + (self.base + self.n))


def ada_modulation(nc, a):
    N = 3 * D // 512
    w_dram = a["ada_w"].rearrange("l s (k p) n -> (l s) p k n", p=P)
    b_dram = a["ada_b"].rearrange("l s n -> (l s) n")
    with Phase(nc, "ada") as ph:
        c_col = ph.sb("c_col", [P, KC, 2])
        c_exp = ph.sb("c_exp", [P, KC, 2])
        c_silu = ph.sb("c_silu", [P, KC, 2])
        w = ph.sb("w", [P, 2, KC, 512])
        bias = ph.sb("bias", [2, 3 * D])
        row = ph.sb("row", [2, 3 * D])
        bank = ph.banks(2)
        c_loaded, w_loaded0, w_loaded1 = ph.sem("c_loaded"), ph.sem("w_loaded0"), ph.sem("w_loaded1")
        w_loaded = (w_loaded0, w_loaded1)
        b_loaded, exp_done, silu_done = ph.sem("b_loaded"), ph.sem("exp_done"), ph.sem("silu_done")
        mm_done, row_done, stored, vec = ph.sem("mm_done"), ph.sem("row_done"), ph.sem("stored"), ph.sem("vec")
        with nc.Block() as block:

            @block.sync
            def _(sp):
                for q, src in enumerate((a["c_prompt"], a["c_sample"])):
                    sp.dma_start(c_col[:, :, q], src.rearrange("a (k p) -> p (a k)", p=P),
                                 allow_slow_non_contiguous=True).then_inc(c_loaded, 16)
                with sp.Fori(0, 4) as m:
                    for n in range(N):
                        i = m * N + n
                        at = sp.snap(i + 1)
                        which = sp.snap(m)
                        sp.wait_ge(mm_done, at)
                        sp.dma_start(w[:, n % 2], w_dram[ds(which, 1), :, :, n * 512:(n + 1) * 512].rearrange(
                            "a p k n -> p (a k) n")).then_inc(w_loaded[n % 2], 16)

            @block.scalar
            def _(act):
                act.wait_ge(c_loaded, 32)
                nc.scalar.activation(c_exp[:], c_col[:], ACT.Exp, scale=-1.0).then_inc(exp_done, 1)
                with act.Fori(0, 4) as m:
                    act.wait_ge(row_done, m * N + 1)
                    act.dma_start(bias[:], b_dram[ds(m, 1), :].broadcast_to([2, 3 * D])).then_inc(b_loaded, 16)
                    act.wait_ge(row_done, m * N + N + 1)
                    act.dma_start(a["mod"][ds(m, 1)].rearrange("a s n -> (a s) n"), row[:]).then_inc(stored, 16)
                act.wait_ge(stored, 16 * 5)

            @block.vector
            def _(dve):
                link = Chain(dve, vec, 2)
                dve.wait_ge(exp_done, 1)
                link(nc.vector.tensor_scalar(c_exp[:], c_exp[:], 1.0, None, ALU.add))
                link(nc.vector.reciprocal(c_exp[:], c_exp[:]))
                nc.vector.tensor_tensor(c_silu[:], c_col[:], c_exp[:], ALU.mult).then_inc(silu_done, 1)
                dve.sem_inc(row_done, 1)
                dve.sem_inc(stored, 16)
                with dve.Fori(0, 4) as m:
                    dve.wait_ge(b_loaded, m * 16 + 16)
                    dve.wait_ge(stored, m * 16 + 16)
                    for n in range(N):
                        dve.wait_ge(mm_done, m * N + (n + 3))
                        cols = slice(n * 512, (n + 1) * 512)
                        nc.vector.tensor_tensor(row[:, cols], bank[n % 2][0:2, :], bias[:, cols],
                                                ALU.add).then_inc(row_done, 1)

            @block.tensor
            def _(pe):
                pe.wait_ge(silu_done, 1)
                pe.sem_inc(mm_done, 2)
                with pe.Fori(0, 4) as m:
                    for n in range(N):
                        i = m * N + n
                        pe.wait_ge(w_loaded[n % 2], m * (16 * N // 2) + 16 * (n // 2 + 1))
                        if n >= 2:
                            pe.wait_ge(row_done, i)
                        else:
                            pe.wait_ge(row_done, m * N + 1)
                        for k in range(KC):
                            mm = nc.tensor.matmul(bank[n % 2][0:2, :], c_silu[:, k, :], w[:, n % 2, k, :],
                                                  start=k == 0, stop=k == KC - 1)
                        mm.then_inc(mm_done, 1)


RWC = 12
CONV0, GATE0, LOW0, AB0 = 12, 24, 28, 31
CHUNKS = 32
PAD = 2
SAMPLE0 = PAD + S_PROMPT + 2 * PAD
ZW = SAMPLE0 + S_SAMPLE + PAD
SPAN = ZW - 2 * PAD


def column_of(c):
    if c < RWC:
        return c * P
    if c < LOW0:
        return (c + 3) * P
    return (c - 16) * P if c < AB0 else AB0 * P


def input_projection(nc, a):
    x_dram, mod, zt, zf = a["x_in"], a["mod"], a["zt"], a["zf"]
    w_dram = a["ab_w_in"][0].rearrange("(k p) n -> p k n", p=P)
    GR = ((0, 512), (512, 512), (1024, 256))
    with Phase(nc, "inp") as ph:
        ident = ph.sb("ident", [P, P])
        hT = ph.sb("hT", [P, KC, T])
        x = ph.sb("x", [P, 2, D])
        scol = ph.sb("scol", [P, 2, 2, KC])
        w = ph.sb("w", [P, 2, KC, P])
        z = ph.sb("z", [P, 2, ZW])
        cb = ph.sb("cb", [P, 2, T])
        tb = ph.sb("tb", [P, 2, TILES, P])
        mu = ph.sb("mu", [P, 15])
        half_mu = ph.sb("half_mu", [P, 15])
        keep = ph.sb("keep", [P, 15])
        taps = ph.sb("taps", [P, 5, 12])
        acc = ph.sb("acc", [P, 2, ZW])
        bank = ph.banks(8)
        zbank = ((bank[0], bank[1], bank[2]), (bank[3], bank[4], bank[5]))
        tbank = (bank[6], bank[7], bank[6])
        cst, xt, ht, prep, vec = (ph.sem(n) for n in ("cst", "x_turned", "hT_ready", "prep", "vec"))
        x_loaded = (ph.sem("x_loaded0"), ph.sem("x_loaded1"))
        w_loaded = (ph.sem("w_loaded0"), ph.sem("w_loaded1"))
        stored = (ph.sem("stored0"), ph.sem("stored1"))
        z_mm, z_ev, cb_ready, conv, tr_mm, t_ev = (
            ph.sem(n) for n in ("z_mm", "z_ev", "cb_ready", "conv", "tr_mm", "t_ev"))
        zf_stored = [ph.sem(f"zf_stored{n}") for n in range(3)]

        def parts(j):
            return ((z[:, j, PAD:PAD + S_PROMPT], cb[:, j, 0:S_PROMPT]),
                    (z[:, j, SAMPLE0:SAMPLE0 + S_SAMPLE], cb[:, j, S_PROMPT:T]))

        with nc.Block() as block:

            @block.sync
            def _(sp):
                sp.dma_start(ident[:], a["const_f"][:, CONST["ident"]]).then_inc(cst, 16)
                for q in range(2):
                    for part in range(2):
                        sp.dma_start(scol[:, q, part], mod[0, q, part * D:(part + 1) * D].rearrange("(k p) -> p k", p=P),
                                     allow_slow_non_contiguous=True).then_inc(cst, 16)
                sp.dma_start(mu[:], a["rw_mu"][0].rearrange("(c p) -> p c", p=P),
                             allow_slow_non_contiguous=True).then_inc(cst, 16)
                for tap in range(5):
                    sp.dma_start(taps[:, tap], a["gd_conv"][0, tap].rearrange("(c p) -> p c", p=P),
                                 allow_slow_non_contiguous=True).then_inc(cst, 16)
                with sp.Fori(0, TILES // 2) as p:
                    for j in range(2):
                        at = sp.snap(2 * p + (j + 1))
                        row = sp.snap((2 * p + j) * P)
                        sp.wait_ge(xt, at)
                        sp.dma_start(x[:, j], x_dram[ds(row, P), :]).then_inc(x_loaded[j], 16)
                sp.sem_inc(stored[0], 16)
                sp.sem_inc(stored[1], 16)

                def store(c, j):
                    at, col = (3 * c + 6, c * P) if isinstance(c, int) else (sp.snap(3 * c + 6), sp.snap(c * P))
                    sp.wait_ge(t_ev, at)
                    sp.dma_start(zt[:, ds(col, P)].rearrange("(t p) f -> p t f", p=P), tb[:, j]).then_inc(stored[j], 16)

                with sp.Fori(0, LOW0 // 2) as p:
                    for j in range(2):
                        store(2 * p + j, j)
                for c in range(LOW0, CHUNKS):
                    if c < AB0:
                        sp.wait_ge(cb_ready, c + 3)
                        sp.dma_start(zf[(c - LOW0) * P:(c - LOW0 + 1) * P, :], cb[:, c % 2]).then_inc(zf_stored[c - LOW0], 16)
                    store(c, c % 2)
                for j in range(2):
                    sp.wait_ge(stored[j], 16 * (CHUNKS // 2 + 1))
                for n in range(3):
                    sp.wait_ge(zf_stored[n], 16)

            @block.tensor
            def _(pe):
                pe.wait_ge(cst, 16 * 11)
                pe.sem_inc(xt, 2)
                with pe.Fori(0, TILES // 2) as p:
                    for j in range(2):
                        pe.wait_ge(x_loaded[j], 16 * p + 16)
                        pe.wait_ge(ht, 2 * p + (j + 1))
                        for k in range(KC):
                            mm = nc.tensor.transpose(bank[2 * j + k // 4][:, (k % 4) * P:(k % 4 + 1) * P],
                                                     x[:, j, k * P:(k + 1) * P], ident[:])
                        mm.then_inc(xt, 1)
                pe.wait_ge(ht, TILES + 2)
                pe.sem_inc(z_mm, 6)
                pe.sem_inc(tr_mm, 6)

                def project(c, j, pair):
                    pe.wait_ge(w_loaded[j], 16 * pair + 16)
                    if not isinstance(c, int) or c > 0:
                        pe.wait_ge(z_ev, 3 * c)
                    for g, (t0, n) in enumerate(GR):
                        for k in range(KC):
                            mm = nc.tensor.matmul(zbank[j][g][:, 0:n], w[:, j, k, :], hT[:, k, t0:t0 + n],
                                                  start=k == 0, stop=k == KC - 1)
                        mm.then_inc(z_mm, 1)

                def turn(c, j):
                    pe.wait_ge(cb_ready, c + 3)
                    pe.wait_ge(t_ev, 3 * c + 3)
                    for g, (t0, n) in enumerate(GR):
                        if g == 2:
                            pe.wait_ge(t_ev, 3 * c + 4)
                        for t in range(n // P):
                            mm = nc.tensor.transpose(tbank[g][:, t * P:(t + 1) * P],
                                                     cb[:, j, t0 + t * P:t0 + (t + 1) * P], ident[:])
                        mm.then_inc(tr_mm, 1)

                project(0, 0, 0)
                with pe.Fori(0, CHUNKS // 2 - 1) as p:
                    project(2 * p + 1, 1, p)
                    turn(2 * p, 0)
                    project(2 * p + 2, 0, p + 1)
                    turn(2 * p + 1, 1)
                project(CHUNKS - 1, 1, CHUNKS // 2 - 1)
                turn(CHUNKS - 2, 0)
                turn(CHUNKS - 1, 1)

            @block.scalar
            def _(act):
                act.sem_inc(z_ev, 3)
                act.sem_inc(t_ev, 3)

                def evacuate(c, j):
                    act.wait_ge(cb_ready, c + 1)
                    for g in range(3):
                        n = GR[g][1]
                        act.wait_ge(z_mm, 3 * c + (g + 7))
                        start = PAD + GR[g][0] if g < 2 else SAMPLE0
                        nc.scalar.activation(z[:, j, start:start + n], zbank[j][g][:, 0:n], ACT.Copy).then_inc(z_ev, 1)

                def turned(c, j, pair):
                    act.wait_ge(stored[j], 16 * pair + 16)
                    for g, (t0, n) in enumerate(GR):
                        act.wait_ge(tr_mm, 3 * c + (g + 7))
                        nc.scalar.activation(tb[:, j, t0 // P:(t0 + n) // P, :].rearrange("p t f -> p (t f)"),
                                             tbank[g][:, 0:n], ACT.Copy).then_inc(t_ev, 1)

                def from_z(c, j, f, n_prep):
                    act.wait_ge(z_ev, 3 * c + 6)
                    act.wait_ge(tr_mm, 3 * c + 3)
                    (z0, c0), (z1, c1) = parts(j)
                    nc.scalar.activation(c0, z0, f).then_inc(prep, 1)
                    act.wait_ge(prep, n_prep)
                    nc.scalar.activation(c1, z1, f).then_inc(cb_ready, 1)

                def in_place(j, f, n_conv):
                    act.wait_ge(conv, n_conv)
                    nc.scalar.activation(cb[:, j], cb[:, j], f).then_inc(cb_ready, 1)

                act.wait_ge(prep, 4)
                evacuate(0, 0)
                with act.Fori(0, RWC // 2) as p:
                    for j in range(2):
                        evacuate(2 * p + (j + 1), 1 - j)
                        turned(2 * p + j, j, p)
                with act.Fori(CONV0 // 2, GATE0 // 2) as p:
                    for j in range(2):
                        in_place(j, ACT.Silu, 2 * p + (j + 2 - CONV0))
                        evacuate(2 * p + (j + 1), 1 - j)
                        turned(2 * p + j, j, p)
                with act.Fori(GATE0 // 2, LOW0 // 2) as p:
                    for j in range(2):
                        from_z(2 * p + j, j, ACT.Silu, 2 * p + (j + 5 - GATE0))
                        evacuate(2 * p + (j + 1), 1 - j)
                        turned(2 * p + j, j, p)
                in_place(0, ACT.Tanh, 14)
                evacuate(LOW0 + 1, 1)
                turned(LOW0, 0, LOW0 // 2)
                evacuate(LOW0 + 2, 0)
                turned(LOW0 + 1, 1, LOW0 // 2)
                in_place(0, ACT.Sigmoid, 15)
                evacuate(AB0, 1)
                turned(LOW0 + 2, 0, LOW0 // 2 + 1)
                act.wait_ge(zf_stored[1], 16)
                from_z(AB0, 1, ACT.Copy, 9)
                turned(AB0, 1, AB0 // 2)

            @block.vector
            def _(dve):
                for lo, hi in ((0, PAD), (PAD + S_PROMPT, SAMPLE0), (SAMPLE0 + S_SAMPLE, ZW)):
                    nc.vector.memset(z[:, :, lo:hi], 0.0).then_inc(prep, 1)
                dve.wait_ge(cst, 16 * 11)
                link = Chain(dve, vec, 3)
                link(nc.vector.tensor_scalar(scol[:, :, 1], scol[:, :, 1], 1.0, None, ALU.add))
                link(nc.vector.tensor_scalar(half_mu[:], mu[:], 0.5, None, ALU.mult))
                link(nc.vector.tensor_scalar(keep[:], mu[:], -1.0, 1.0, ALU.mult, ALU.add))
                dve.sem_inc(prep, 1)
                dve.sem_inc(ht, 2)
                for q, (first, last) in enumerate(SEQ_TILES):
                    with dve.Fori(first // 2, last // 2) as p:
                        for j in range(2):
                            dve.wait_ge(xt, 2 * p + (j + 3))
                            at = dve.snap((2 * p + j) * P)
                            for k in range(KC):
                                ins = nc.vector.tensor_scalar(hT[:, k, ds(at, P)],
                                                              bank[2 * j + k // 4][:, (k % 4) * P:(k % 4 + 1) * P],
                                                              scol[:, q, 1, k:k + 1], scol[:, q, 0, k:k + 1], ALU.mult, ALU.add)
                            ins.then_inc(ht, 1)
                dve.sem_inc(cb_ready, 2)
                dve.sem_inc(conv, 1)

                def shift(c, j, m, step, signal, last, n_last):
                    dve.wait_ge(z_ev, 3 * c + 6)
                    dve.wait_ge(tr_mm, 3 * c + 3)
                    dve.wait_ge(last, n_last)
                    nc.vector.tensor_tensor(acc[:, 0, 0:SPAN], z[:, j, PAD - 1:PAD - 1 + SPAN],
                                            z[:, j, PAD + 1:PAD + 1 + SPAN], ALU.add).then_inc(vec, 1)
                    dve.wait_ge(vec, step + 1)
                    nc.vector.tensor_scalar(acc[:, 1, 0:SPAN], z[:, j, PAD:PAD + SPAN], keep[:, m], None,
                                            ALU.mult).then_inc(vec, 1)
                    dve.wait_ge(vec, step + 2)
                    for n, (lo, hi, out) in enumerate(((0, S_PROMPT, 0), (SAMPLE0 - PAD, SAMPLE0 - PAD + S_SAMPLE, S_PROMPT))):
                        nc.vector.scalar_tensor_tensor(cb[:, j, out:out + hi - lo], acc[:, 0, lo:hi], half_mu[:, m],
                                                       acc[:, 1, lo:hi], ALU.mult, ALU.add).then_inc(signal if n else vec, 1)

                with dve.Fori(0, RWC // 2) as p:
                    for j in range(2):
                        shift(2 * p + j, j, ds(dve.snap(2 * p + j), 1), 6 * p + (3 * j + 3),
                              cb_ready, cb_ready, 2 * p + (j + 2))
                steps = 3 + 3 * RWC
                dve.wait_ge(cb_ready, RWC + 2)
                with dve.Fori(CONV0 // 2, GATE0 // 2) as p:
                    for j in range(2):
                        tap = [taps[:, k, ds(dve.snap(2 * p + (j - CONV0)), 1)] for k in range(5)]
                        step = 10 * p + (5 * j + steps - 5 * CONV0)
                        dve.wait_ge(z_ev, 6 * p + (3 * j + 6))
                        dve.wait_ge(tr_mm, 6 * p + (3 * j + 3))
                        dve.wait_ge(conv, 2 * p + (j + 1 - CONV0))
                        nc.vector.tensor_scalar(acc[:, 0, 0:SPAN], z[:, j, 0:SPAN], tap[0], None, ALU.mult).then_inc(vec, 1)
                        for k in range(1, 4):
                            dve.wait_ge(vec, step + k)
                            nc.vector.scalar_tensor_tensor(acc[:, k % 2, 0:SPAN], z[:, j, k:k + SPAN], tap[k],
                                                           acc[:, (k - 1) % 2, 0:SPAN], ALU.mult, ALU.add).then_inc(vec, 1)
                        dve.wait_ge(vec, step + 4)
                        for n, (lo, hi, out) in enumerate(((0, S_PROMPT, 0), (SAMPLE0 - PAD, SAMPLE0 - PAD + S_SAMPLE, S_PROMPT))):
                            nc.vector.scalar_tensor_tensor(cb[:, j, out:out + hi - lo], z[:, j, lo + 4:hi + 4], tap[4],
                                                           acc[:, 1, lo:hi], ALU.mult, ALU.add).then_inc(conv if n else vec, 1)
                steps += 5 * (GATE0 - CONV0)
                shift(LOW0, 0, slice(12, 13), steps, conv, conv, 13)
                shift(LOW0 + 1, 1, slice(13, 14), steps + 3, cb_ready, conv, 14)
                dve.wait_ge(zf_stored[0], 16)
                shift(LOW0 + 2, 0, slice(14, 15), steps + 6, conv, cb_ready, LOW0 + 4)

            @block.gpsimd
            def _(pool):
                for first, last, shift in ((0, RWC, 0), (RWC, LOW0, 3 * P)):
                    with pool.Fori(first // 2, last // 2) as p:
                        for j in range(2):
                            at = pool.snap(6 * p + (3 * j + 3))
                            col = pool.snap((2 * p + j) * P + shift)
                            pool.wait_ge(z_mm, at)
                            pool.dma_start(w[:, j], w_dram[:, :, ds(col, P)]).then_inc(w_loaded[j], 16)
                for c in range(LOW0, CHUNKS):
                    n = P if c < AB0 else 4 * GD_H
                    pool.wait_ge(z_mm, 3 * c + 3)
                    pool.dma_start(w[:, c % 2, :, 0:n], w_dram[:, :, column_of(c):column_of(c) + n]).then_inc(w_loaded[c % 2], 16)




def mixer_runs():
    return [(lo, hi, 0, lo + hi - 1) for lo, hi in SEQ_TILES]


def units(bank):
    return bank[:].rearrange("p (q t) -> p q t", q=4)


class Inverse:
    X_TURN, Y_TURN, D_TURN = 2 * LEVELS, LEVELS, LEVELS - 1

    def __init__(self, ph, neg_aT, y_bank, t_bank):
        self.neg_aT, self.y_bank, self.t_bank = neg_aT, y_bank, t_bank
        self.X = ph.sb("X", [P, 2, 4, P])
        self.XT = ph.sb("XT", [P, 2, 4, P])
        self.Y = ph.sb("Y", [P, 2, 4, P])
        self.cleared = ph.sem("Y_cleared")
        self.x_done = [ph.sem(f"x_done{e}") for e in range(2)]
        self.y_mm = [ph.sem(f"y_mm{e}") for e in range(2)]
        self.y_ev = [ph.sem(f"y_ev{e}") for e in range(2)]
        self.update = ph.sem("update")
        self.dt_mm = [ph.sem(f"dt_mm{e}") for e in range(2)]

    @staticmethod
    def half(ap, n, second):
        if len(ap.shape) == 2:
            return ap.rearrange("p (g two b) -> p g two b", two=2, b=1 << n)[:, :, second, :]
        return ap.rearrange("p q (g two b) -> p q g two b", two=2, b=1 << n)[:, :, :, second, :]

    def tensor(self, pe, i, between=lambda n: None):
        for n in range(LEVELS):
            for e in range(2):
                pe.wait_ge(self.x_done[e], i * self.X_TURN + max(1, 2 * n))
                for q in range(4):
                    mm = pe.matmul(self.y_bank[e][:, q * P:(q + 1) * P], self.neg_aT(e)[:, q, :], self.X[:, e, q, :],
                                   start=True, stop=True)
                mm.then_inc(self.y_mm[e], 1)
            if n == 0:
                between(0)
                continue
            for e in range(2):
                pe.wait_ge(self.y_ev[e], i * self.D_TURN + n)
                pe.wait_ge(self.x_done[e], i * self.X_TURN + (2 * n + 1))
                if n < LEVELS - 1:
                    for q in range(4):
                        pe.matmul(self.y_bank[e][:, q * P:(q + 1) * P], self.XT[:, e, q, :], self.Y[:, e, q, :],
                                  start=True, stop=True)
                for q in range(4):
                    mm = pe.matmul(self.t_bank[e][:, q * P:(q + 1) * P], self.Y[:, e, q, :], self.XT[:, e, q, :],
                                   start=True, stop=True)
                mm.then_inc(self.dt_mm[e], 1)
            between(n)

    def scalar(self, act, i, direction, between=lambda n: None):
        for n in range(1, LEVELS):
            for e in range(2):
                act.wait_ge(self.y_mm[e], i * self.Y_TURN + (n + 1))
                if n > 1:
                    act.wait_ge(self.dt_mm[e], i * self.D_TURN + (n - 1))
                act.activation(self.half(self.Y[:, e], n, direction(e)), self.half(units(self.y_bank[e]), n, direction(e)), ACT.Copy).then_inc(
                    self.y_ev[e], 1)
            between(n)

    def vector(self, dve, i, levels, direction, between=lambda n: None):
        def update(e, x, n, second, src):
            mask = self.half(levels[:, 1 - second, n, :], n, second)
            dve.copy_predicated(self.half(x[:, e], n, second),
                                mask.unsqueeze(1).broadcast_to([P, 4, mask.shape[1], mask.shape[2]]),
                                self.half(src, n, second)).then_inc(self.x_done[e], 1)
        for n in range(LEVELS):
            for e in range(2):
                d = direction(e)
                if n == 0:
                    dve.wait_ge(self.y_mm[e], i * self.Y_TURN + 1)
                else:
                    dve.wait_ge(self.dt_mm[e], i * self.D_TURN + n)
                dve.sem_inc(self.update, 1)
                if n < LEVELS - 1:
                    update(e, self.X, n, d, units(self.y_bank[e]))
                update(e, self.XT, n, 1 - d, units(self.t_bank[e]) if n else self.neg_aT(e))
            between(n)


def heads(ap, n):
    return ap.rearrange("p (h n) -> p h n", n=n)


def per_head(col, n):
    return col.unsqueeze(2).broadcast_to([P, col.shape[1], n])


def rwkv_mixer(nc, a):
    zt, zf, y_out, bonus_out = a["zt"], a["zf"], a["rw_y"], a["rw_bonus"]
    with Phase(nc, "rwkv") as ph:
        cf = ph.sb("consts", [P, CONST_W])
        levels = ph.sb("levels", [P, 2, LEVELS, P], I32)
        rkv = ph.sb("rkv", [P, 3, RW_W])
        low = ph.sb("low", [65, 2, P])
        up = ph.sb("up", [65, 2, 2, RW_W])
        rows = ph.sb("rows", [P, 3, RW_W])
        gates = ph.sb("gates", [P, 2, RW_W])
        dec = ph.sb("dec", [P, 3, RW_W])
        ec = ph.sb("ec", [P, 4])
        zero = ph.sb("zero", [P, D])
        kk = ph.sb("kk", [P, RW_W])
        kdir = ph.sb("kdir", [P, RW_W])
        tmp = ph.sb("tmp", [P, RW_W])
        tmp2 = ph.sb("tmp2", [P, RW_W])
        norm = ph.sb("norm", [P, RW_H])
        bonus = ph.sb("bonus", [P, RW_H])
        alpha = ph.sb("alpha", [P, RW_W])
        rho = ph.sb("rho", [P, RW_W])
        beta = ph.sb("beta", [P, RW_W])
        kappa = ph.sb("kappa", [P, RW_W])
        arT = ph.sb("arT", [P, 4, 2, P])
        bT = ph.sb("bT", [P, 4, P])
        kT = ph.sb("kT", [P, 4, P])
        BP = ph.sb("BP", [P, 2, 4, 2, P])
        KP = ph.sb("KP", [P, 2, 4, 2, P])
        H = ph.sb("H", [P, 4, P])
        Hp = ph.sb("Hp", [P, 4, P])
        Xs = ph.sb("Xs", [P, RW_W])
        Un = ph.sb("Un", [P, RW_W])
        y = ph.sb("y", [P, RW_W])
        bank = ph.banks(8)
        inv = Inverse(ph, lambda e: BP[:, e, :, 0, :], (bank[1], bank[3]), (bank[2], bank[4]))
        cst, ins_l, v_l, vec, vec_p, reset, h_done, half_mm, ec_ready = (ph.sem(n) for n in (
            "cst", "inputs_loaded", "v_loaded", "vec", "vec_prepare", "reset", "state_done", "half_mm", "ec_ready"))
        zeroed, zero_st = ph.sem("zeroed"), ph.sem("zero_stored")
        raw, e_done, sig, cum, dec_ready, sq, root = (
            ph.sem(n) for n in ("raw_mm", "exp_raw", "sigmoids", "cum_mm", "decays", "squares", "root"))
        ops, tr, tr_ev, prod, prod_ev, hp, x_mm, x_ev, u_mm, u_ev, y_mm, y_ev, h_mm, done, prep_done, y_st, b_rd, b_st, b_free = (
            ph.sem(n) for n in ("operands", "turned", "turned_ev", "products", "products_ev", "state_scaled", "x_mm", "x_ev",
                                "u_mm", "u_ev", "out_mm", "out_ev", "state_mm", "turn_done", "prep_done", "y_stored",
                                "bonus_ready", "bonus_stored", "bonus_free"))

        operands = (alpha, rho, beta, kappa)
        current = {}
        plan = [(d, d * TILES + lo, d * TILES + hi, lo, hi) for d in range(2) for lo, hi in SEQ_TILES]

        def run_turns(eng, turn, start=lambda run: None):
            for n, (d, first, last, lo, hi) in enumerate(plan):
                current["run"] = (lo, hi)
                start(n)
                with eng.Fori(first, last - 1) as i:
                    turn(i, d, (i + 1, d))
                turn(last - 1, d, (last, plan[n + 1][0]) if n + 1 < len(plan) else None)

        def row_of(d, lo, hi, i):
            return i * P if d == 0 else i * -P + (hi - 1 + lo + TILES) * P

        with nc.Block() as block:

            @block.sync
            def _(sp):
                sp.dma_start(cf[:], a["const_f"]).then_inc(cst, 16)
                sp.dma_start(levels[:].rearrange("p d n t -> p (d n t)"), a["const_levels"]).then_inc(cst, 16)
                for n, name in enumerate(("rw_k_k", "rw_k_a")):
                    sp.dma_start(rows[:, n], a[name].broadcast_to([P, RW_W])).then_inc(cst, 16)
                sp.dma_start(rows[:, 2], a["rw_r_k"].rearrange("a h n -> a (h n)").broadcast_to([P, RW_W])).then_inc(cst, 16)
                for n, (u, b) in enumerate((("rw_w_up", "rw_w0"), ("rw_a_up", "rw_a0"))):
                    sp.dma_start(up[0:64, :, n], a[u][0].rearrange("d r c -> r d c")).then_inc(cst, 16)
                    sp.dma_start(up[64:65, :, n], a[b]).then_inc(cst, 16)
                sp.wait_ge(zeroed, 1)
                sp.dma_start(a["y_rows"][E * P:, :].rearrange("(n p) c -> p n c", p=P),
                             zero[:].unsqueeze(1).broadcast_to([P, OVER, D])).then_inc(zero_st, 16)
                for d, first, last, lo, hi in plan:
                    with sp.Fori(first, last) as i:
                        at = sp.snap(i + 1)
                        row = sp.snap(row_of(d, lo, hi, i))
                        sp.wait_ge(prep_done, at)
                        sp.dma_start(rkv[:, 0:2, :].rearrange("p a c -> p (a c)"), zt[ds(row, P), 0:2 * RW_W]).then_inc(ins_l, 16)
                        for n in range(2):
                            sp.dma_start(low[0:64, n, :], zf[n * P + 64 * d:n * P + 64 * d + 64, ds(row, P)]).then_inc(ins_l, 16)
                        at2 = sp.snap(i + 1)
                        sp.wait_ge(done, at2)
                        sp.dma_start(rkv[:, 2, :], zt[ds(row, P), 2 * RW_W:3 * RW_W]).then_inc(v_l, 16)

                sp.wait_ge(zero_st, 16)

            @block.tensor
            def _(pe):
                pe.wait_ge(cst, 16 * 9)
                ident = cf[:, CONST["ident"]]

                def prepare(i, d, n):
                    if n == 0:
                        pe.wait_ge(ins_l, i * 48 + 48)
                        for w in range(2):
                            pe.matmul(bank[(0, 7)[w]][:], low[:, w, :], up[:, d, w, :], start=True, stop=True).then_inc(raw, 1)
                    if n == 3:
                        pe.wait_ge(sig, i + 1)
                        pe.wait_ge(e_done, i * 2 + 2)
                        pe.matmul(bank[0][:], cf[:, CONST[f"cum_incl{d}"]], gates[:, 0], start=True, stop=True)
                        pe.matmul(bank[7][:], cf[:, CONST[f"cum_excl{d}"]], gates[:, 0], start=True, stop=True).then_inc(cum, 1)

                def turned(i, which):
                    for n in which:
                        pe.wait_ge(ops, i * 4 + (n + 1))
                        for q in range(4):
                            mm = pe.transpose(bank[1 + n][:, q * P:(q + 1) * P], operands[n][:, q * P:(q + 1) * P], ident)
                        mm.then_inc(tr, 1)

                def half_sum(i):
                    for q in range(4):
                        mm = pe.matmul(bank[5][:, q:q + 1], gates[:, 0, q * P:(q + 1) * P], cf[:, CONST["half"]],
                                       start=True, stop=True)
                    mm.then_inc(half_mm, 1)

                def busy(k):
                    for _ in range(k):
                        pe.matmul(bank[7][:, 0:256], cf[:, 0:P], cf[:, 0:256], start=True, stop=True)

                def turn(i, d, following):
                    busy(3)
                    turned(i, (2, 3))
                    busy(6)
                    pe.wait_ge(tr_ev, i * 4 + 4)
                    pe.wait_ge(ec_ready, i + 1)
                    pe.wait_ge(done, i + 1)
                    pe.wait_ge(dec_ready, i * 3 + 3)
                    for kind, src in ((0, bT), (1, kT)):
                        for q in range(4):
                            for e in range(2):
                                half = slice(64 * e, 64 * e + 64)
                                b = bank[(1 + 2 * kind + 4 * e + q // 2) % 8]
                                mm = pe.matmul(b[:, (q % 2) * 256:(q % 2 + 1) * 256], src[half, q, :],
                                               arT[half, q].rearrange("p a t -> p (a t)"), start=True, stop=True)
                                if q % 2 == 1:
                                    mm.then_inc(prod, 1)
                    pe.wait_ge(prod_ev, i * 8 + 8)
                    pe.wait_ge(hp, i + 1)
                    pe.wait_ge(v_l, i * 16 + 16)
                    for b, part in ((5, 0), (6, 1)):
                        for q in range(4):
                            pe.matmul(bank[b][:, q * P:(q + 1) * P], arT[:, q, part, :], Hp[:, q, :], start=q == 0, stop=False,
                                      skip_group_check=True)
                            for e in range(2):
                                c = (2 * q + e) * 64
                                mm = pe.matmul(bank[b][:, c:c + 64], KP[:, e, q, part, :], rkv[:, 2, c:c + 64],
                                               start=False, stop=part == 0, skip_group_check=True)
                        if part == 0:
                            mm.then_inc(x_mm, 1)
                    inv.tensor(pe, i, lambda n: following and prepare(*following, n))
                    pe.wait_ge(x_ev, i + 1)
                    if following:
                        pe.wait_ge(dec_ready, i * 3 + 6)
                    for e in range(2):
                        pe.wait_ge(inv.x_done[e], i * inv.X_TURN + inv.X_TURN)
                    for q in range(4):
                        for e in range(2):
                            c = (2 * q + e) * 64
                            mm = pe.matmul(bank[7][:, c:c + 64], inv.XT[:, e, q, :], Xs[:, c:c + 64], start=True, stop=True)
                    mm.then_inc(u_mm, 1)
                    if following:
                        half_sum(following[0])
                        turned(following[0], (0, 1))
                    pe.wait_ge(u_ev, i + 1)
                    for q in range(4):
                        for e in range(2):
                            c = (2 * q + e) * 64
                            mm = pe.matmul(bank[6][:, c:c + 64], BP[:, e, q, 1, :], Un[:, c:c + 64], start=False, stop=True,
                                           skip_group_check=True)
                    mm.then_inc(y_mm, 1)
                    for q in range(4):
                        pair = slice(q * P, (q + 1) * P)
                        pe.matmul(bank[0][:, pair], kappa[:, pair], rkv[:, 2, pair], start=True, stop=False)
                        mm = pe.matmul(bank[0][:, pair], beta[:, pair], Un[:, pair], start=False, stop=True)
                    mm.then_inc(h_mm, 1)

                for n in range(LEVELS):
                    prepare(0, 0, n)
                half_sum(0)
                turned(0, (0, 1))
                run_turns(pe, turn)

            @block.scalar
            def _(act):
                act.sem_inc(y_st, 16)
                act.wait_ge(inv.cleared, 1)

                def prepare(i, n):
                    if n == 1:
                        for w in range(2):
                            act.wait_ge(raw, i * 2 + (w + 1))
                            act.activation(gates[:, w], bank[(0, 7)[w]][:], ACT.Exp, scale=-1.0).then_inc(e_done, 1)
                    if n == 4:
                        act.wait_ge(cum, i + 1)
                        act.activation(dec[:, 2], bank[7][:], ACT.Exp).then_inc(dec_ready, 1)
                        act.activation(dec[:, 0], bank[0][:], ACT.Exp).then_inc(dec_ready, 1)
                        act.activation(dec[:, 1], bank[0][:], ACT.Exp, scale=-1.0).then_inc(dec_ready, 1)
                        act.wait_ge(sq, i + 1)
                        act.activation(norm[:], norm[:], ACT.Sqrt).then_inc(root, 1)

                def turned(i, which):
                    for n in which:
                        dst = (arT[:, :, 0, :], arT[:, :, 1, :], bT[:], kT[:])[n]
                        act.wait_ge(tr, i * 4 + (n + 1))
                        act.activation(dst, heads(bank[1 + n][:], P), ACT.Copy).then_inc(tr_ev, 1)

                def turn(i, d, following):
                    turned(i, (2, 3))
                    act.wait_ge(half_mm, i + 1)
                    act.wait_ge(h_done, i + 1)
                    act.activation(ec[:], bank[5][:, 0:4], ACT.Exp).then_inc(ec_ready, 1)
                    act.wait_ge(x_mm, i + 1)
                    act.activation(Xs[:], bank[5][:], ACT.Copy).then_inc(x_ev, 1)
                    inv.scalar(act, i, lambda e: d, lambda n: following and prepare(following[0], n))
                    act.wait_ge(u_mm, i + 1)
                    act.activation(Un[:], bank[7][:], ACT.Copy, scale=-1.0).then_inc(u_ev, 1)
                    if following:
                        turned(following[0], (0, 1))
                    act.wait_ge(y_mm, i + 1)
                    act.wait_ge(y_st, i * 16 + 16)
                    act.activation(y[:], bank[6][:], ACT.Copy).then_inc(y_ev, 1)
                    row = row_of(d, *current["run"], i)
                    row = row if isinstance(i, int) else act.snap(row)
                    act.wait_ge(y_ev, i + 1)
                    act.dma_start(y_out[d, ds(row, P), :], y[:]).then_inc(y_st, 16)

                for n in range(LEVELS):
                    prepare(0, n)
                turned(0, (0, 1))
                run_turns(act, turn)
                act.wait_ge(y_st, 16 * (2 * TILES + 1))

            @block.gpsimd
            def _(pool):
                for d, first, last, lo, hi in plan:
                    with pool.Fori(first, last) as i:
                        pool.wait_ge(b_rd, i + 1)
                        pool.dma_start(bonus_out[d, ds(pool.snap(row_of(d, lo, hi, i)), P), :], bonus[:]).then_inc(b_st, 16)
                        pool.wait_ge(b_st, i * 16 + 16)
                        pool.sem_inc(b_free, 1)

            @block.vector
            def _(dve):
                dve.memset(zero[:], 0.0).then_inc(zeroed, 1)
                dve.memset(inv.Y[:], 0.0).then_inc(inv.cleared, 1)
                dve.memset(low[64:65], 1.0).then_inc(vec, 1)
                dve.wait_ge(vec, 1)
                dve.wait_ge(cst, 16 * 9)
                dve.sem_inc(prep_done, 1)
                dve.sem_inc(done, 1)
                dve.sem_inc(b_free, 1)
                dve.sem_inc(h_done, 1)
                state = {}

                def prepare(i, n):
                    if n == 0:
                        state["link"] = Chain(dve, vec_p, 14)
                        state["link"].turn(i)
                    link = state["link"]
                    if n == 0:
                        dve.wait_ge(ins_l, i * 48 + 48)
                        link(dve.tensor_tensor(kk[:], rkv[:, 1], rows[:, 0], ALU.mult))
                        link(dve.tensor_tensor(tmp[:], kk[:], kk[:], ALU.mult))
                        link(dve.tensor_reduce(norm[:], heads(tmp[:], 64), AX.X, ALU.add))
                        dve.tensor_scalar(norm[:], norm[:], 1e-12, None, ALU.add).then_inc(sq, 1)
                    if n == 2:
                        dve.wait_ge(e_done, i * 2 + 1)
                        link(dve.tensor_scalar(gates[:, 0], gates[:, 0], 1.0, None, ALU.add))
                        dve.reciprocal(gates[:, 0], gates[:, 0]).then_inc(sig, 1)
                    if n == 3:
                        dve.wait_ge(e_done, i * 2 + 2)
                        link(dve.tensor_scalar(gates[:, 1], gates[:, 1], 1.0, None, ALU.add))
                        link(dve.reciprocal(gates[:, 1], gates[:, 1]))
                    if n == 4:
                        link(dve.scalar_tensor_tensor(tmp[:], gates[:, 1], -1.0, rows[:, 1], ALU.add, ALU.mult))
                        link(dve.scalar_tensor_tensor(kdir[:], tmp[:], 1.0, rkv[:, 1], ALU.add, ALU.mult))
                        link(dve.tensor_tensor(tmp[:], rkv[:, 0], rows[:, 2], ALU.mult))
                        link(dve.tensor_tensor(tmp2[:], tmp[:], kdir[:], ALU.mult))
                    if n == 5:
                        dve.wait_ge(b_free, i + 1)
                        link(dve.tensor_reduce(bonus[:], heads(tmp2[:], 64), AX.X, ALU.add))
                        dve.sem_inc(b_rd, 1)
                        dve.wait_ge(root, i + 1)
                        link(dve.reciprocal(norm[:], norm[:]))
                        link(dve.tensor_tensor(heads(kk[:], 64), heads(kk[:], 64), per_head(norm[:], 64), ALU.mult))
                        link(dve.tensor_tensor(tmp[:], kk[:], gates[:, 1], ALU.mult))
                    if n == 6:
                        dve.wait_ge(dec_ready, i * 3 + 3)
                        dve.tensor_tensor(alpha[:], kk[:], dec[:, 2], ALU.mult).then_inc(ops, 1)
                        dve.tensor_tensor(rho[:], rkv[:, 0], dec[:, 0], ALU.mult).then_inc(ops, 1)
                        dve.wait_ge(ops, i * 4 + 2)
                        dve.sem_inc(prep_done, 1)
                        link.end()

                def beta_kappa():
                    dve.tensor_tensor(beta[:], tmp[:], dec[:, 1], ALU.mult).then_inc(ops, 1)
                    dve.tensor_tensor(kappa[:], kdir[:], dec[:, 1], ALU.mult).then_inc(ops, 1)

                def turn(i, d, following):
                    link = Chain(dve, vec, 6, 1)
                    link.turn(i)
                    for e in range(2):
                        for x in (inv.X, inv.XT):
                            link(dve.tensor_copy(x[:, e], cf[:, CONST["ident"]].unsqueeze(1).broadcast_to([P, 4, P])))
                        dve.sem_inc(inv.x_done[e], 1)
                    dve.wait_ge(ops, i * 4 + 4)
                    dve.wait_ge(ec_ready, i + 1)
                    dve.tensor_tensor(Hp[:], H[:], per_head(ec[:], P), ALU.mult).then_inc(hp, 1)
                    for kind, dst, mask in ((0, BP, f"mask_b{d}"), (1, KP, f"mask_k{d}")):
                        for q in (0, 2):
                            for e in range(2):
                                b = bank[(1 + 2 * kind + 4 * e + q // 2) % 8]
                                dve.wait_ge(prod, i * 8 + (4 * kind + q + e + 1))
                                dve.tensor_tensor(dst[:, e, q:q + 2].rearrange("p q a t -> p q (a t)"),
                                                  heads(b[:], 256),
                                                  cf[:, CONST[mask]].unsqueeze(1).broadcast_to([P, 2, 256]),
                                                  ALU.mult).then_inc(prod_ev, 1)
                    inv.vector(dve, i, levels, lambda e: d, lambda n: following and prepare(following[0], n))
                    dve.wait_ge(h_mm, i + 1)
                    if following:
                        beta_kappa()
                    link(dve.tensor_tensor(H[:], heads(bank[0][:], P),
                                           cf[:, CONST["diag2"]].unsqueeze(1).broadcast_to([P, 4, P]), ALU.mult))
                    dve.wait_ge(hp, i + 1)
                    link(dve.tensor_tensor(H[:], H[:], Hp[:], ALU.add))
                    dve.tensor_tensor(H[:], H[:], per_head(ec[:], P), ALU.mult).then_inc(h_done, 1)
                    dve.wait_ge(h_done, i + 2)
                    dve.wait_ge(y_ev, i + 1)
                    dve.sem_inc(done, 1)
                    link.end()

                def clear_state(run):
                    dve.memset(H[:], 0.0).then_inc(reset, 1)
                    dve.wait_ge(reset, run + 1)

                for n in range(LEVELS):
                    prepare(0, n)
                beta_kappa()
                run_turns(dve, turn, clear_state)


def deltanet_mixer(nc, a):
    zt, o_out = a["zt"], a["gd_o"]
    QKV0, AB = RWC * P, AB0 * P
    with Phase(nc, "delta") as ph:
        cf = ph.sb("consts", [P, CONST_W])
        levels = ph.sb("levels", [P, 2, LEVELS, P], I32)
        dt = ph.sb("dt", [P, 8])
        neg_a = ph.sb("neg_a", [P, 8])
        qkv = ph.sb("qkv", [P, 2, 3, GD_W])
        ab = ph.sb("ab", [P, 2, 16])
        sqr = ph.sb("sqr", [P, 2, 8, P])
        norm = ph.sb("norm", [P, 16])
        g = ph.sb("g", [P, 8])
        t8 = ph.sb("t8", [P, 3, 8])
        beta = ph.sb("beta", [P, 8])
        gb = ph.sb("gb", [P, 8, P])
        gc = ph.sb("gc", [P, 16])
        eg = ph.sb("eg", [P, 3, 8])
        bg = ph.sb("bg", [P, 8])
        DD = ph.sb("DD", [P, 2, 4, 2, P])
        kb = ph.sb("kb", [P, 2, GD_W])
        kd = ph.sb("kd", [P, 2, GD_W])
        kT = ph.sb("kT", [P, 2, 4, P])
        kqT = ph.sb("kqT", [P, 2, 4, 2, P])
        BP = ph.sb("BP", [P, 2, 4, 2, P])
        S = ph.sb("S", [P, 2, 4, P])
        vb = ph.sb("vb", [P, 2, GD_W])
        W = ph.sb("W", [P, 2, GD_W])
        qs = ph.sb("qs", [P, 2, GD_W])
        o = ph.sb("o", [P, 2, GD_W])
        bank = ph.banks(8)
        inv = Inverse(ph, lambda e: BP[:, e, :, 0, :], (bank[0], bank[2]), (bank[1], bank[3]))
        cst, q_l, vec, vec_p, reset, go = (ph.sem(n) for n in ("cst", "inputs_loaded", "vec", "vec_prepare", "reset", "go"))
        (sq, root, e1, ln, ln_in, g_r, gsum, g_ev, grow, dd_in, dd_e, kb_r, tr, tr_ev, prod, prod_ev, ks, x_r, w_mm, w_ev, o_mm,
         o_r, done, free, st, eb, ex) = (
            ph.sem(n) for n in ("squares", "root", "exp_abs", "softplus_ln", "ln_in", "g_ready", "g_summed", "g_exps", "g_rows",
                                "diff", "diff_exp", "operands", "turned", "turned_ev", "products", "products_ev", "state_mm",
                                "x_ready", "w_mm", "w_ev", "out_mm", "out_ready", "turn_done", "inputs_free", "stored",
                                "exp_b", "exp_in"))

        def run_turns(eng, turn, start=lambda run: None):
            for n, (first, last, shift, total) in enumerate(mixer_runs()):
                start(n)
                with eng.Fori(first, last - 1) as i:
                    turn(i, total, i + 1)
                turn(last - 1, total, last if last < TILES else None)

        with nc.Block() as block:

            @block.sync
            def _(sp):
                sp.dma_start(cf[:], a["const_f"]).then_inc(cst, 16)
                sp.dma_start(levels[:].rearrange("p d n t -> p (d n t)"), a["const_levels"]).then_inc(cst, 16)
                sp.dma_start(dt[:], a["gd_dt_bias"].rearrange("a d h -> a (d h)").broadcast_to([P, 8])).then_inc(cst, 16)
                sp.dma_start(neg_a[:], a["gd_A_log"].rearrange("a d h -> a (d h)").broadcast_to([P, 8])).then_inc(cst, 16)
                for first, last, shift, total in mixer_runs():
                    with sp.Fori(first, last) as i:
                        at = sp.snap(i + 1)
                        row = (sp.snap(i * P), sp.snap(i * -P + total * P))
                        sp.wait_ge(free, at)
                        for d in range(2):
                            sp.dma_start(qkv[:, d].rearrange("p a c -> p (a c)"), zt[ds(row[d], P), QKV0:QKV0 + 3 * GD_W]).then_inc(q_l, 16)
                            sp.dma_start(ab[:, d], zt[ds(row[d], P), AB:AB + 16]).then_inc(q_l, 16)

            @block.tensor
            def _(pe):
                pe.wait_ge(cst, 64)
                ident = cf[:, CONST["ident"]]
                for first, last, shift, total in mixer_runs():
                    with pe.Fori(first, last) as i:
                        pe.wait_ge(done, i + 1)
                        pe.wait_ge(g_r, i * 2 + 1)
                        for d in range(2):
                            pe.matmul(bank[0][:, 4 * d:4 * d + 4], cf[:, CONST[f"incl{d}"]], g[:, 4 * d:4 * d + 4],
                                      start=True, stop=True)
                        pe.matmul(bank[0][:, 8:16], cf[:, CONST["ones"]], g[:], start=True, stop=True).then_inc(gsum, 1)
                        pe.wait_ge(g_r, i * 2 + 2)
                        for d in range(2):
                            for h in range(4):
                                mm = pe.matmul(bank[1 + d][:, h * P:(h + 1) * P], gb[:, 4 * d + h, :], cf[:, CONST[f"incl{d}"]],
                                               start=True, stop=True)
                            mm.then_inc(grow, 1)
                        pe.wait_ge(kb_r, i + 1)
                        for n in range(6):
                            d, part = n % 2, n // 2
                            src = (qkv[:, d, 1], kb[:, d], qkv[:, d, 0])[part]
                            b = (3, 4, 5, 6, 7, 3)[n]
                            if n == 5:
                                pe.wait_ge(tr_ev, i * 6 + 1)
                            for h in range(4):
                                mm = pe.transpose(bank[b][:, h * P:(h + 1) * P], src[:, h * P:(h + 1) * P], ident)
                            mm.then_inc(tr, 1)
                        pe.wait_ge(tr_ev, i * 6 + 6)
                        pe.wait_ge(dd_e, i * 2 + 2)
                        for d in range(2):
                            for h in range(4):
                                mm = pe.matmul(bank[2 * d + h // 2][:, (h % 2) * 256:(h % 2 + 1) * 256], kT[:, d, h, :],
                                               kqT[:, d, h].rearrange("p a t -> p (a t)"), start=True, stop=True)
                                if h % 2:
                                    mm.then_inc(prod, 1)
                        for d in range(2):
                            for part, src in ((0, kT[:, d]), (1, kqT[:, d, :, 1, :])):
                                for h in range(4):
                                    mm = pe.matmul(bank[4 + 2 * d + part][:, h * P:(h + 1) * P], src[:, h, :], S[:, d, h, :],
                                                   start=True, stop=True)
                                mm.then_inc(ks, 1)
                        pe.wait_ge(prod_ev, i * 4 + 4)
                        inv.tensor(pe, i)
                        pe.wait_ge(x_r, i * 2 + 2)
                        for d in range(2):
                            pe.wait_ge(inv.x_done[d], i * inv.X_TURN + inv.X_TURN)
                            for h in range(4):
                                mm = pe.matmul(bank[4 + 2 * d][:, h * P:(h + 1) * P], inv.XT[:, d, h, :], vb[:, d, h * P:(h + 1) * P],
                                               start=True, stop=True)
                            mm.then_inc(w_mm, 1)
                        for d in range(2):
                            pe.wait_ge(w_ev, i * 2 + (d + 1))
                            for h in range(4):
                                mm = pe.matmul(bank[5 + 2 * d][:, h * P:(h + 1) * P], BP[:, d, h, 1, :], W[:, d, h * P:(h + 1) * P],
                                               start=True, stop=True)
                            mm.then_inc(o_mm, 1)
                            for h in range(4):
                                mm = pe.matmul(bank[4 + 2 * d][:, h * P:(h + 1) * P], kd[:, d, h * P:(h + 1) * P], W[:, d, h * P:(h + 1) * P],
                                               start=True, stop=True)
                            mm.then_inc(o_mm, 1)

            @block.scalar
            def _(act):
                act.wait_ge(cst, 64)
                act.activation(neg_a[:], neg_a[:], ACT.Exp).then_inc(reset, 1)
                act.sem_inc(st, 32)
                act.wait_ge(inv.cleared, 1)

                def prepare(i, n):
                    if n == 2:
                        act.wait_ge(sq, i + 1)
                        act.activation(norm[:], norm[:], ACT.Sqrt).then_inc(root, 1)
                    if n == 3:
                        act.wait_ge(ex, i + 1)
                        act.activation(t8[:, 1], t8[:, 1], ACT.Exp, scale=-1.0).then_inc(e1, 1)
                        act.activation(beta[:].rearrange("p (d h) -> p d h", d=2), t8[:, 2].rearrange("p (d h) -> p d h", d=2),
                                       ACT.Exp, scale=-1.0).then_inc(eb, 1)
                    if n == 4:
                        act.wait_ge(ln_in, i + 1)
                        act.activation(t8[:, 1], t8[:, 1], ACT.Ln).then_inc(ln, 1)

                def turn(i, total, following):
                    act.wait_ge(gsum, i + 1)
                    act.activation(gc[:], bank[0][:, 0:16], ACT.Copy).then_inc(g_ev, 1)
                    act.wait_ge(g_ev, i * 4 + 1)
                    act.activation(eg[:, 0:2].rearrange("p a h -> p (a h)"), gc[:], ACT.Exp).then_inc(g_ev, 1)
                    act.wait_ge(go, i + 1)
                    act.activation(eg[:, 2], t8[:, 0], ACT.Exp).then_inc(g_ev, 1)
                    act.sem_inc(g_ev, 1)
                    for d in range(2):
                        act.wait_ge(dd_in, i * 2 + (d + 1))
                        act.activation(DD[:, d, :, 1, :], DD[:, d, :, 1, :], ACT.Exp).then_inc(dd_e, 1)
                    for n in range(6):
                        d, part = n % 2, n // 2
                        b = (3, 4, 5, 6, 7, 3)[n]
                        dst = (kT[:, d], kqT[:, d, :, 0, :], kqT[:, d, :, 1, :])[part]
                        act.wait_ge(tr, i * 6 + (n + 1))
                        act.activation(dst, heads(bank[b][:], P), ACT.Copy).then_inc(tr_ev, 1)
                    inv.scalar(act, i, lambda e: e, lambda n: following is not None and prepare(following, n))
                    for d in range(2):
                        act.wait_ge(w_mm, i * 2 + (d + 1))
                        act.activation(W[:, d], bank[4 + 2 * d][:], ACT.Copy).then_inc(w_ev, 1)
                    for d in range(2):
                        row = i * P if d == 0 else i * -P + total * P
                        row = row if isinstance(i, int) else act.snap(row)
                        act.wait_ge(o_r, i * 2 + (d + 1))
                        act.dma_start(o_out[d, ds(row, P), :], o[:, d]).then_inc(st, 16)

                for n in range(LEVELS):
                    prepare(0, n)
                run_turns(act, turn)
                act.wait_ge(st, 32 * (TILES + 1))

            @block.vector
            def _(dve):
                dve.memset(inv.Y[:], 0.0).then_inc(inv.cleared, 1)
                dve.wait_ge(cst, 64)
                dve.wait_ge(reset, 1)
                dve.tensor_scalar(neg_a[:], neg_a[:], -1.0, None, ALU.mult).then_inc(vec, 1)
                dve.wait_ge(vec, 1)
                dve.sem_inc(done, 1)
                dve.sem_inc(free, 1)
                prep = Chain(dve, vec_p, 17)

                def prepare(i, n):
                    link = prep
                    if n == 1:
                        link.turn(i)
                        dve.wait_ge(q_l, i * 64 + 64)
                        for d in range(2):
                            x = qkv[:, d, 0:2].rearrange("p a (h n) -> p (a h) n", n=P)
                            link(dve.tensor_tensor(sqr[:, d], x, x, ALU.mult))
                        link(dve.tensor_reduce(norm[:], sqr[:].rearrange("p d h n -> p (d h) n"), AX.X, ALU.add))
                        dve.tensor_scalar(norm[:], norm[:], 1e-12, None, ALU.add).then_inc(sq, 1)
                    if n == 2:
                        by_d = lambda t: t.rearrange("p (d h) -> p d h", d=2)
                        for d in range(2):
                            link(dve.tensor_tensor(t8[:, 0, 4 * d:4 * d + 4], ab[:, d, 4 * d:4 * d + 4], dt[:, 4 * d:4 * d + 4], ALU.add))
                            link(dve.tensor_copy(t8[:, 2, 4 * d:4 * d + 4], ab[:, d, 8 + 4 * d:12 + 4 * d]))
                        link(dve.tensor_scalar(t8[:, 1], t8[:, 0], -1.0, None, ALU.mult))
                        dve.tensor_tensor(t8[:, 1], t8[:, 1], t8[:, 0], ALU.max).then_inc(ex, 1)
                    if n == 3:
                        dve.wait_ge(e1, i + 1)
                        dve.tensor_scalar(t8[:, 1], t8[:, 1], 1.0, None, ALU.add).then_inc(ln_in, 1)
                        dve.wait_ge(eb, i + 1)
                        link(dve.tensor_scalar(beta[:], beta[:], 1.0, None, ALU.add))
                        link(dve.reciprocal(beta[:], beta[:]))
                    if n == 4:
                        dve.wait_ge(ln, i + 1)
                        link(dve.scalar_tensor_tensor(t8[:, 0], t8[:, 0], 0.0, t8[:, 1], ALU.max, ALU.add))
                        dve.tensor_tensor(g[:], t8[:, 0], neg_a[:], ALU.mult).then_inc(g_r, 1)
                        dve.wait_ge(g_r, i * 2 + 1)
                        dve.tensor_copy(gb[:], per_head(g[:], P)).then_inc(g_r, 1)
                    if n == 5:
                        dve.wait_ge(root, i + 1)
                        link(dve.reciprocal(norm[:], norm[:]))
                        n4 = norm[:].rearrange("p (d a h) -> p d a h", d=2, a=2)
                        for d in range(2):
                            link(dve.scalar_tensor_tensor(heads(qkv[:, d, 0], P), heads(qkv[:, d, 0], P), GD_N ** -0.5,
                                                          per_head(n4[:, d, 0], P), ALU.mult, ALU.mult))
                            link(dve.tensor_tensor(heads(qkv[:, d, 1], P), heads(qkv[:, d, 1], P), per_head(n4[:, d, 1], P), ALU.mult))
                    if n == 6:
                        for d in range(2):
                            ins = dve.tensor_tensor(heads(kb[:, d], P), heads(qkv[:, d, 1], P), per_head(beta[:, 4 * d:4 * d + 4], P), ALU.mult)
                            if d == 0:
                                link(ins)
                            else:
                                ins.then_inc(kb_r, 1)
                        link.end()

                def turn(i, total, following):
                    link = Chain(dve, vec, 19, 1)
                    link.turn(i)
                    dve.wait_ge(g_ev, i * 4 + 2)
                    dve.tensor_tensor(t8[:, 0], gc[:, 8:16], gc[:, 0:8], ALU.subtract).then_inc(go, 1)
                    link(dve.tensor_tensor(bg[:], beta[:], eg[:, 0], ALU.mult))
                    for d in range(2):
                        dve.wait_ge(grow, i * 2 + (d + 1))
                        for h in range(4):
                            ins = dve.scalar_tensor_tensor(DD[:, d, h, 1, :], bank[1 + d][:, h * P:(h + 1) * P],
                                                           gc[:, 4 * d + h:4 * d + h + 1], cf[:, CONST[f"floor{d}"]],
                                                           ALU.subtract, ALU.add)
                            if h == 3:
                                ins.then_inc(dd_in, 1)
                    dve.wait_ge(g_ev, i * 4 + 4)
                    for d in range(2):
                        link(dve.tensor_tensor(heads(kd[:, d], P), heads(qkv[:, d, 1], P), per_head(eg[:, 2, 4 * d:4 * d + 4], P), ALU.mult))
                        link(dve.tensor_tensor(heads(vb[:, d], P), heads(qkv[:, d, 2], P), per_head(beta[:, 4 * d:4 * d + 4], P), ALU.mult))
                        dve.wait_ge(dd_e, i * 2 + (d + 1))
                        link(dve.tensor_tensor(DD[:, d, :, 0, :], DD[:, d, :, 1, :],
                                               cf[:, CONST[f"mask_b{d}"]][:, 0:P].unsqueeze(1).broadcast_to([P, 4, P]), ALU.mult))
                    dve.wait_ge(tr, i * 6 + 6)
                    dve.sem_inc(free, 1)
                    for e in range(2):
                        for x in (inv.X, inv.XT):
                            link(dve.tensor_copy(x[:, e], cf[:, CONST["ident"]].unsqueeze(1).broadcast_to([P, 4, P])))
                        dve.sem_inc(inv.x_done[e], 1)
                    for d in range(2):
                        for n in range(2):
                            dve.wait_ge(prod, i * 4 + (2 * d + n + 1))
                            dve.tensor_tensor(BP[:, d, 2 * n:2 * n + 2].rearrange("p h a t -> p (h a t)"), bank[2 * d + n][:],
                                              DD[:, d, 2 * n:2 * n + 2].rearrange("p h a t -> p (h a t)"), ALU.mult).then_inc(prod_ev, 1)
                    for d in range(2):
                        dve.wait_ge(ks, i * 4 + (2 * d + 2))
                        link(dve.tensor_tensor(sqr[:, d, 0:4], heads(bank[4 + 2 * d][:], P), per_head(bg[:, 4 * d:4 * d + 4], P), ALU.mult))
                        dve.tensor_tensor(vb[:, d], vb[:, d], sqr[:, d, 0:4].rearrange("p h n -> p (h n)"), ALU.subtract).then_inc(x_r, 1)
                        link(dve.tensor_tensor(heads(qs[:, d], P), heads(bank[5 + 2 * d][:], P), per_head(eg[:, 0, 4 * d:4 * d + 4], P), ALU.mult))
                    inv.vector(dve, i, levels, lambda e: e, lambda n: following is not None and prepare(following, n))
                    dve.wait_ge(st, i * 32 + 32)
                    for d in range(2):
                        link(dve.tensor_tensor(S[:, d], S[:, d], per_head(eg[:, 1, 4 * d:4 * d + 4], P), ALU.mult))
                        dve.wait_ge(o_mm, i * 4 + (2 * d + 2))
                        dve.tensor_tensor(o[:, d], bank[5 + 2 * d][:], qs[:, d], ALU.add).then_inc(o_r, 1)
                        link(dve.tensor_tensor(S[:, d].rearrange("p h n -> p (h n)"), S[:, d].rearrange("p h n -> p (h n)"),
                                               bank[4 + 2 * d][:], ALU.add))
                    dve.sem_inc(done, 1)
                    link.end()

                def clear_state(run):
                    dve.memset(S[:], 0.0).then_inc(reset, 1)
                    dve.wait_ge(reset, run + 2)

                for n in range(LEVELS):
                    prepare(0, n)
                run_turns(dve, turn, clear_state)




def mod_row(a, m, q, part):
    return a["mod"][m, q:q + 1, part * D:(part + 1) * D].broadcast_to([P, D])


def normed(dve, link, step, x, out, stats, mv, var_ready, root, n_ready, g_row, b_row):
    for c in range(2):
        link(dve.bn_stats(stats[:, c], x[:, c * 512:(c + 1) * 512]))
    dve.sem_inc(step, 1)
    link(dve.bn_aggr(mv[:, 0:2], stats[:].rearrange("p a b -> p (a b)")))
    dve.tensor_scalar(mv[:, 2:3], mv[:, 1:2], LN_EPS, None, ALU.add).then_inc(var_ready, 1)
    dve.wait_ge(root, n_ready)
    link(dve.reciprocal(mv[:, 2:3], mv[:, 2:3]))
    link(dve.tensor_scalar(x[:], x[:], mv[:, 0:1], mv[:, 2:3], ALU.subtract, ALU.mult))
    link(dve.tensor_tensor(x[:], x[:], g_row, ALU.mult))
    link(dve.tensor_tensor(out[:], x[:], b_row, ALU.add))


def close_mixer(nc, a, layer):
    x_in, x_out, h_out = a["x_in" if layer == 0 else "x_mid2"], a["x_mid"], a["h_rows"]
    w_dram = (a["ab_w_out"] if layer == 0 else a["at_w_out"])[0]
    m = 2 * layer
    with Phase(nc, f"close{layer}") as ph:
        cf = ph.sb("consts", [P, CONST["incl0"].start])
        tok = ph.sb("tok", [P, TILES], I32)
        zero = ph.sb("zero", [P, BLOCKS], I32)
        w_out = ph.sb("w_out", [P, KC, D])
        rows = ph.sb("rows", [P, 2, 5, D])
        x = ph.sb("x", [P, 2, D])
        cat = ph.sb("cat", [P, 2, D])
        catT = ph.sb("catT", [P, KC, P])
        x1 = ph.sb("x1", [P, D])
        x2 = ph.sb("x2", [P, D])
        h = ph.sb("h", [P, D])
        hT = ph.sb("hT", [P, KC, P])
        stats = ph.sb("stats", [P, 2, 6])
        mv = ph.sb("mv", [P, 3])
        rw = ph.sb("rw", [P, KC, E])
        rb = ph.sb("rb", [P, E])
        sc = ph.sb("sc", [P, 2, E])
        r8 = ph.sb("r8", [P, 8, 8])
        r32 = ph.sb("r32", [P, 2, E])
        r4 = ph.sb("r4", [P, 8, PER])
        r1 = ph.sb("r1", [P, 4])
        one = ph.sb("one", [P, 2, TILES + 1, E])
        gate = ph.sb("gate", [P, 2, TILES])
        gsum = ph.sb("gsum", [P, TILES])
        upto = ph.sb("upto", [P, TILES + 1, E])
        place = ph.sb("place", [P, TILES + 1, E])
        nb = ph.sb("nb", [P, 4, E])
        cmp = ph.sb("cmp", [P, BLOCKS, E])
        dest = ph.sb("dest", [P, 2, TILES])
        dest_i = ph.sb("dest_i", [P, 2, TILES], I32)
        blk = ph.sb("blk", [P, 2, BLOCKS])
        blk_i = ph.sb("blk_i", [P, BLOCKS], I32)
        if layer == 0:
            yo = ph.sb("yo", [P, 2, 2, RW_W])
            bon = ph.sb("bon", [P, 2, RW_H])
            v = ph.sb("v", [P, RW_W])
            og = ph.sb("og", [P, GD_W])
            glow = ph.sb("glow", [P, P])
            gup = ph.sb("gup", [P, RW_W])
            gn = ph.sb("gn", [P, 2, RW_W])
            ng = ph.sb("ng", [P, GD_N])
            sq_t = ph.sb("sq_t", [P, RW_W])
            hs = ph.sb("hs", [P, 4, RW_H])
        bank = ph.banks(8)
        cst, rows_l, heads_l, heads_free, x_free, vec, vec_a, vec_c, vec_r, own, step = (
            ph.sem(n) for n in ("cst", "rows_loaded", "heads_loaded", "heads_free", "x_free", "vec", "vec_join",
                                "vec_norm", "vec_route", "own", "step"))
        x_l = [ph.sem(f"x_loaded{j}") for j in range(2)]
        gate_mm, hv, hroot, cat_r, cat_tr, cat_ev, out_mm, var_r, root, x1_r, h_r, x_st, h_st, h_tr, h_ev, lg, sg = (
            ph.sem(n) for n in ("gate_mm", "head_vars", "head_roots", "cat_ready", "cat_turned", "cat_ev", "out_mm", "var_ready",
                                "root", "x1_ready", "h_ready", "x_stored", "h_stored", "h_turned", "h_ev", "logits",
                                "exp_logits"))
        pos_in, pos_mm, dest_r, tab, tab_z = (ph.sem(n) for n in ("one_hots_ready", "pos_mm", "dest_ready", "tables_stored", "table_zeroed"))
        scat = ph.sem("scattered")
        XW = 16 if layer == 0 else 32
        NCST = 9 if layer == 0 else 5

        with nc.Block() as block:

            @block.sync
            def _(sp):
                sp.dma_start(cf[:], a["const_f"][:, 0:CONST["incl0"].start]).then_inc(cst, 16)
                sp.dma_start(tok[:], a["const_tok"]).then_inc(cst, 16)
                sp.dma_start(w_out[:], w_dram.rearrange("(k p) n -> p k n", p=P)).then_inc(cst, 16)
                sp.dma_start(rw[:], a["router_w"].rearrange("(k p) n -> p k n", p=P)).then_inc(cst, 16)
                sp.dma_start(rb[:], a["router_bias"].rearrange("(a n) -> a n", a=1).broadcast_to([P, E])).then_inc(cst, 16)
                if layer == 0:
                    sp.dma_start(gup[:], a["rw_g_up"][0]).then_inc(cst, 16)
                    sp.dma_start(gn[:, 0], a["rw_gn_g"].broadcast_to([P, RW_W])).then_inc(cst, 16)
                    sp.dma_start(gn[:, 1], a["rw_gn_b"].broadcast_to([P, RW_W])).then_inc(cst, 16)
                    sp.dma_start(ng[:], a["gd_norm_g"].broadcast_to([P, GD_N])).then_inc(cst, 16)
                sp.wait_ge(tab_z, 1)
                sp.dma_start(a["row_tok"].rearrange("(b p) o -> p (b o)", p=P), zero[:],
                             allow_slow_non_contiguous=True).then_inc(tab, 16)
                def load_rows(q):
                    for n, src in enumerate((mod_row(a, m, q, 2), mod_row(a, m + 1, q, 1), mod_row(a, m + 1, q, 0),
                                             a["ln_g"][layer, 0:1].broadcast_to([P, D]),
                                             a["ln_b"][layer, 0:1].broadcast_to([P, D]))):
                        sp.dma_start(rows[:, q, n], src).then_inc(rows_l, 16)

                def load(i, j):
                    dyn = not isinstance(i, int)
                    at, at2, row = (sp.snap(i + 1), sp.snap(i + 1), sp.snap(i * P)) if dyn else (i + 1, i + 1, i * P)
                    if layer == 0:
                        sp.wait_ge(heads_free, at)
                        sp.dma_start(yo[:, 0], a["rw_y"][:, ds(row, P), :].rearrange("d p c -> p d c")).then_inc(heads_l, 16)
                        sp.dma_start(yo[:, 1], a["gd_o"][:, ds(row, P), :].rearrange("d p c -> p d c")).then_inc(heads_l, 16)
                        sp.dma_start(bon[:], a["rw_bonus"][:, ds(row, P), :].rearrange("d p c -> p d c"),
                                     allow_slow_non_contiguous=True).then_inc(heads_l, 16)
                        sp.dma_start(v[:], a["zt"][ds(row, P), 2 * RW_W:3 * RW_W]).then_inc(heads_l, 16)
                        sp.dma_start(og[:], a["zt"][ds(row, P), GATE0 * P:LOW0 * P]).then_inc(heads_l, 16)
                        sp.dma_start(glow[:], a["zf"][2 * P:3 * P, ds(row, P)]).then_inc(heads_l, 16)
                    sp.wait_ge(x_free, at2)
                    sp.dma_start(x[:, j], x_in[ds(row, P), :]).then_inc(x_l[j], 16)
                    if layer == 1:
                        sp.dma_start(cat[:, j], a["at_o"][ds(row, P), :]).then_inc(x_l[j], 16)

                load_rows(0)
                with sp.Fori(0, TP // 2) as p:
                    for j in range(2):
                        load(2 * p + j, j)
                load_rows(1)
                for i in range(TP, TILES):
                    load(i, i % 2)

            @block.tensor
            def _(pe):
                pe.wait_ge(cst, 16 * NCST)
                ident = cf[:, CONST["ident"]]

                def gate_product(i):
                    if layer == 0:
                        pe.wait_ge(heads_l, i * 96 + 96)
                        pe.matmul(bank[7][:], glow[:], gup[:], start=True, stop=True).then_inc(gate_mm, 1)

                def project(i, j, p):
                    pe.wait_ge(cat_r, i + 1) if layer == 0 else pe.wait_ge(x_l[j], XW * p + XW)
                    pe.wait_ge(cat_ev, 2 * i + 2)
                    for k in range(KC):
                        mm = pe.transpose(bank[k // 4][:, (k % 4) * P:(k % 4 + 1) * P], cat[:, j, k * P:(k + 1) * P], ident)
                        if k % 4 == 3:
                            mm.then_inc(cat_tr, 1)
                    pe.wait_ge(cat_ev, 2 * i + 4)
                    pe.wait_ge(x_free, i + 2)
                    for c in range(2):
                        for k in range(KC):
                            mm = pe.matmul(bank[2 + c][:], catT[:, k, :], w_out[:, k, c * 512:(c + 1) * 512],
                                           start=k == 0, stop=k == KC - 1)
                        mm.then_inc(out_mm, 1)

                def router(i):
                    pe.wait_ge(h_r, i + 1)
                    for k in range(KC):
                        mm = pe.transpose(bank[4 + k // 4][:, (k % 4) * P:(k % 4 + 1) * P], h[:, k * P:(k + 1) * P], ident)
                        if k % 4 == 3:
                            mm.then_inc(h_tr, 1)
                    pe.wait_ge(h_ev, i * 2 + 2)
                    for k in range(KC):
                        mm = pe.matmul(bank[6][:, 0:E], hT[:, k, :], rw[:, k, :], start=k == 0, stop=k == KC - 1)
                    mm.then_inc(lg, 1)

                gate_product(0)
                project(0, 0, 0)
                gate_product(1)
                with pe.Fori(0, TP // 2) as p:
                    for j in range(2):
                        gate_product(2 * p + (j + 2))
                        project(2 * p + (j + 1), 1 - j, p + j)
                        router(2 * p + j)
                project(TP + 1, 1, TP // 2)
                router(TP)
                router(TP + 1)
                pe.wait_ge(pos_in, 1)
                pe.matmul(bank[0][:, 0:TILES * E], cf[:, CONST["before"]],
                          one[:, 0, 0:TILES].rearrange("p t e -> p (t e)"), start=True, stop=False, skip_group_check=True)
                pe.matmul(bank[0][:, 0:TILES * E], cf[:, CONST["before"]],
                          one[:, 1, 0:TILES].rearrange("p t e -> p (t e)"), start=False, stop=False, skip_group_check=True)
                pe.matmul(bank[0][:, 0:(TILES + 1) * E], cf[:, CONST["ones"]], upto[:].rearrange("p t e -> p (t e)"),
                          start=False, stop=True, skip_group_check=True).then_inc(pos_mm, 1)

            @block.scalar
            def _(act):
                act.sem_inc(x_st, 16)
                act.sem_inc(h_st, 16)
                act.sem_inc(cat_ev, 2)

                def head_roots(i):
                    if layer == 0:
                        act.wait_ge(hv, i + 1)
                        act.activation(hs[:, 0:2], hs[:, 0:2], ACT.Sqrt).then_inc(hroot, 1)

                def copy_cat(i):
                    for c in range(2):
                        act.wait_ge(cat_tr, 2 * i + (c + 1))
                        act.activation(catT[:, 4 * c:4 * c + 4].rearrange("p k t -> p (k t)"), bank[c][:], ACT.Copy).then_inc(cat_ev, 1)

                def close(i):
                    row = i * P if isinstance(i, int) else act.snap(i * P)
                    act.wait_ge(var_r, i + 1)
                    act.activation(mv[:, 2:3], mv[:, 2:3], ACT.Sqrt).then_inc(root, 1)
                    act.wait_ge(x1_r, i + 1)
                    act.dma_start(x_out[ds(row, P), :], x1[:]).then_inc(x_st, 16)
                    act.wait_ge(h_r, i + 1)
                    act.dma_start(h_out[ds(row, P), :], h[:]).then_inc(h_st, 16)

                def logits(i):
                    for c in range(2):
                        act.wait_ge(h_tr, 2 * i + (c + 1))
                        act.activation(hT[:, 4 * c:4 * c + 4].rearrange("p k t -> p (k t)"), bank[4 + c][:], ACT.Copy).then_inc(h_ev, 1)
                    act.wait_ge(lg, i + 1)
                    act.activation(sc[:, 0], bank[6][:, 0:E], ACT.Exp, scale=-1.0).then_inc(sg, 1)

                head_roots(0)
                copy_cat(0)
                head_roots(1)
                with act.Fori(0, TP // 2) as p:
                    for j in range(2):
                        copy_cat(2 * p + (j + 1))
                        close(2 * p + j)
                        head_roots(2 * p + (j + 2))
                        logits(2 * p + j)
                copy_cat(TP + 1)
                close(TP)
                logits(TP)
                close(TP + 1)
                logits(TP + 1)
                act.wait_ge(x_st, 16 * (TILES + 1))
                act.wait_ge(h_st, 16 * (TILES + 1))

            @block.vector
            def _(dve):
                dve.memset(zero[:], 0).then_inc(tab_z, 1)
                dve.wait_ge(cst, 16 * NCST)
                dve.sem_inc(heads_free, 1)
                dve.sem_inc(x_free, 2)
                rank = cf[:, CONST["rank"]]

                def join(i, j):
                    if layer == 1:
                        return
                    link = Chain(dve, vec_a, 21)
                    link.turn(i)
                    dve.wait_ge(heads_l, i * 96 + 96)
                    ys, os_ = yo[:, 0, 0], yo[:, 1, 0]
                    link(dve.tensor_tensor(ys, ys, yo[:, 0, 1], ALU.add))
                    link(dve.tensor_tensor(os_, os_, yo[:, 1, 1], ALU.add))
                    link(dve.tensor_reduce(hs[:, 2], heads(ys, 64), AX.X, ALU.add))
                    link(dve.tensor_scalar(hs[:, 2], hs[:, 2], 1.0 / RW_N, None, ALU.mult))
                    link(dve.tensor_tensor(heads(ys, 64), heads(ys, 64), per_head(hs[:, 2], 64), ALU.subtract))
                    link(dve.tensor_tensor(sq_t[:], ys, ys, ALU.mult))
                    link(dve.tensor_reduce(hs[:, 0], heads(sq_t[:], 64), AX.X, ALU.add))
                    link(dve.tensor_scalar(hs[:, 0], hs[:, 0], 1.0 / RW_N, RW_GN_EPS, ALU.mult, ALU.add))
                    link(dve.tensor_tensor(sq_t[:], os_, os_, ALU.mult))
                    link(dve.tensor_reduce(hs[:, 1, 0:4], heads(sq_t[:], P), AX.X, ALU.add))
                    link(dve.tensor_copy(hs[:, 1, 4:8], hs[:, 1, 0:4]))
                    dve.tensor_scalar(hs[:, 1], hs[:, 1], 1.0 / GD_N, GD_NORM_EPS, ALU.mult, ALU.add).then_inc(hv, 1)
                    link(dve.tensor_tensor(bon[:, 0], bon[:, 0], bon[:, 1], ALU.add))
                    link(dve.tensor_tensor(heads(v[:], 64), heads(v[:], 64), per_head(bon[:, 0], 64), ALU.mult))
                    dve.wait_ge(hroot, i + 1)
                    link(dve.reciprocal(hs[:, 0:2], hs[:, 0:2]))
                    link(dve.tensor_tensor(heads(ys, 64), heads(ys, 64), per_head(hs[:, 0], 64), ALU.mult))
                    link(dve.tensor_tensor(ys, ys, gn[:, 0], ALU.mult))
                    link(dve.tensor_tensor(ys, ys, gn[:, 1], ALU.add))
                    link(dve.tensor_tensor(ys, ys, v[:], ALU.add))
                    dve.wait_ge(gate_mm, i + 1)
                    link(dve.tensor_tensor(cat[:, j, 0:RW_W], ys, bank[7][:], ALU.mult))
                    link(dve.tensor_tensor(heads(os_, P), heads(os_, P), per_head(hs[:, 1, 0:4], P), ALU.mult))
                    link(dve.tensor_tensor(heads(os_, P), heads(os_, P), ng[:].unsqueeze(1).broadcast_to([P, 4, P]), ALU.mult))
                    dve.tensor_tensor(cat[:, j, RW_W:], os_, og[:], ALU.mult).then_inc(cat_r, 1)
                    dve.wait_ge(cat_r, i + 1)
                    dve.sem_inc(heads_free, 1)
                    link.end()

                def residual(i, j, p, q):
                    link = Chain(dve, vec_c, 11)
                    link.turn(i)
                    dve.wait_ge(x_l[j], XW * p + XW)
                    dve.wait_ge(x_st, i * 16 + 16)
                    for c in range(2):
                        cols = slice(c * 512, (c + 1) * 512)
                        dve.wait_ge(out_mm, 2 * i + (c + 1))
                        link(dve.tensor_tensor(x2[:, cols], bank[2 + c][:], rows[:, q, 0, cols], ALU.mult))
                    link(dve.scalar_tensor_tensor(x2[:], x[:, j], ALPHA, x2[:], ALU.mult, ALU.add))
                    dve.sem_inc(x_free, 1)
                    normed(dve, link, step, x2, x1, stats, mv, var_r, root, i + 1, rows[:, q, 3], rows[:, q, 4])
                    dve.sem_inc(x1_r, 1)
                    link(dve.tensor_tensor(x2[:], x1[:], rows[:, q, 1], ALU.mult))
                    dve.wait_ge(h_st, i * 16 + 16)
                    dve.tensor_tensor(h[:], x2[:], rows[:, q, 2], ALU.add).then_inc(h_r, 1)
                    link.end()

                def route(i):
                    link = Chain(dve, vec_r, 29)
                    link.turn(i)
                    dve.wait_ge(sg, i + 1)
                    link(dve.tensor_scalar(sc[:, 0], sc[:, 0], 1.0, None, ALU.add))
                    link(dve.reciprocal(sc[:, 0], sc[:, 0]))
                    link(dve.tensor_tensor(sc[:, 1], sc[:, 0], rb[:], ALU.add))
                    g4 = sc[:, 1].rearrange("p (g e) -> p g e", e=PER)
                    pairs = [(e1, e2) for e1 in range(PER) for e2 in range(e1 + 1, PER)]
                    for n, (e1, e2) in enumerate(pairs):
                        ins = dve.tensor_tensor(r8[:, n], g4[:, :, e1], g4[:, :, e2], ALU.add)
                    link(ins)
                    link(dve.tensor_reduce(r8[:, 6], r8[:, 0:6].rearrange("p a g -> p g a"), AX.X, ALU.max))
                    link(dve.tensor_reduce(r1[:, 0:1], r8[:, 6], AX.X, ALU.max))
                    link(dve.tensor_scalar(r8[:, 6], r8[:, 6], r1[:, 0:1], None, ALU.is_equal))
                    link(dve.scalar_tensor_tensor(r8[:, 6], rank[:, 0:8], -64.0, r8[:, 6], ALU.add, ALU.mult))
                    link(dve.tensor_reduce(r1[:, 1:2], r8[:, 6], AX.X, ALU.min))
                    link(dve.tensor_scalar(r8[:, 7], r8[:, 6], r1[:, 1:2], None, ALU.is_equal))
                    pick = per_head(r8[:, 7], PER)
                    for n in range(2):
                        ins = dve.tensor_tensor(r32[:, n].rearrange("p (g e) -> p g e", e=PER),
                                                sc[:, n].rearrange("p (g e) -> p g e", e=PER), pick, ALU.mult)
                    link(ins)
                    for n in range(2):
                        ins = dve.tensor_reduce(r4[:, n], r32[:, n].rearrange("p (g e) -> p e g", e=PER), AX.X, ALU.add)
                    link(ins)
                    for c in range(2):
                        link(dve.tensor_reduce(r1[:, 2:3], r4[:, 1], AX.X, ALU.max))
                        link(dve.tensor_scalar(r4[:, 4], r4[:, 1], r1[:, 2:3], None, ALU.is_equal))
                        link(dve.scalar_tensor_tensor(r4[:, 4], rank[:, 0:PER], -64.0, r4[:, 4], ALU.add, ALU.mult))
                        link(dve.tensor_reduce(r1[:, 3:4], r4[:, 4], AX.X, ALU.min))
                        link(dve.tensor_scalar(r4[:, 2 + c], r4[:, 4], r1[:, 3:4], None, ALU.is_equal))
                        if c == 0:
                            link(dve.scalar_tensor_tensor(r4[:, 1], r4[:, 2], NEG, r4[:, 1], ALU.mult, ALU.add))
                        link(dve.tensor_tensor(r4[:, 5 + c], r4[:, 2 + c], r4[:, 0], ALU.mult))
                        link(dve.tensor_reduce(gate[:, c, ds(i, 1)], r4[:, 5 + c], AX.X, ALU.add))
                        link(dve.tensor_tensor(one[:, c, ds(i, 1)].rearrange("p t (g e) -> p (t g) e", e=PER), pick,
                                               r4[:, 2 + c].unsqueeze(1).broadcast_to([P, GROUPS, PER]), ALU.mult))
                    link.end()

                def rows_of(q):
                    dve.wait_ge(rows_l, 80 * (q + 1))
                    dve.tensor_scalar(rows[:, q, 0:2], rows[:, q, 0:2], 1.0, None, ALU.add).then_inc(own, 1)
                    dve.wait_ge(own, q + 1)

                join(0, 0)
                rows_of(0)
                join(1, 1)
                with dve.Fori(0, TP // 2) as p:
                    for j in range(2):
                        residual(2 * p + j, j, p, 0)
                        join(2 * p + (j + 2), j)
                        route(dve.snap(2 * p + j))
                rows_of(1)
                residual(TP, 0, TP // 2, 1)
                route(TP)
                residual(TP + 1, 1, TP // 2, 1)
                route(TP + 1)
                more = Chain(dve, vec)
                more(dve.tensor_tensor(gsum[:], gate[:, 0], gate[:, 1], ALU.add))
                more(dve.reciprocal(gsum[:], gsum[:]))
                for c in range(2):
                    more(dve.tensor_tensor(gate[:, c], gate[:, c], gsum[:], ALU.mult))
                more(dve.memset(upto[:, 0], 0.0))
                for t in range(TILES):
                    more(dve.tensor_tensor(place[:, 0], one[:, 0, t], one[:, 1, t], ALU.add))
                    more(dve.tensor_tensor(upto[:, t + 1], upto[:, t], place[:, 0], ALU.add))
                dve.sem_inc(pos_in, 1)
                dve.wait_ge(pos_mm, 1)
                more(dve.tensor_copy(place[:].rearrange("p t e -> p (t e)"), bank[0][:, 0:(TILES + 1) * E]))
                more(dve.tensor_scalar(nb[:, 0], place[:, TILES], 1.0 / P, None, ALU.mult))
                more(dve.tensor_tensor(cmp[:, 0:MAX_OVER].rearrange("p m e -> p e m"), per_head(nb[:, 0], MAX_OVER),
                                       rank[:, 1:1 + MAX_OVER].unsqueeze(1).broadcast_to([P, E, MAX_OVER]), ALU.is_gt))
                more(dve.tensor_reduce(nb[:, 1], cmp[:, 0:MAX_OVER].rearrange("p m e -> p e m"), AX.X, ALU.add))
                more(dve.tensor_tensor_scan(nb[:, 2], cf[:, CONST["ones"]][:, 0:E], nb[:, 1], 0.0, ALU.mult, ALU.add))
                more(dve.tensor_tensor(nb[:, 3], nb[:, 2], nb[:, 1], ALU.subtract))
                more(dve.tensor_tensor(nb[:, 3], nb[:, 3], rank[:, 0:E], ALU.subtract))
                more(dve.tensor_scalar(nb[:, 3], nb[:, 3], float(E - 1), float(P), ALU.add, ALU.mult))
                more(dve.tensor_scalar(upto[:, 0:TILES], place[:, 0:TILES], float(P), None, ALU.is_ge))
                more(dve.tensor_tensor(upto[:, 0:TILES], upto[:, 0:TILES], nb[:, 3].unsqueeze(1).broadcast_to([P, TILES, E]), ALU.mult))
                more(dve.tensor_tensor(place[:, 0:TILES], place[:, 0:TILES], upto[:, 0:TILES], ALU.add))
                more(dve.tensor_scalar(nb[:, 0], rank[:, 0:E], float(P), None, ALU.mult))
                more(dve.tensor_tensor(place[:, 0:TILES], place[:, 0:TILES], nb[:, 0].unsqueeze(1).broadcast_to([P, TILES, E]), ALU.add))
                for c in range(2):
                    more(dve.tensor_tensor(one[:, c, 0:TILES], one[:, c, 0:TILES], place[:, 0:TILES], ALU.mult))
                    more(dve.tensor_reduce(dest[:, c], one[:, c, 0:TILES], AX.X, ALU.add))
                more(dve.tensor_copy(dest_i[:], dest[:]))
                more(dve.tensor_tensor(cmp[:, 0:OVER], nb[:, 2].unsqueeze(1).broadcast_to([P, OVER, E]), per_head(rank[:, 0:OVER], E), ALU.is_le))
                more(dve.tensor_reduce(blk[:, 0, 0:OVER], cmp[:, 0:OVER], AX.X, ALU.add))
                more(dve.tensor_scalar(blk[:, 1, 0:OVER], blk[:, 0, 0:OVER], float(E - 1), None, ALU.min))
                more(dve.tensor_copy(blk[:, 1, OVER:OVER + 1], nb[:, 2, E - 1:E]))
                more(dve.tensor_copy(blk_i[:, 0:OVER + 1], blk[:, 1, 0:OVER + 1]))
                dve.sem_inc(dest_r, 1)

            @block.gpsimd
            def _(pool):
                pool.wait_ge(dest_r, 1)
                pool.wait_ge(tab, 16)
                for c in range(2):
                    for t in range(TILES):
                        pool.indirect_dma_start(out=a["row_tok"], out_offset=bass.IndirectOffsetOnAxis(ap=dest_i[:, c, t:t + 1], axis=0),
                                                in_=tok[:, t:t + 1], in_offset=None).then_inc(scat, 16)
                pool.dma_start(a["dest"], dest_i[:].rearrange("p c t -> p (c t)")).then_inc(scat, 16)
                pool.dma_start(a["gates"], gate[:].rearrange("p c t -> p (c t)")).then_inc(scat, 16)
                pool.dma_start(a["blk"], blk_i[0:1, 0:OVER + 1]).then_inc(scat, 16)
                pool.wait_ge(scat, 16 * (2 * TILES + 3))


def experts(nc, a, layer):
    wg, wu, wd = (a[n][layer] for n in ("moe_w_gate", "moe_w_up", "moe_w_down"))
    with Phase(nc, f"moe{layer}") as ph:
        ident = ph.sb("ident", [P, P])
        rt = ph.sb("rt", [BLOCKS, P], I32)
        rtf = ph.sb("rtf", [BLOCKS, P])
        idx = ph.sb("idx", [P, BLOCKS], I32)
        idxc = ph.sb("idxc", [P, 2, 1], I32)
        blk = ph.sb("blk", [1, OVER + 1], I32)
        wgu = ph.sb("wgu", [P, 2, KC, 2, FF])
        wdn = ph.sb("wdn", [P, 2, 2, D])
        x = ph.sb("x", [P, 2, D])
        xT = ph.sb("xT", [P, 2, KC, P])
        sg = ph.sb("sg", [P, 2, FF])
        hid = ph.sb("hid", [P, 2, FF])
        hidT = ph.sb("hidT", [P, 2, 2, P])
        y = ph.sb("y", [P, 2, D])
        bank = ph.banks(8)
        cst, t_mm, idx_r, idx_c, x_tr, xt_ev, gu_mm, sg_r, hid_r, h_tr, ht_ev, y_mm, own = (ph.sem(n) for n in (
            "cst", "idx_turned", "idx_ready", "idx_copied", "x_turned", "xT_ev", "gate_up_mm", "silu_ready", "hid_ready",
            "hid_turned", "hidT_ev", "y_mm", "own"))
        y_ev = [ph.sem(f"y_ev{c}") for c in range(2)]
        w_l = [ph.sem(f"gate_up_loaded{j}") for j in range(2)]
        wd_l = [ph.sem(f"down_loaded{j}") for j in range(2)]
        x_l = [ph.sem(f"x_loaded{j}") for j in range(2)]
        y_st = [ph.sem(f"y_stored{j}") for j in range(2)]
        SECTIONS = ((0, E), (E, OVER))

        def both_sections(eng, body):
            body(0, E)
            more = eng.value_load(blk[0:1, OVER:OVER + 1], min_val=0, max_val=OVER)
            with eng.If(more > 0):
                body(E, OVER)
            with eng.Else():
                pass

        with nc.Block() as block:

            @block.sync
            def _(sp):
                sp.dma_start(ident[:], a["const_f"][:, CONST["ident"]]).then_inc(cst, 16)
                sp.dma_start(rt[:], a["row_tok"].rearrange("(b p) o -> b (p o)", p=P)).then_inc(cst, 16)
                sp.dma_start(blk[:], a["blk"]).then_inc(cst, 16)

                def body(first, count):
                    with sp.Fori(first // 2, (first + count) // 2) as p:
                        for j in range(2):
                            e = sp.snap(2 * p + j) if first == 0 else sp.value_load(blk[0:1, ds(2 * p + (j - E), 1)], min_val=0, max_val=E - 1)
                            at = sp.snap(2 * p + (j + 1))
                            sp.wait_ge(gu_mm, at)
                            sp.dma_start(wgu[:, j, :, 0, :], wg[ds(e, 1)].rearrange("a (k p) n -> p (a k) n", p=P)).then_inc(w_l[j], 16)
                            sp.dma_start(wgu[:, j, :, 1, :], wu[ds(e, 1)].rearrange("a (k p) n -> p (a k) n", p=P)).then_inc(w_l[j], 16)

                sp.wait_ge(cst, 48)
                both_sections(sp, body)

            @block.gpsimd
            def _(pool):
                pool.wait_ge(cst, 48)
                pool.wait_ge(idx_r, 2)

                def body(first, count):
                    with pool.Fori(first // 2, (first + count) // 2) as p:
                        for j in range(2):
                            pool.wait_ge(x_tr, 2 * p + (j + 1))
                            pool.tensor_copy(idxc[:, j], idx[:, ds(pool.snap(2 * p + j), 1)]).then_inc(idx_c, 1)
                            pool.wait_ge(idx_c, 2 * p + (j + 1))
                            pool.sem_inc(own, 1)
                            pool.indirect_dma_start(out=x[:, j], out_offset=None, in_=a["h_rows"],
                                                    in_offset=bass.IndirectOffsetOnAxis(ap=idxc[:, j], axis=0)).then_inc(x_l[j], 16)

                both_sections(pool, body)

            @block.tensor
            def _(pe):
                pe.wait_ge(cst, 48)
                pe.wait_ge(idx_r, 1)
                pe.transpose(bank[0][:, 0:BLOCKS], rtf[:], ident[0:BLOCKS, 0:BLOCKS]).then_inc(t_mm, 1)
                pe.wait_ge(idx_r, 2)
                pe.sem_inc(x_tr, 2)
                pe.sem_inc(y_mm, 4)
                pe.sem_inc(gu_mm, 2)

                def turn_x(b, j, p):
                    pe.wait_ge(x_l[j], 16 * p + 16)
                    pe.wait_ge(xt_ev, 2 * b + 2)
                    for k in range(KC):
                        mm = pe.transpose(bank[k // 4][:, (k % 4) * P:(k % 4 + 1) * P], x[:, j, k * P:(k + 1) * P], ident[:])
                    mm.then_inc(x_tr, 1)

                def gate_up(b, j, p):
                    pe.wait_ge(w_l[j], 32 * p + 32)
                    pe.wait_ge(xt_ev, 2 * b + 4)
                    for k in range(KC):
                        mm = pe.matmul(bank[2 + j][:], xT[:, j, k, :], wgu[:, j, k].rearrange("p a n -> p (a n)"),
                                       start=k == 0, stop=k == KC - 1)
                    mm.then_inc(gu_mm, 1)

                def turn_hid(b, j, p):
                    pe.wait_ge(hid_r, b + 1)
                    pe.wait_ge(ht_ev, b + 1)
                    for k in range(2):
                        mm = pe.transpose(bank[4][:, k * P:(k + 1) * P], hid[:, j, k * P:(k + 1) * P], ident[:])
                    mm.then_inc(h_tr, 1)

                def down(b, j, p):
                    pe.wait_ge(ht_ev, b + 2)
                    pe.wait_ge(wd_l[j], 16 * p + 16)
                    for c in range(2):
                        pe.wait_ge(y_ev[c], b + 1)
                        for k in range(2):
                            mm = pe.matmul(bank[5 + c][:], hidT[:, j, k, :], wdn[:, j, k, c * 512:(c + 1) * 512],
                                           start=k == 0, stop=k == 1)
                        mm.then_inc(y_mm, 1)

                def body(first, count):
                    h = first // 2
                    last = first + count - 1
                    turn_x(first, 0, h)
                    gate_up(first, 0, h)
                    turn_x(first + 1, 1, h)
                    turn_hid(first, 0, h)
                    with pe.Fori(h, h + count // 2 - 1) as p:
                        gate_up(2 * p + 1, 1, p)
                        turn_x(2 * p + 2, 0, p + 1)
                        down(2 * p, 0, p)
                        turn_hid(2 * p + 1, 1, p)
                        gate_up(2 * p + 2, 0, p + 1)
                        turn_x(2 * p + 3, 1, p + 1)
                        down(2 * p + 1, 1, p)
                        turn_hid(2 * p + 2, 0, p + 1)
                    gate_up(last, 1, last // 2)
                    down(last - 1, 0, last // 2)
                    turn_hid(last, 1, last // 2)
                    down(last, 1, last // 2)

                both_sections(pe, body)

            @block.scalar
            def _(act):
                act.wait_ge(cst, 48)
                act.sem_inc(xt_ev, 2)
                act.sem_inc(ht_ev, 1)
                act.sem_inc(y_ev[0], 1)
                act.sem_inc(y_st[0], 16)
                act.sem_inc(y_st[1], 16)
                over = [False]

                def copy_x(b, j):
                    act.wait_ge(x_tr, b + 3)
                    for c in range(2):
                        act.activation(xT[:, j, 4 * c:4 * c + 4].rearrange("p k t -> p (k t)"), bank[c][:], ACT.Copy).then_inc(xt_ev, 1)

                def silu(b, j):
                    act.wait_ge(gu_mm, b + 3)
                    act.activation(sg[:, j], bank[2 + j][:, 0:FF], ACT.Silu).then_inc(sg_r, 1)

                def copy_hid(b, j):
                    act.wait_ge(h_tr, b + 1)
                    act.activation(hidT[:, j].rearrange("p k t -> p (k t)"), bank[4][:, 0:FF], ACT.Copy).then_inc(ht_ev, 1)

                def load_down(b, j):
                    e = b if isinstance(b, int) and b < E else None
                    if e is None:
                        e = act.snap(b * 1) if not over[0] else act.value_load(blk[0:1, ds(b - E, 1)], min_val=0, max_val=E - 1)
                    act.dma_start(wdn[:, j], wd[ds(e, 1)].rearrange("a (k p) n -> p (a k) n", p=P)).then_inc(wd_l[j], 16)

                def store(b, j, p, ahead=True):
                    act.wait_ge(y_mm, 2 * b + 6)
                    if ahead:
                        load_down(b + 2, j)
                    act.wait_ge(y_st[j], 16 * p + 16)
                    act.activation(y[:, j, 0:512], bank[5][:], ACT.Copy).then_inc(y_ev[0], 1)
                    row = b * P if isinstance(b, int) else act.snap(b * P)
                    act.wait_ge(y_ev[0], b + 2)
                    act.wait_ge(y_ev[1], b + 2)
                    act.dma_start(a["y_rows"][ds(row, P), :], y[:, j]).then_inc(y_st[j], 16)

                def body(first, count):
                    h = first // 2
                    last = first + count - 1
                    over[0] = first > 0
                    load_down(first, 0)
                    load_down(first + 1, 1)
                    copy_x(first, 0)
                    silu(first, 0)
                    copy_x(first + 1, 1)
                    copy_hid(first, 0)
                    with act.Fori(h, h + count // 2 - 1) as p:
                        silu(2 * p + 1, 1)
                        copy_x(2 * p + 2, 0)
                        store(2 * p, 0, p)
                        copy_hid(2 * p + 1, 1)
                        silu(2 * p + 2, 0)
                        copy_x(2 * p + 3, 1)
                        store(2 * p + 1, 1, p)
                        copy_hid(2 * p + 2, 0)
                    silu(last, 1)
                    store(last - 1, 0, last // 2, False)
                    copy_hid(last, 1)
                    store(last, 1, last // 2, False)
                    for j in range(2):
                        act.wait_ge(y_st[j], 16 * ((first + count) // 2 + 1))

                both_sections(act, body)

            @block.vector
            def _(dve):
                dve.wait_ge(cst, 48)
                dve.tensor_copy(rtf[:], rt[:]).then_inc(idx_r, 1)
                dve.wait_ge(t_mm, 1)
                dve.tensor_copy(idx[:], bank[0][:, 0:BLOCKS]).then_inc(idx_r, 1)
                dve.sem_inc(y_ev[1], 1)

                def hidden(b, j):
                    dve.wait_ge(sg_r, b + 1)
                    dve.tensor_tensor(hid[:, j], sg[:, j], bank[2 + j][:, FF:2 * FF], ALU.mult).then_inc(hid_r, 1)

                def second_half(b, j, p):
                    dve.wait_ge(y_mm, 2 * b + 6)
                    dve.wait_ge(y_st[j], 16 * p + 16)
                    dve.tensor_copy(y[:, j, 512:D], bank[6][:]).then_inc(y_ev[1], 1)

                def body(first, count):
                    h = first // 2
                    last = first + count - 1
                    hidden(first, 0)
                    with dve.Fori(h, h + count // 2 - 1) as p:
                        hidden(2 * p + 1, 1)
                        second_half(2 * p, 0, p)
                        hidden(2 * p + 2, 0)
                        second_half(2 * p + 1, 1, p)
                    hidden(last, 1)
                    second_half(last - 1, 0, last // 2)
                    second_half(last, 1, last // 2)

                both_sections(dve, body)


def combine(nc, a, layer):
    m = 2 * layer + 1
    with Phase(nc, f"comb{layer}") as ph:
        rows = ph.sb("rows", [P, 3, D])
        dest = ph.sb("dest", [P, 2, TILES], I32)
        gates = ph.sb("gates", [P, 2, TILES])
        idxc = ph.sb("idxc", [P, 2, 2, 1], I32)
        y = ph.sb("y", [P, 2, 2, D])
        x = ph.sb("x", [P, 2, D])
        t = ph.sb("t", [P, D])
        out = ph.sb("out", [P, 2, D])
        stats = ph.sb("stats", [P, 2, 6])
        mv = ph.sb("mv", [P, 3])
        cst, rows_l, rows_free, in_free, vec, own, step, idx_c, idx_s, var_r, root, out_r = (ph.sem(n) for n in (
            "cst", "rows_loaded", "rows_free", "inputs_free", "vec", "own", "step", "idx_copied", "idx_waited", "var_ready", "root", "out_ready"))
        x_l = [ph.sem(f"x_loaded{j}") for j in range(2)]
        y_l = [ph.sem(f"y_loaded{j}") for j in range(2)]
        st = [ph.sem(f"stored{j}") for j in range(2)]

        with nc.Block() as block:

            @block.sync
            def _(sp):
                sp.dma_start(dest[:].rearrange("p c t -> p (c t)"), a["dest"]).then_inc(cst, 16)
                sp.dma_start(gates[:].rearrange("p c t -> p (c t)"), a["gates"]).then_inc(cst, 16)
                for q, (lo, hi) in enumerate(SEQ_TILES):
                    sp.wait_ge(rows_free, q + 1)
                    for n, src in enumerate((mod_row(a, m, q, 2), a["ln_g"][layer, 1:2].broadcast_to([P, D]),
                                             a["ln_b"][layer, 1:2].broadcast_to([P, D]))):
                        sp.dma_start(rows[:, n], src).then_inc(rows_l, 16)
                    with sp.Fori(lo // 2, hi // 2) as p:
                        for j in range(2):
                            at = sp.snap(2 * p + (j + 1))
                            row = sp.snap((2 * p + j) * P)
                            sp.wait_ge(in_free, at)
                            sp.dma_start(x[:, j], a["x_mid"][ds(row, P), :]).then_inc(x_l[j], 16)

            @block.gpsimd
            def _(pool):
                pool.wait_ge(cst, 32)
                with pool.Fori(0, TILES // 2) as p:
                    for j in range(2):
                        pool.wait_ge(in_free, 2 * p + (j + 1))
                        for c in range(2):
                            pool.tensor_copy(idxc[:, j, c], dest[:, c, ds(pool.snap(2 * p + j), 1)]).then_inc(idx_c, 1)
                        pool.wait_ge(idx_c, 4 * p + (2 * j + 2))
                        pool.sem_inc(idx_s, 1)
                        for c in range(2):
                            pool.indirect_dma_start(out=y[:, j, c], out_offset=None, in_=a["y_rows"],
                                                    in_offset=bass.IndirectOffsetOnAxis(ap=idxc[:, j, c], axis=0)).then_inc(y_l[j], 16)

            @block.scalar
            def _(act):
                act.sem_inc(st[0], 16)
                act.sem_inc(st[1], 16)
                for q, (lo, hi) in enumerate(SEQ_TILES):
                    with act.Fori(lo // 2, hi // 2) as p:
                        for j in range(2):
                            act.wait_ge(var_r, 2 * p + (j + 1))
                            act.activation(mv[:, 2:3], mv[:, 2:3], ACT.Sqrt).then_inc(root, 1)
                            row = act.snap(2 * p * P + (j - lo) * P if layer else 2 * p * P + j * P)
                            act.wait_ge(out_r, 2 * p + (j + 1))
                            if layer == 0:
                                dst = a["x_mid2"][ds(row, P), :]
                            else:
                                dst = a["y_prompt" if q == 0 else "y_sample"][0, ds(row, P), :]
                            act.dma_start(dst, out[:, j]).then_inc(st[j], 16)
                for j in range(2):
                    act.wait_ge(st[j], 16 * (TILES // 2 + 1))

            @block.vector
            def _(dve):
                dve.sem_inc(rows_free, 1)
                dve.sem_inc(in_free, 2)
                dve.wait_ge(cst, 32)
                per = 11
                link = Chain(dve, vec, 2 * per)
                for q, (lo, hi) in enumerate(SEQ_TILES):
                    dve.wait_ge(rows_l, 48 * (q + 1))
                    dve.tensor_scalar(rows[:, 0], rows[:, 0], 1.0, None, ALU.add).then_inc(own, 1)
                    dve.wait_ge(own, q + 1)
                    with dve.Fori(lo // 2, hi // 2) as p:
                        link.turn(p)
                        for j in range(2):
                            g = [gates[:, c, ds(dve.snap(2 * p + j), 1)] for c in range(2)]
                            dve.wait_ge(y_l[j], 32 * p + 32)
                            link(dve.tensor_scalar(y[:, j, 0], y[:, j, 0], g[0], None, ALU.mult))
                            link(dve.scalar_tensor_tensor(y[:, j, 0], y[:, j, 1], g[1], y[:, j, 0], ALU.mult, ALU.add))
                            link(dve.tensor_tensor(y[:, j, 0], y[:, j, 0], rows[:, 0], ALU.mult))
                            dve.wait_ge(x_l[j], 16 * p + 16)
                            dve.wait_ge(st[j], 16 * p + 16)
                            link(dve.scalar_tensor_tensor(t[:], x[:, j], ALPHA, y[:, j, 0], ALU.mult, ALU.add))
                            dve.sem_inc(in_free, 1)
                            normed(dve, link, step, t, out[:, j], stats, mv, var_r, root, 2 * p + (j + 1), rows[:, 1], rows[:, 2])
                            dve.sem_inc(out_r, 1)
                    if q == 0:
                        dve.sem_inc(rows_free, 1)
                link.end()



PAIRS = AT_H // 2
KV0 = AT_H * AT_N
V0 = KV0 + AT_KV * AT_N
VW = AT_KV * AT_N
SLOTS = TILES + 3
EMPTY = (0, TP + 1, SLOTS - 1)


def attention_projection(nc, a):
    with Phase(nc, "qkv") as ph:
        ident = ph.sb("ident", [P, P])
        w = ph.sb("w", [P, KC, AT_COLS])
        scol = ph.sb("scol", [P, 2, 2, KC])
        x = ph.sb("x", [P, 2, D])
        rope = ph.sb("rope", [P, 2, ROPE])
        hT = ph.sb("hT", [P, 2, KC, P])
        z = ph.sb("z", [P, 2, AT_COLS])
        r = ph.sb("r", [P, 4, AT_H + AT_KV, HALF_ROPE])
        kd = ph.sb("kd", [P, 2, AT_KV, 2, AT_N])
        qT = ph.sb("qT", [P, 2, PAIRS, P])
        kT = ph.sb("kT", [P, 2, AT_KV, P])
        zero = ph.sb("zero", [P, AT_KV, P])
        bank = ph.banks(8)
        cst, zeroed, z_st, x_tr, h_ev, z_mm, z_ev, rot, vec, kd_r, tr, tr_ev = (ph.sem(n) for n in (
            "cst", "zeroed", "zero_stored", "x_turned", "hT_ev", "z_mm", "z_ev", "rotated", "vec", "k_doubled", "turned",
            "turned_ev"))
        x_l = [ph.sem(f"x_loaded{j}") for j in range(2)]
        st = [ph.sem(f"stored{j}") for j in range(2)]

        with nc.Block() as block:

            @block.sync
            def _(sp):
                sp.dma_start(ident[:], a["const_f"][:, CONST["ident"]]).then_inc(cst, 16)
                for q in range(2):
                    for part in range(2):
                        sp.dma_start(scol[:, q, part], a["mod"][2, q, part * D:(part + 1) * D].rearrange("(k p) -> p k", p=P),
                                     allow_slow_non_contiguous=True).then_inc(cst, 16)
                sp.dma_start(w[:], a["at_w_in"][0].rearrange("(k p) n -> p k n", p=P)).then_inc(cst, 16)
                sp.wait_ge(zeroed, 1)
                for slot in EMPTY:
                    sp.dma_start(a["kT_rows"][:, :, slot * P:(slot + 1) * P], zero[:]).then_inc(z_st, 16)
                    sp.dma_start(a["v_rows"][slot * P:(slot + 1) * P, :],
                                 zero[:].rearrange("p g t -> p (g t)")[:, 0:VW]).then_inc(z_st, 16)
                with sp.Fori(0, TILES // 2) as p:
                    for j in range(2):
                        at = sp.snap(2 * p + (j + 1))
                        row = sp.snap((2 * p + j) * P)
                        sp.wait_ge(rot, at)
                        sp.dma_start(x[:, j], a["x_mid2"][ds(row, P), :]).then_inc(x_l[j], 16)
                        sp.dma_start(rope[:, j], a["const_rope"][ds(row, P), :]).then_inc(x_l[j], 16)
                sp.wait_ge(z_st, 16 * 6)

            @block.tensor
            def _(pe):
                pe.wait_ge(cst, 16 * 6)

                def turn_x(i, j, p):
                    pe.wait_ge(x_l[j], 32 * p + 32)
                    pe.wait_ge(h_ev, i + 1)
                    for k in range(KC):
                        mm = pe.transpose(bank[k // 4][:, (k % 4) * P:(k % 4 + 1) * P], x[:, j, k * P:(k + 1) * P], ident[:])
                    mm.then_inc(x_tr, 1)

                def product(i, j, c):
                    pe.wait_ge(h_ev, i + 2)
                    pe.wait_ge(z_ev, 3 * i + (c + 1))
                    for k in range(KC):
                        mm = pe.matmul(bank[2 + c][:], hT[:, j, k, :], w[:, k, c * 512:(c + 1) * 512],
                                       start=k == 0, stop=k == KC - 1)
                    mm.then_inc(z_mm, 1)

                def turn_qk(i, j):
                    pe.wait_ge(kd_r, i + 1)
                    pe.wait_ge(tr_ev, 3 * i + 3)
                    for n in range(12):
                        src = z[:, j, n * P:(n + 1) * P] if n < PAIRS else kd[:, j, n - PAIRS].rearrange("p a c -> p (a c)")
                        mm = pe.transpose(bank[5 + n // 4][:, (n % 4) * P:(n % 4 + 1) * P], src, ident[:])
                        if n % 4 == 3:
                            mm.then_inc(tr, 1)

                def tile(i, j, p, first=False, last=False):
                    product(i, j, 0)
                    if not first:
                        turn_qk(i - 1, 1 - j)
                    product(i, j, 1)
                    if not last:
                        turn_x(i + 1, 1 - j, p + j)
                    product(i, j, 2)

                turn_x(0, 0, 0)
                tile(0, 0, 0, first=True)
                with pe.Fori(0, TILES // 2 - 1) as p:
                    tile(2 * p + 1, 1, p)
                    tile(2 * p + 2, 0, p + 1)
                tile(TILES - 1, 1, TILES // 2 - 1, last=True)
                turn_qk(TILES - 1, 1)

            @block.scalar
            def _(act):
                act.wait_ge(cst, 16 * 6)
                act.sem_inc(z_ev, 3)
                act.sem_inc(tr_ev, 3)
                act.sem_inc(st[0], 48)
                act.sem_inc(st[1], 48)

                def copy_z(i, j, c):
                    act.wait_ge(z_mm, 3 * i + (c + 1))
                    act.activation(z[:, j, c * 512:(c + 1) * 512], bank[2 + c][:], ACT.Copy).then_inc(z_ev, 1)

                def store(i, j, q):
                    for c in range(3):
                        act.wait_ge(tr, 3 * i + (c + 1))
                        dst = (qT[:, j, 0:4], qT[:, j, 4:8], kT[:, j])[c]
                        act.activation(dst.rearrange("p k t -> p (k t)"), bank[5 + c][:], ACT.Copy,
                                       scale=AT_N ** -0.5 if c < 2 else 1.0).then_inc(tr_ev, 1)
                    act.wait_ge(tr_ev, 3 * i + 6)
                    tile, slot = (i, (i + 1 + q) * P) if isinstance(i, int) else (act.snap(i * 1), act.snap(i * P + (1 + q) * P))
                    act.dma_start(a["qT_rows"][ds(tile, 1)].rearrange("a p n -> (a p) n"),
                                  qT[:, j].rearrange("p k t -> p (k t)")).then_inc(st[j], 16)
                    act.dma_start(a["kT_rows"][:, :, ds(slot, P)], kT[:, j]).then_inc(st[j], 16)
                    act.dma_start(a["v_rows"][ds(slot, P), :], z[:, j, V0:AT_COLS]).then_inc(st[j], 16)

                def tile(i, j, p, q=None):
                    act.wait_ge(st[j], 48 * p + 48)
                    copy_z(i, j, 0)
                    if q is not None:
                        store(i - 1, 1 - j, q)
                    copy_z(i, j, 1)
                    copy_z(i, j, 2)
                    act.wait_ge(rot, i + 3)
                    act.activation(kd[:, j], z[:, j, KV0:V0].rearrange("p (g n) -> p g n", n=AT_N).unsqueeze(2)
                                   .broadcast_to([P, AT_KV, 2, AT_N]), ACT.Copy).then_inc(kd_r, 1)

                tile(0, 0, 0)
                with act.Fori(0, TP // 2 - 1) as p:
                    tile(2 * p + 1, 1, p, 0)
                    tile(2 * p + 2, 0, p + 1, 0)
                for i in range(TP - 1, TILES):
                    tile(i, i % 2, i // 2, 0 if i <= TP else 1)
                store(TILES - 1, (TILES - 1) % 2, 1)
                for j in range(2):
                    act.wait_ge(st[j], 48 * (TILES // 2 + 1))

            @block.vector
            def _(dve):
                dve.memset(zero[:], 0.0).then_inc(zeroed, 1)
                dve.wait_ge(cst, 16 * 6)
                link = Chain(dve, vec, 5, 1)
                dve.tensor_scalar(scol[:, :, 1], scol[:, :, 1], 1.0, None, ALU.add).then_inc(vec, 1)
                dve.wait_ge(vec, 1)
                dve.sem_inc(h_ev, 1)
                dve.sem_inc(rot, 2)

                def scale_shift(i, j, q):
                    dve.wait_ge(x_tr, i + 1)
                    for k in range(KC):
                        ins = dve.tensor_scalar(hT[:, j, k], bank[k // 4][:, (k % 4) * P:(k % 4 + 1) * P],
                                                scol[:, q, 1, k:k + 1], scol[:, q, 0, k:k + 1], ALU.mult, ALU.add)
                    ins.then_inc(h_ev, 1)

                def rotate(i, j):
                    link.turn(i)
                    hz = z[:, j, 0:V0].rearrange("p (h n) -> p h n", n=AT_N)
                    x1, x2 = hz[:, :, 0:HALF_ROPE], hz[:, :, HALF_ROPE:ROPE]
                    cos, sin = (rope[:, j, c * HALF_ROPE:(c + 1) * HALF_ROPE].unsqueeze(1)
                                .broadcast_to([P, AT_H + AT_KV, HALF_ROPE]) for c in range(2))
                    dve.wait_ge(z_ev, 3 * i + 6)
                    dve.wait_ge(rot, i + 2)
                    link(dve.tensor_tensor(r[:, 0], x1, cos, ALU.mult))
                    link(dve.tensor_tensor(r[:, 1], x2, sin, ALU.mult))
                    link(dve.tensor_tensor(r[:, 2], x2, cos, ALU.mult))
                    link(dve.tensor_tensor(r[:, 3], x1, sin, ALU.mult))
                    link(dve.tensor_tensor(x1, r[:, 0], r[:, 1], ALU.subtract))
                    dve.tensor_tensor(x2, r[:, 2], r[:, 3], ALU.add).then_inc(rot, 1)
                    link.end()

                scale_shift(0, 0, 0)
                with dve.Fori(0, TP // 2 - 1) as p:
                    for j in range(2):
                        scale_shift(2 * p + (j + 1), 1 - j, 0)
                        rotate(2 * p + j, j)
                for i in range(TP - 2, TILES):
                    if i + 1 < TILES:
                        scale_shift(i + 1, (i + 1) % 2, int(i + 1 >= TP))
                    rotate(i, i % 2)


def window_attention(nc, a):
    W3 = 3 * P
    with Phase(nc, "attn") as ph:
        ident = ph.sb("ident", [P, P])
        sink = ph.sb("sink", [P, AT_H])
        qT = ph.sb("qT", [P, 2, 2, PAIRS, P])
        kT = ph.sb("kT", [P, 2, AT_KV, W3])
        v = ph.sb("v", [P, 2, 3, VW])
        band = ph.sb("band", [P, 2, W3])
        s = ph.sb("s", [P, 4, W3])
        pT = ph.sb("pT", [P, 2, 3, P])
        mx = ph.sb("mx", [P, AT_H])
        neg = ph.sb("neg", [P, AT_H])
        total = ph.sb("total", [P, AT_H])
        es = ph.sb("es", [P, AT_H])
        o = ph.sb("o", [P, AT_H, AT_N])
        bank = ph.banks(8)
        cst, in_free, s_mm, m_r, n_r, e_r, t_mm, o_mm, es_in, es_r, o_r, done, vec, init, step = (ph.sem(n) for n in (
            "cst", "inputs_free", "scores_mm", "max_ready", "neg_ready", "exp_ready", "probs_turned", "out_mm",
            "sink_diff", "sink_exp", "out_ready", "turn_done", "vec", "total_zeroed", "step"))
        t_ev = [ph.sem(f"turned_ev{e}") for e in range(2)]
        in_l = [ph.sem(f"inputs_loaded{j}") for j in range(2)]
        st = ph.sem("stored")
        cleared = ph.sem("queries_cleared")

        with nc.Block() as block:

            @block.sync
            def _(sp):
                sp.wait_ge(cleared, 1)
                sp.dma_start(ident[:], a["const_f"][:, CONST["ident"]]).then_inc(cst, 16)
                sp.dma_start(sink[:], a["at_sink"].broadcast_to([P, AT_H])).then_inc(cst, 16)
                for q, (lo, hi) in enumerate(SEQ_TILES):
                    with sp.Fori(lo // 2, hi // 2) as p:
                        for j in range(2):
                            at = sp.snap(2 * p + (j + 1))
                            tile = sp.snap(2 * p + j)
                            slot = sp.snap(2 * p * P + (j + q) * P)
                            sp.wait_ge(in_free, at)
                            for e in range(2):
                                half = slice(64 * e, 64 * e + 64)
                                sp.dma_start(qT[half, j, e].rearrange("p k t -> p (k t)"),
                                             a["qT_rows"][ds(tile, 1), half].rearrange("a p n -> (a p) n")).then_inc(in_l[j], 16)
                            sp.dma_start(kT[:, j], a["kT_rows"][:, :, ds(slot, W3)]).then_inc(in_l[j], 16)
                            sp.dma_start(v[:, j], a["v_rows"][ds(slot, W3), :].rearrange("(c p) n -> p c n", p=P)).then_inc(in_l[j], 16)
                            sp.dma_start(band[:, j], a["const_band"][ds(tile, 1)].rearrange("a p n -> (a p) n")).then_inc(in_l[j], 16)

            @block.tensor
            def _(pe):
                pe.wait_ge(cst, 32)
                pe.wait_ge(cleared, 1)
                pe.sem_inc(o_mm, 2)
                pe.sem_inc(t_mm, 4)
                with pe.Fori(0, TILES // 2) as p:
                    for j in range(2):
                        i = 2 * p + j
                        pe.wait_ge(in_l[j], 80 * p + 80)
                        for n in range(AT_H + 3):
                            if n < AT_H:
                                pe.wait_ge(m_r, i * AT_H + (n + 1))
                                pe.matmul(bank[n % 3][:, 0:W3], qT[:, j, n % 2, n // 2, :], kT[:, j, n // 4, :],
                                          start=True, stop=True).then_inc(s_mm, 1)
                            h = n - 2
                            if 0 <= h < AT_H:
                                pe.wait_ge(e_r, i * AT_H + (h + 1))
                                pe.wait_ge(t_ev[h % 2], i * PAIRS + (h // 2 + 1))
                                for c in range(3):
                                    mm = pe.transpose(bank[3 + h % 2][:, c * P:(c + 1) * P], s[:, h % 4, c * P:(c + 1) * P], ident[:])
                                mm.then_inc(t_mm, 1)
                            h = n - 3
                            if 0 <= h < AT_H:
                                pe.wait_ge(t_ev[h % 2], i * PAIRS + (h // 2 + 2))
                                if h == 0:
                                    pe.wait_ge(done, i + 1)
                                g = (h // 4) * AT_N
                                for c in range(3):
                                    mm = pe.matmul(bank[5 + h // 8][:, (h % 8) * AT_N:(h % 8 + 1) * AT_N], pT[:, h % 2, c, :],
                                                   v[:, j, c, g:g + AT_N], start=c == 0, stop=c == 2)
                                mm.then_inc(o_mm, 1)

            @block.scalar
            def _(act):
                act.sem_inc(st, 16)
                act.sem_inc(t_ev[1], 1)
                with act.Fori(0, TILES // 2) as p:
                    for j in range(2):
                        i = 2 * p + j
                        act.wait_ge(init, i + 1)
                        for n in range(AT_H + 2):
                            if n < AT_H:
                                act.wait_ge(n_r, i * AT_H + (n + 1))
                                act.activation(s[:, n % 4], s[:, n % 4], ACT.Exp, bias=neg[:, n:n + 1],
                                               accum_out=total[:, n:n + 1]).then_inc(e_r, 1)
                            h = n - 2
                            if h >= 0 and h % 2:
                                act.wait_ge(t_mm, i * AT_H + (h + 5))
                                act.wait_ge(o_mm, i * AT_H + (h + 1))
                                act.activation(pT[:, 1].rearrange("p c t -> p (c t)"), bank[4][:, 0:W3], ACT.Copy).then_inc(t_ev[1], 1)
                        act.wait_ge(es_in, i + 1)
                        act.activation(es[:], es[:], ACT.Exp).then_inc(es_r, 1)
                        row = act.snap(i * P)
                        act.wait_ge(o_r, i + 1)
                        act.dma_start(a["at_o"][ds(row, P), :], o[:].rearrange("p h n -> p (h n)")).then_inc(st, 16)
                act.wait_ge(st, 16 * (TILES + 1))

            @block.vector
            def _(dve):
                dve.memset(qT[:], 0.0).then_inc(cleared, 1)
                dve.wait_ge(cst, 32)
                dve.sem_inc(done, 1)
                dve.sem_inc(in_free, 2)
                dve.sem_inc(m_r, 3)
                dve.sem_inc(t_ev[0], 1)
                link = Chain(dve, vec, 4)
                with dve.Fori(0, TILES // 2) as p:
                    for j in range(2):
                        i = 2 * p + j
                        link.turn(i)
                        link(dve.memset(total[:], 0.0))
                        dve.sem_inc(init, 1)
                        dve.wait_ge(in_l[j], 80 * p + 80)
                        for n in range(AT_H + 2):
                            if n < AT_H:
                                dve.wait_ge(t_mm, i * AT_H + (n + 1))
                                dve.wait_ge(s_mm, i * AT_H + (n + 1))
                                dve.sem_inc(step, 1)
                                dve.tensor_tensor_reduce(s[:, n % 4], bank[n % 3][:, 0:W3], band[:, j], 1.0, sink[:, n:n + 1],
                                                         ALU.add, ALU.max, mx[:, n:n + 1]).then_inc(m_r, 1)
                                dve.wait_ge(m_r, i * AT_H + (n + 4))
                                dve.tensor_scalar(neg[:, n:n + 1], mx[:, n:n + 1], -1.0, None, ALU.mult).then_inc(n_r, 1)
                            h = n - 2
                            if h >= 0 and h % 2 == 0:
                                dve.wait_ge(t_mm, i * AT_H + (h + 5))
                                dve.wait_ge(o_mm, i * AT_H + (h + 1))
                                dve.tensor_copy(pT[:, 0].rearrange("p c t -> p (c t)"), bank[3][:, 0:W3]).then_inc(t_ev[0], 1)
                        dve.wait_ge(n_r, i * AT_H + AT_H)
                        dve.tensor_tensor(es[:], sink[:], neg[:], ALU.add).then_inc(es_in, 1)
                        dve.wait_ge(es_r, i + 1)
                        link(dve.tensor_tensor(total[:], total[:], es[:], ALU.add))
                        link(dve.reciprocal(total[:], total[:]))
                        dve.wait_ge(o_mm, i * AT_H + (AT_H + 2))
                        dve.sem_inc(in_free, 1)
                        dve.wait_ge(st, 16 * i + 16)
                        link(dve.tensor_tensor(o[:, 0:8], heads(bank[5][:], AT_N), per_head(total[:, 0:8], AT_N), ALU.mult))
                        dve.tensor_tensor(o[:, 8:16], heads(bank[6][:], AT_N), per_head(total[:, 8:16], AT_N), ALU.mult).then_inc(o_r, 1)
                        dve.wait_ge(o_r, i + 1)
                        dve.sem_inc(done, 1)
                        link.end()


def trunk(nc, a):
    def scratch(name, shape, dt=F32):
        a[name] = nc.dram_tensor(f"scratch_{name}", shape, dt).ap()

    scratch("mod", (2 * DEPTH, 2, 3 * D))
    scratch("zt", (T, CHUNKS * P))
    scratch("zf", (3 * P, T))
    scratch("rw_y", (2, T, RW_W))
    scratch("rw_bonus", (2, T, RW_H))
    scratch("gd_o", (2, T, GD_W))
    scratch("x_mid", (T, D))
    scratch("x_mid2", (T, D))
    scratch("h_rows", (T, D))
    scratch("y_rows", (BLOCKS * P, D))
    scratch("row_tok", (BLOCKS * P, 1), I32)
    scratch("dest", (P, 2 * TILES), I32)
    scratch("gates", (P, 2 * TILES))
    scratch("blk", (1, OVER + 1), I32)
    scratch("qT_rows", (TILES, P, PAIRS * P))
    scratch("kT_rows", (P, AT_KV, SLOTS * P))
    scratch("v_rows", (SLOTS * P, VW))
    scratch("at_o", (T, D))
    ada_modulation(nc, a)
    input_projection(nc, a)
    rwkv_mixer(nc, a)
    deltanet_mixer(nc, a)
    close_mixer(nc, a, 0)
    experts(nc, a, 0)
    combine(nc, a, 0)
    attention_projection(nc, a)
    window_attention(nc, a)
    close_mixer(nc, a, 1)
    experts(nc, a, 1)
    combine(nc, a, 1)


_WEIGHTS = ["c_prompt", "c_sample", "ada_w", "ada_b", "ln_g", "ln_b", "ab_w_in", "rw_mu", "rw_w0", "rw_w_up", "rw_a0",
            "rw_a_up", "rw_g_up", "rw_k_k", "rw_k_a", "rw_r_k", "rw_gn_g", "rw_gn_b", "gd_conv", "gd_A_log", "gd_dt_bias",
            "gd_norm_g", "ab_w_out", "at_w_in", "at_sink", "at_w_out", "router_w", "router_bias", "moe_w_gate", "moe_w_up",
            "moe_w_down"]


def kernel(**inputs):
    import concourse.bacc as _bacc
    from concourse import mybir as _mybir
    from concourse.bass_utils import run_bass_kernel_spmd as _run

    nc = _bacc.Bacc("TRN2", target_bir_lowering=False, num_devices=1)
    given = {n: np.ascontiguousarray(inputs[n]) for n in _WEIGHTS}
    given["x_in"] = np.concatenate([np.asarray(inputs["x_prompt"])[0], np.asarray(inputs["x_sample"])[0]])
    given.update(constant_tables())
    arrays = {f"in_{n}_dram": v for n, v in given.items()}
    args = {n: nc.dram_tensor(f"in_{n}_dram", v.shape, _mybir.dt.from_np(v.dtype), kind="ExternalInput").ap()
            for n, v in given.items()}
    for n, length in (("y_prompt", S_PROMPT), ("y_sample", S_SAMPLE)):
        args[n] = nc.dram_tensor(f"out_{n}_dram", (1, length, D), F32, kind="ExternalOutput").ap()
    trunk(nc, args)
    r = _run(nc, [arrays], core_ids=[0])
    return tuple(r.results[0][f"out_{n}_dram"] for n in ("y_prompt", "y_sample"))
```
